# Optimizing a Trainium2 kernel written in Bass

```python
import jax, jax.numpy as jnp
from jax import lax
import numpy as np

D_MODEL = 1024
BATCH = 1
SEQ = 256
DEPTH = 2

MEM_LEN = 256
HEAD_DIM = 64
LRU_WIDTH = 256
LRU_BLOCKS = 4
LRU_BLOCK = LRU_WIDTH // LRU_BLOCKS
CONV_WIDTH = 4
LRU_C = 8.0
FOX_HEADS = 8
FOX_WIDTH = FOX_HEADS * HEAD_DIM
RET_HEADS = 4
RET_WIDTH = RET_HEADS * HEAD_DIM
MIX_WIDTH = LRU_WIDTH + FOX_WIDTH + RET_WIDTH
SPLIT_SIZES = (LRU_WIDTH, LRU_WIDTH, FOX_WIDTH, FOX_WIDTH, FOX_WIDTH, FOX_HEADS, RET_WIDTH, RET_WIDTH, RET_WIDTH, RET_WIDTH)
IN_WIDTH = sum(SPLIT_SIZES)
CROSS_HEADS = 4
CROSS_HEAD_DIM = D_MODEL // CROSS_HEADS
D_FF = ((8 * D_MODEL + 3 * 256 - 1) // (3 * 256)) * 256
Q_BLOCK = 128
RET_CHUNK = 128
ROPE_THETA = 10000.0
EPS = 1e-6


def rms_norm(x, g):
    xf = x.astype(jnp.float32)
    y = xf * lax.rsqrt(jnp.mean(xf * xf, axis=-1, keepdims=True) + EPS)
    return (y * g.astype(jnp.float32)).astype(x.dtype)

def causal_depthwise_conv(x, w, b):
    c = x.shape[-1]
    xp = jnp.pad(x, ((0, 0), (CONV_WIDTH - 1, 0), (0, 0)))
    out = lax.conv_general_dilated(xp, w.astype(x.dtype)[:, None, :], window_strides=(1,), padding='VALID', dimension_numbers=('NWC', 'WIO', 'NWC'), feature_group_count=c)
    return out + b.astype(x.dtype)

def rg_lru(x, w_r, b_r, w_i, b_i, lam):
    bsz, s, _ = x.shape
    xb = x.reshape(bsz, s, LRU_BLOCKS, LRU_BLOCK)
    r = jax.nn.sigmoid((jnp.einsum('bsni,nij->bsnj', xb, w_r).reshape(bsz, s, LRU_WIDTH) + b_r).astype(jnp.float32))
    i = jax.nn.sigmoid((jnp.einsum('bsni,nij->bsnj', xb, w_i).reshape(bsz, s, LRU_WIDTH) + b_i).astype(jnp.float32))
    log_a = -LRU_C * r * jax.nn.softplus(-lam.astype(jnp.float32))
    a = jnp.exp(log_a)
    u = jnp.sqrt(-jnp.expm1(2.0 * log_a)) * (i * x.astype(jnp.float32))

    def combine(left, right):
        a1, b1 = left
        a2, b2 = right
        return a1 * a2, a2 * b1 + b2

    _, h = lax.associative_scan(combine, (a, u), axis=1)
    return h.astype(x.dtype)

def forgetting_attention(q, k, v, f_logit, b_f):
    bsz, s, _ = q.shape
    q = q.reshape(bsz, s, FOX_HEADS, HEAD_DIM).transpose(0, 2, 1, 3)
    k = k.reshape(bsz, s, FOX_HEADS, HEAD_DIM).transpose(0, 2, 1, 3)
    v = v.reshape(bsz, s, FOX_HEADS, HEAD_DIM).transpose(0, 2, 1, 3)
    log_f = jax.nn.log_sigmoid((f_logit + b_f).astype(jnp.float32))
    c = jnp.cumsum(log_f, axis=1).transpose(0, 2, 1)
    key_pos = jnp.arange(s)
    scale = HEAD_DIM ** -0.5

    def block(bi):
        start = bi * Q_BLOCK
        qb = lax.dynamic_slice_in_dim(q, start, Q_BLOCK, axis=2)
        cb = lax.dynamic_slice_in_dim(c, start, Q_BLOCK, axis=2)
        logits = jnp.einsum('bhqd,bhkd->bhqk', qb, k).astype(jnp.float32) * scale + cb[..., None] - c[:, :, None, :]
        q_pos = start + jnp.arange(Q_BLOCK)
        mask = key_pos[None, :] <= q_pos[:, None]
        p = jax.nn.softmax(jnp.where(mask, logits, -jnp.inf), axis=-1)
        return jnp.einsum('bhqk,bhkd->bhqd', p.astype(v.dtype), v)

    out = lax.map(block, jnp.arange(s // Q_BLOCK))
    return out.transpose(1, 0, 3, 2, 4).reshape(bsz, s, FOX_WIDTH)

def rotary(x, positions):
    half = x.shape[-1] // 2
    inv_freq = ROPE_THETA ** (-jnp.arange(half, dtype=jnp.float32) / half)
    ang = positions.astype(jnp.float32)[..., None] * inv_freq
    cos = jnp.cos(ang)[:, :, None, :]
    sin = jnp.sin(ang)[:, :, None, :]
    xf = x.astype(jnp.float32)
    x1, x2 = xf[..., :half], xf[..., half:]
    return jnp.concatenate([x1 * cos - x2 * sin, x1 * sin + x2 * cos], axis=-1)

def retention(q, k, v, g, positions):
    bsz, s, _ = q.shape
    n_chunks = s // RET_CHUNK
    shp = (bsz, n_chunks, RET_CHUNK, RET_HEADS, HEAD_DIM)
    qc = rotary(q.reshape(bsz, s, RET_HEADS, HEAD_DIM), positions).reshape(shp)
    kc = (rotary(k.reshape(bsz, s, RET_HEADS, HEAD_DIM), positions) * HEAD_DIM ** -0.5).reshape(shp)
    vc = v.astype(jnp.float32).reshape(shp)
    log_gamma = jnp.log1p(-jnp.exp2(-5.0 - jnp.arange(RET_HEADS, dtype=jnp.float32)))
    idx = jnp.arange(RET_CHUNK, dtype=jnp.float32)
    diff = idx[:, None] - idx[None, :]
    decay = jnp.where(diff >= 0, jnp.exp(log_gamma[:, None, None] * jnp.maximum(diff, 0.0)), 0.0)
    scores = jnp.einsum('bnihd,bnjhd->bnhij', qc, kc) * decay[None, None]
    y_inner = jnp.einsum('bnhij,bnjhd->bnihd', scores, vc)
    k_w = jnp.exp(log_gamma[None, :] * (RET_CHUNK - 1.0 - idx)[:, None])
    u = jnp.einsum('bnjhd,bnjhe,jh->bnhde', kc, vc, k_w)
    chunk_decay = jnp.exp(log_gamma * RET_CHUNK)[None, :, None, None]

    def step(state, u_n):
        return chunk_decay * state + u_n, state

    init = jnp.zeros((bsz, RET_HEADS, HEAD_DIM, HEAD_DIM), jnp.float32)
    _, prev_states = lax.scan(step, init, u.transpose(1, 0, 2, 3, 4))
    q_w = jnp.exp(log_gamma[None, :] * (idx + 1.0)[:, None])
    y_cross = jnp.einsum('bnihd,nbhde,ih->bnihe', qc, prev_states, q_w)
    y = (y_inner + y_cross).reshape(bsz, s, RET_HEADS, HEAD_DIM)
    mu = jnp.mean(y, axis=-1, keepdims=True)
    var = jnp.mean(jnp.square(y - mu), axis=-1, keepdims=True)
    y = ((y - mu) * lax.rsqrt(var + EPS)).reshape(bsz, s, RET_WIDTH)
    return (jax.nn.silu(g.astype(jnp.float32)) * y).astype(g.dtype)

def parallel_mixer(h, positions, w_in, conv_w, conv_b, w_rg, b_rg, w_ig, b_ig, lru_lambda, fox_b_f, w_out):
    proj = h @ w_in
    lx, ly, fq, fk, fv, ff, rq, rk, rv, rg = jnp.split(proj, np.cumsum(SPLIT_SIZES)[:-1].tolist(), axis=-1)
    lru_out = rg_lru(causal_depthwise_conv(lx, conv_w, conv_b), w_rg, b_rg, w_ig, b_ig, lru_lambda) * jax.nn.gelu(ly)
    fox_out = forgetting_attention(fq, fk, fv, ff, fox_b_f)
    ret_out = retention(rq, rk, rv, rg, positions)
    return jnp.concatenate([lru_out, fox_out.astype(h.dtype), ret_out], axis=-1) @ w_out

def memory_cross_attention(h, mem_n, w_q, w_k, w_v, w_o):
    bsz, s, _ = h.shape
    m = mem_n.shape[1]
    q = (h @ w_q).reshape(bsz, s, CROSS_HEADS, CROSS_HEAD_DIM)
    k = (mem_n @ w_k).reshape(bsz, m, CROSS_HEADS, CROSS_HEAD_DIM)
    v = (mem_n @ w_v).reshape(bsz, m, CROSS_HEADS, CROSS_HEAD_DIM)
    logits = jnp.einsum('bshd,bmhd->bhsm', q, k).astype(jnp.float32) * CROSS_HEAD_DIM ** -0.5
    p = jax.nn.softmax(logits, axis=-1)
    o = jnp.einsum('bhsm,bmhd->bshd', p.astype(v.dtype), v).reshape(bsz, s, D_MODEL)
    return o @ w_o

def swiglu(h, w_gate, w_up, w_down):
    return (jax.nn.silu(h @ w_gate) * (h @ w_up)) @ w_down

def first_inputs(seed: int = 0) -> dict:
    key = jax.random.key(seed)
    ks = jax.random.split(key, 32)

    def nrm(k, shape, scale):
        return scale * jax.random.normal(k, shape, jnp.float32)

    def gain(k, shape):
        return 1.0 + 0.02 * jax.random.normal(k, shape, jnp.float32)

    u = jax.random.uniform(ks[12], (DEPTH, LRU_WIDTH), jnp.float32, 0.9, 0.999)
    a_base = u ** (1.0 / LRU_C)
    lru_lambda = jnp.log(a_base) - jnp.log1p(-a_base)
    return {
        'x': nrm(ks[0], (BATCH, SEQ, D_MODEL), 1.0),
        'mem': nrm(ks[1], (BATCH, MEM_LEN, D_MODEL), 1.0),
        'positions': jnp.tile(jnp.arange(SEQ, dtype=jnp.int32)[None, :], (BATCH, 1)),
        'pre_mix_g': gain(ks[2], (DEPTH, D_MODEL)),
        'post_mix_g': gain(ks[3], (DEPTH, D_MODEL)),
        'w_in': nrm(ks[4], (DEPTH, D_MODEL, IN_WIDTH), D_MODEL ** -0.5),
        'conv_w': nrm(ks[5], (DEPTH, CONV_WIDTH, LRU_WIDTH), CONV_WIDTH ** -0.5),
        'conv_b': nrm(ks[6], (DEPTH, LRU_WIDTH), 0.01),
        'w_rg': nrm(ks[7], (DEPTH, LRU_BLOCKS, LRU_BLOCK, LRU_BLOCK), LRU_BLOCK ** -0.5),
        'b_rg': nrm(ks[8], (DEPTH, LRU_WIDTH), 0.01),
        'w_ig': nrm(ks[9], (DEPTH, LRU_BLOCKS, LRU_BLOCK, LRU_BLOCK), LRU_BLOCK ** -0.5),
        'b_ig': nrm(ks[10], (DEPTH, LRU_WIDTH), 0.01),
        'lru_lambda': lru_lambda,
        'fox_b_f': 2.0 + nrm(ks[11], (DEPTH, FOX_HEADS), 0.5),
        'w_out': nrm(ks[13], (DEPTH, MIX_WIDTH, D_MODEL), MIX_WIDTH ** -0.5),
        'pre_cross_g': gain(ks[14], (DEPTH, D_MODEL)),
        'post_cross_g': gain(ks[15], (DEPTH, D_MODEL)),
        'mem_norm_g': gain(ks[16], (D_MODEL,)),
        'w_cq': nrm(ks[17], (DEPTH, D_MODEL, D_MODEL), D_MODEL ** -0.5),
        'w_ck': nrm(ks[18], (DEPTH, D_MODEL, D_MODEL), D_MODEL ** -0.5),
        'w_cv': nrm(ks[19], (DEPTH, D_MODEL, D_MODEL), D_MODEL ** -0.5),
        'w_co': nrm(ks[20], (DEPTH, D_MODEL, D_MODEL), D_MODEL ** -0.5),
        'pre_ffn_g': gain(ks[21], (DEPTH, D_MODEL)),
        'post_ffn_g': gain(ks[22], (DEPTH, D_MODEL)),
        'w_gate': nrm(ks[23], (DEPTH, D_MODEL, D_FF), D_MODEL ** -0.5),
        'w_up': nrm(ks[24], (DEPTH, D_MODEL, D_FF), D_MODEL ** -0.5),
        'w_down': nrm(ks[25], (DEPTH, D_FF, D_MODEL), D_FF ** -0.5),
    }

def first_block(x, mem, positions, pre_mix_g, post_mix_g, w_in, conv_w, conv_b, w_rg, b_rg, w_ig, b_ig, lru_lambda, fox_b_f, w_out, pre_cross_g, post_cross_g, mem_norm_g, w_cq, w_ck, w_cv, w_co, pre_ffn_g, post_ffn_g, w_gate, w_up, w_down):
    mem_n = rms_norm(mem, mem_norm_g)
    for l in range(DEPTH):
        h = rms_norm(x, pre_mix_g[l])
        mix = parallel_mixer(h, positions, w_in[l], conv_w[l], conv_b[l], w_rg[l], b_rg[l], w_ig[l], b_ig[l], lru_lambda[l], fox_b_f[l], w_out[l])
        x = x + rms_norm(mix, post_mix_g[l])
        h = rms_norm(x, pre_cross_g[l])
        x = x + rms_norm(memory_cross_attention(h, mem_n, w_cq[l], w_ck[l], w_cv[l], w_co[l]), post_cross_g[l])
        h = rms_norm(x, pre_ffn_g[l])
        x = x + rms_norm(swiglu(h, w_gate[l], w_up[l], w_down[l]), post_ffn_g[l])
    return x


DEPTH_2 = 1

D_MIX = D_MODEL
N_HEADS = 8
N_KV_HEADS = 2
D_ATTN = N_HEADS * HEAD_DIM
D_KV = N_KV_HEADS * HEAD_DIM
WINDOW = 128
BLOCK = 128
D_GMLP = D_MIX - D_ATTN
CHUNK = 128
N_GMLP_GROUPS = 8
GMLP_GROUP_DIM = D_GMLP // N_GMLP_GROUPS
D_IN = D_ATTN + 2 * D_KV + 2 * D_GMLP
N_EXPERTS = 16
CAPACITY_FACTOR = 2
D_FF_EXPERT = 2816
MASK_VALUE = -1e30


def rms_norm_2(x, g):
    xf = x.astype(jnp.float32)
    y = xf * lax.rsqrt(jnp.mean(xf * xf, axis=-1, keepdims=True) + EPS)
    return (y * g.astype(jnp.float32)).astype(x.dtype)

def layer_norm(x, g, b):
    xf = x.astype(jnp.float32)
    mu = jnp.mean(xf, axis=-1, keepdims=True)
    xc = xf - mu
    y = xc * lax.rsqrt(jnp.mean(xc * xc, axis=-1, keepdims=True) + EPS)
    return (y * g.astype(jnp.float32) + b.astype(jnp.float32)).astype(x.dtype)

def modulate(h, shift, scale):
    return h * (1 + scale[:, None, :]) + shift[:, None, :]

def alibi_slopes(n):
    return jnp.exp2(-8.0 * jnp.arange(1, n + 1, dtype=jnp.float32) / n)

def windowed_gqa(q, k, v, sink):
    b, s = q.shape[:2]
    nb = s // BLOCK
    g = N_HEADS // N_KV_HEADS
    qb = q.reshape(b, nb, BLOCK, N_KV_HEADS, g, HEAD_DIM)

    def band(t):
        tp = jnp.pad(t, ((0, 0), (BLOCK, BLOCK), (0, 0), (0, 0)))
        tp = tp.reshape(b, nb + 2, BLOCK, N_KV_HEADS, HEAD_DIM)
        return jnp.concatenate([tp[:, :-2], tp[:, 1:-1], tp[:, 2:]], axis=2)

    kb, vb = band(k), band(v)
    scores = jnp.einsum('bnqkgd,bnskd->bnkgqs', qb, kb).astype(jnp.float32) * (HEAD_DIM ** -0.5)
    blk = jnp.arange(nb)[:, None] * BLOCK
    q_pos = blk + jnp.arange(BLOCK)[None, :]
    k_pos = blk - BLOCK + jnp.arange(3 * BLOCK)[None, :]
    dist = jnp.abs(q_pos[:, :, None] - k_pos[:, None, :])
    valid = (dist <= WINDOW) & (k_pos[:, None, :] >= 0) & (k_pos[:, None, :] < s)
    slopes = alibi_slopes(N_HEADS).reshape(N_KV_HEADS, g)
    scores = scores - slopes[:, :, None, None] * dist[None, :, None, None].astype(jnp.float32)
    scores = jnp.where(valid[None, :, None, None], scores, MASK_VALUE)
    sink_l = sink.astype(jnp.float32).reshape(N_KV_HEADS, g)[:, :, None]
    m = jnp.maximum(scores.max(axis=-1), sink_l)
    p = jnp.exp(scores - m[..., None])
    denom = p.sum(axis=-1) + jnp.exp(sink_l - m)
    probs = (p / denom[..., None]).astype(v.dtype)
    out = jnp.einsum('bnkgqs,bnskd->bnqkgd', probs, vb)
    return out.reshape(b, s, D_ATTN)

def spatial_gating(u, v, ln_g, ln_b, w_s, b_s):
    b, s = v.shape[:2]
    nb = s // CHUNK
    vn = layer_norm(v, ln_g, ln_b).reshape(b, nb, CHUNK, N_GMLP_GROUPS, GMLP_GROUP_DIM)
    z = jnp.einsum('gts,bnsgc->bntgc', w_s, vn) + b_s.T[:, :, None]
    return u * z.reshape(b, s, D_GMLP)

def expert_choice_ffn(h, w_router, w_gate, w_up, w_down):
    b, s, d = h.shape
    cap = CAPACITY_FACTOR * s // N_EXPERTS
    aff = jax.nn.softmax((h @ w_router).astype(jnp.float32), axis=-1)
    gates, idx = lax.top_k(jnp.swapaxes(aff, 1, 2), cap)
    xs = jax.vmap(lambda hb, ib: hb[ib])(h, idx)
    hid = jax.nn.silu(jnp.einsum('becd,edf->becf', xs, w_gate)) * jnp.einsum('becd,edf->becf', xs, w_up)
    out = jnp.einsum('becf,efd->becd', hid, w_down) * gates[..., None].astype(h.dtype)
    return jax.vmap(lambda ob, ib: jnp.zeros((s, d), h.dtype).at[ib.reshape(-1)].add(ob.reshape(-1, d)))(out, idx)

def second_inputs(seed: int = 0) -> dict:
    key = jax.random.key(seed)
    ks = jax.random.split(key, 24)
    nrm = jax.random.normal
    L, D = DEPTH_2, D_MODEL
    return {
        "x": nrm(ks[0], (BATCH, SEQ, D), jnp.float32),
        "c": nrm(ks[1], (BATCH, D), jnp.float32),
        "w_ada": nrm(ks[2], (L, D, 6 * D), jnp.float32) * (0.5 * D ** -0.5),
        "b_ada": 0.01 * nrm(ks[3], (L, 6 * D), jnp.float32),
        "norm_pre_mix": 1.0 + 0.1 * nrm(ks[4], (L, D), jnp.float32),
        "norm_post_mix": 1.0 + 0.1 * nrm(ks[5], (L, D), jnp.float32),
        "w_in": nrm(ks[6], (L, D, D_IN), jnp.float32) * D ** -0.5,
        "sink": 0.5 * nrm(ks[7], (L, N_HEADS), jnp.float32),
        "sgu_ln_g": 1.0 + 0.1 * nrm(ks[8], (L, D_GMLP), jnp.float32),
        "sgu_ln_b": 0.01 * nrm(ks[9], (L, D_GMLP), jnp.float32),
        "w_s": nrm(ks[10], (L, N_GMLP_GROUPS, CHUNK, CHUNK), jnp.float32) * CHUNK ** -0.5,
        "b_s": 1.0 + 0.1 * nrm(ks[11], (L, N_GMLP_GROUPS, CHUNK), jnp.float32),
        "norm_out_attn": 1.0 + 0.1 * nrm(ks[12], (L, D_ATTN), jnp.float32),
        "norm_out_gmlp": 1.0 + 0.1 * nrm(ks[13], (L, D_GMLP), jnp.float32),
        "w_out": nrm(ks[14], (L, D_MIX, D), jnp.float32) * D_MIX ** -0.5,
        "norm_pre_ffn": 1.0 + 0.1 * nrm(ks[15], (L, D), jnp.float32),
        "norm_post_ffn": 1.0 + 0.1 * nrm(ks[16], (L, D), jnp.float32),
        "w_router": nrm(ks[17], (L, D, N_EXPERTS), jnp.float32) * D ** -0.5,
        "w_gate": nrm(ks[18], (L, N_EXPERTS, D, D_FF_EXPERT), jnp.float32) * D ** -0.5,
        "w_up": nrm(ks[19], (L, N_EXPERTS, D, D_FF_EXPERT), jnp.float32) * D ** -0.5,
        "w_down": nrm(ks[20], (L, N_EXPERTS, D_FF_EXPERT, D), jnp.float32) * D_FF_EXPERT ** -0.5,
    }

def second_block(x, c, w_ada, b_ada, norm_pre_mix, norm_post_mix, w_in, sink, sgu_ln_g, sgu_ln_b,
              w_s, b_s, norm_out_attn, norm_out_gmlp, w_out, norm_pre_ffn, norm_post_ffn,
              w_router, w_gate, w_up, w_down):
    b, s, _ = x.shape
    for l in range(DEPTH_2):
        mod = jax.nn.silu(c) @ w_ada[l] + b_ada[l]
        shift1, scale1, gate1, shift2, scale2, gate2 = jnp.split(mod, 6, axis=-1)

        h = modulate(rms_norm_2(x, norm_pre_mix[l]), shift1, scale1)
        proj = h @ w_in[l]
        q, k, v, zg = jnp.split(proj, [D_ATTN, D_ATTN + D_KV, D_ATTN + 2 * D_KV], axis=-1)
        attn = windowed_gqa(q.reshape(b, s, N_HEADS, HEAD_DIM),
                            k.reshape(b, s, N_KV_HEADS, HEAD_DIM),
                            v.reshape(b, s, N_KV_HEADS, HEAD_DIM), sink[l])
        u, vg = jnp.split(jax.nn.gelu(zg), 2, axis=-1)
        gm = spatial_gating(u, vg, sgu_ln_g[l], sgu_ln_b[l], w_s[l], b_s[l])
        mix = jnp.concatenate([rms_norm_2(attn, norm_out_attn[l]), rms_norm_2(gm, norm_out_gmlp[l])], axis=-1)
        x = x + gate1[:, None, :] * rms_norm_2(mix @ w_out[l], norm_post_mix[l])

        h2 = modulate(rms_norm_2(x, norm_pre_ffn[l]), shift2, scale2)
        y = expert_choice_ffn(h2, w_router[l], w_gate[l], w_up[l], w_down[l])
        x = x + gate2[:, None, :] * rms_norm_2(y, norm_post_ffn[l])
    return x


def setup_inputs(seed=0):
    out = dict(first_inputs(seed))
    for name, value in second_inputs(seed + 1).items():
        if name != "x":
            out[name + "_2"] = value
    return out


def reference(
    x, mem, positions, pre_mix_g, post_mix_g, w_in, conv_w, conv_b, w_rg, b_rg, w_ig, b_ig,
    lru_lambda, fox_b_f, w_out, pre_cross_g, post_cross_g, mem_norm_g, w_cq, w_ck, w_cv, w_co,
    pre_ffn_g, post_ffn_g, w_gate, w_up, w_down, c_2, w_ada_2, b_ada_2, norm_pre_mix_2,
    norm_post_mix_2, w_in_2, sink_2, sgu_ln_g_2, sgu_ln_b_2, w_s_2, b_s_2, norm_out_attn_2,
    norm_out_gmlp_2, w_out_2, norm_pre_ffn_2, norm_post_ffn_2, w_router_2, w_gate_2, w_up_2,
    w_down_2,
):
    x = first_block(
        x, mem, positions, pre_mix_g, post_mix_g, w_in, conv_w, conv_b, w_rg, b_rg, w_ig, b_ig,
        lru_lambda, fox_b_f, w_out, pre_cross_g, post_cross_g, mem_norm_g, w_cq, w_ck, w_cv,
        w_co, pre_ffn_g, post_ffn_g, w_gate, w_up, w_down,
    )
    return second_block(
        x, c_2, w_ada_2, b_ada_2, norm_pre_mix_2, norm_post_mix_2, w_in_2, sink_2, sgu_ln_g_2,
        sgu_ln_b_2, w_s_2, b_s_2, norm_out_attn_2, norm_out_gmlp_2, w_out_2, norm_pre_ffn_2,
        norm_post_ffn_2, w_router_2, w_gate_2, w_up_2, w_down_2,
    )


_drawn_inputs = setup_inputs


def setup_inputs(seed=0):
    import zlib

    import numpy as np

    out = dict(_drawn_inputs(seed))
    spreads = {}
    factors = {'b_rg': 8.0,
     'b_ig': 8.0,
     'post_ffn_g': 3.208,
     'b_ada_2': 6.329,
     'norm_pre_mix_2': 3.564,
     'norm_post_mix_2': 4.075,
     'sink_2': 64.0,
     'sgu_ln_g_2': 21.609,
     'sgu_ln_b_2': 200.0,
     'b_s_2': 5.673,
     'norm_out_attn_2': 5.071,
     'norm_out_gmlp_2': 5.338,
     'norm_post_ffn_2': 4.462}
    for name, (base, spread) in spreads.items():
        noise = np.random.default_rng([zlib.crc32(name.encode()), seed]).standard_normal(out[name].shape)
        drawn = base * np.exp(spread * noise) if base else spread * noise
        out[name] = __import__('jax').numpy.asarray(drawn.astype(out[name].dtype))
    for name, factor in factors.items():
        out[name] = (out[name] * factor).astype(out[name].dtype)
    return out
```

```python
from contextlib import ExitStack

import numpy as np

import concourse.bass as bass
from concourse import mybir

F32 = mybir.dt.float32
I32 = mybir.dt.int32
ALU = mybir.AluOpType
ACT = mybir.ActivationFunctionType
AX = mybir.AxisListType
EPS = 1e-6
NEG = -1e30

PC = {}


def _col(name, n):
    PC[name] = (PC["n"], PC["n"] + n)
    PC["n"] += n


PC["n"] = 0
for _l in range(2):
    for _n, _k in (("pre_mix", 8), ("pre_cross", 8), ("pre_ffn", 8), ("conv_w", 8), ("conv_b", 2),
                   ("b_rg", 2), ("b_ig", 2), ("lam", 2)):
        _col(f"{_n}{_l}", _k)
for _n, _k in (("mem", 8), ("npm2", 8), ("noa2", 4), ("nog2", 4), ("npf2", 8), ("b_ada", 48), ("b_s", 8),
               ("c", 8)):
    _col(_n, _k)

CC = {"ident": (0, 128), "mask": (128, 384), "dec": (384, 1920), "dist": (1920, 2432), "rows": (2432, 2560),
      "freq": (2560, 2592), "iota": (2592, 2624)}
NCONST = 2624


def constants():
    c = np.zeros((128, NCONST), np.float32)
    p = np.arange(128)
    c[:, 0:128] = np.eye(128)
    c[:, 256:384] = np.where(p[None, :] <= p[:, None], 0.0, NEG)
    gamma = np.log1p(-np.exp2(-5.0 - np.arange(4)))
    diff = p[None, :] - p[:, None]
    for h in range(4):
        own = np.where(diff >= 0, np.exp(gamma[h] * np.maximum(diff, 0)), 0.0) / 8
        c[:, 384 + 384 * h:512 + 384 * h] = own
        c[:, 512 + 384 * h:640 + 384 * h] = np.exp(gamma[h] * (diff + 128)) / 8
        c[:, 640 + 384 * h:768 + 384 * h] = own
    for t in range(2):
        d = np.abs(128 * t + p[:, None] - np.arange(256)[None, :])
        c[:, 1920 + 256 * t:2176 + 256 * t] = np.where(d <= 128, -d, -1e33)
    c[:, 2432:2560] = (p % 32 == 0)[:, None]
    c[:, 2560:2592] = (10000.0 ** (-np.arange(32, dtype=np.float32) / np.float32(32))).astype(np.float32)
    c[:, 2592:2624] = 1 + np.arange(32)
    return c


class Queue:

    def __init__(self, key):
        self.key, self.items, self.n, self.seen = key, [], 0, {}

    def wait(self, *toks):
        for t in toks:
            if t is None:
                continue
            if isinstance(t, list):
                self.wait(*t)
            elif self.seen.get(t[0], 0) < t[1]:
                self.seen[t[0]] = t[1]
                self.items.append((t[0], t[1], None))

    def do(self, fn, *toks):
        self.wait(*toks)
        self.n += 1
        self.items.append((self.key, 1, fn))
        return (self.key, self.n)

    def quiet(self, fn, *toks):
        self.wait(*toks)
        self.items.append((None, 0, fn))

    def dma(self, count, key, fn, *toks):
        self.wait(*toks)
        count[key] = count.get(key, 0) + 16
        self.items.append((key, 16, fn))
        return (key, count[key])


class Slots:

    def __init__(self, bufs):
        self.bufs, self.at, self.freed, self.held = bufs, 0, [None] * len(bufs), set()

    def take(self):
        i = self.at % len(self.bufs)
        while i in self.held:
            i = (i + 1) % len(self.bufs)
        self.at = i + 1
        self.held.add(i)
        return i, self.bufs[i], self.freed[i]

    def free(self, i, *toks):
        self.freed[i] = list(toks)
        self.held.discard(i)


def program(nc, D, out, stage=99):
    ctx = ExitStack()
    with ctx:
        _program(nc, ctx, D, out, stage)


def _program(nc, ctx, D, out, stage):
    def sb(name, shape, dt=F32):
        return ctx.enter_context(nc.sbuf_tensor(name, shape, dt))

    keys = ["pe", "act", "dve", "pool", "x", "mem", "cst", "par", "sm", "gb", "ga", "ln", "bd", "wf", "ws", "wr", "out"]
    keys += [f"w{i}" for i in range(11)]
    sems = {k: ctx.enter_context(nc.semaphore("s_" + k)) for k in keys}
    PE, AC, DV, PO, SP = Queue("pe"), Queue("act"), Queue("dve"), Queue("pool"), Queue("sp")
    count = {}

    W = sb("W", [128, 16896])
    CST = sb("CST", [128, NCONST])
    PT = sb("PT", [128, PC["n"]])
    X = sb("X", [128, 2, 1024])
    XN = sb("XN", [128, 2, 1024])
    HT = sb("HT", [128, 8, 256])
    MX = sb("MX", [128, 8, 256])
    CK = sb("CK", [128, 8, 256])
    CV = sb("CV", [128, 2, 1024])
    GA = sb("GA", [128, 2, 1024])
    GB = sb("GB", [128, 1024])
    S = sb("S", [128, 10240])
    T = sb("T", [128, 288])
    PS = ctx.enter_context(nc.psum_tensor("PS", [128, 8, 512], F32))

    place = [0]

    def small(n):
        place[0] += n
        assert place[0] <= 288, place
        return T[:, place[0] - n:place[0]]

    ID = CST[:, 0:128]

    def par(name, i=0, n=None):
        a, b = PC[name]
        return PT[:, a + i:a + i + (n or 1)]

    def flat(ap):
        return ap.rearrange("p a b -> p (a b)")

    def mm(o, l, r, start, stop, *toks, inc=False):
        fn = lambda e: e.matmul(o, l, r, start=start, stop=stop, skip_group_check=True)
        return PE.do(fn, *toks) if inc else PE.quiet(fn, *toks)

    def tr(o, i, *toks, inc=False):
        fn = lambda e: e.transpose(o, i, ID)
        return PE.do(fn, *toks) if inc else PE.quiet(fn, *toks)

    def act(o, i, f, *toks, **kw):
        return AC.do(lambda e: e.activation(o, i, f, **kw), *toks)

    def ts(o, i, s1, s2, o1, o2, *toks, q=DV):
        if s2 is None:
            return q.do(lambda e: e.tensor_scalar(o, i, s1, None, o1), *toks)
        return q.do(lambda e: e.tensor_scalar(o, i, s1, s2, o1, o2), *toks)

    def tt(o, a, b, op, *toks, q=DV):
        return q.do(lambda e: e.tensor_tensor(o, a, b, op), *toks)

    def stt(o, a, s, b, o1, o2, *toks):
        return DV.do(lambda e: e.scalar_tensor_tensor(out=o, in0=a, scalar=s, in1=b, op0=o1, op1=o2), *toks)

    def copy(o, i, *toks, q=DV):
        return q.do(lambda e: e.tensor_copy(o, i), *toks)

    def red(o, i, op, *toks, ax=AX.X):
        return DV.do(lambda e: e.tensor_reduce(o, i, ax, op), *toks)

    def load(key, o, i, *toks):
        return SP.dma(count, key, lambda e: e.dma_start(o, i), *toks)

    ring = Slots([W[:, 2048 * i:2048 * (i + 1)] for i in range(8)])

    def take_w(src, shape):
        i, buf, freed = ring.take()
        a, b = shape
        v = buf[:, 0:a * b].rearrange("p (a b) -> p a b", a=a)
        return i, v, load(f"w{i}", v, src, freed)

    def cols(w, n, width=256):
        return take_w(w[:, n:n + width].rearrange("(k p) n -> p k n", p=128), (8, width))

    def rows(w, n):
        return take_w(w[n:n + 256, :].rearrange("(k p) n -> p k n", p=128), (2, 1024))

    banks = Slots([PS[:, i, :] for i in range(4, 8)])

    def two(b):
        return b.rearrange("p (a b) -> p a b", a=2)

    def proj_t(w, n, src, *toks):
        i, u, got = cols(w, n)
        b, ps, freed = banks.take()
        ps = two(ps)
        PE.wait(got, freed, list(toks))
        for m in range(2):
            for k in range(8):
                t = mm(ps[:, m, :], u[:, k, 128 * m:128 * m + 128], src[:, k, :], k == 0, k == 7, inc=(m == 1 and k == 7))
        ring.free(i, t)
        return b, ps, t

    def proj_r(w, n, src, *toks):
        i, u, got = cols(w, n)
        b, ps, freed = banks.take()
        ps = two(ps)
        PE.wait(got, freed, list(toks))
        for m in range(2):
            for k in range(8):
                t = mm(ps[:, m, :], src[:, k, 128 * m:128 * m + 128], u[:, k, :], k == 0, k == 7, inc=(m == 1 and k == 7))
        ring.free(i, t)
        return b, ps, t

    yfree = [None] * 4

    def proj_y(w, n_units, src, *toks):
        PE.wait(list(toks))
        for u0 in range(n_units):
            i, u, got = rows(w, 256 * u0)
            PE.wait(got)
            for t in range(2):
                for kk in range(2):
                    k = 2 * u0 + kk
                    for h in range(2):
                        if k == 0:
                            PE.wait(yfree[2 * t + h])
                        tok = mm(PS[:, 2 * t + h, :], src[:, k, 128 * t:128 * t + 128], u[:, kk, 512 * h:512 * h + 512],
                                 k == 0, k == 2 * n_units - 1, inc=(kk == 1 and h == 1))
                if t == 0:
                    first = tok
            ring.free(i, tok)
        return [first, tok]

    half = small(1)
    mhalf = small(1)
    zero = small(1)
    junk_free = [None]
    ss4 = small(4)
    ms = small(2)
    rs = small(2)
    rs2 = small(2)
    spl = small(4)
    sp1, sp2, sp3, sp4, sp5 = small(4), small(4), small(4), small(4), small(4)
    hb = small(8)
    cs = small(8)
    MT = small(32)
    gs = small(16)
    bf = small(2)
    snk = small(8)
    nmx = small(16)
    mxx = small(16)
    sms = small(16)
    rcp = small(16)
    esk = small(16)
    st6 = small(12)
    mv = small(4)
    s8 = [small(8) for _ in range(5)]
    posf = small(2)
    aff = small(32)
    amx = small(2)
    asm = small(2)
    CB = sb("CB", [128, 8, 32])
    AD = sb("AD", [128, 256])
    CSN = sb("CSN", [128, 4, 32])
    BD = sb("BD", [128, 4, 128])
    WF = sb("WF", [128, 8, 8])
    JK = sb("JK", [128, 1024])
    PP = [sb(f"PP{i}", [128, 512]) for i in range(3)]
    PQ = [sb(f"PQ{i}", [128, 512]) for i in range(2)]

    pp, pq = Slots(PP), Slots(PQ)

    t_x = [load("x", X[:, t, :], D["x"][0, 128 * t:128 * t + 128, :]) for t in range(2)][1]
    t_mem = [load("mem", XN[:, t, :], D["mem"][0, 128 * t:128 * t + 128, :]) for t in range(2)][1]
    t_cst = load("cst", CST[:, :], D["consts"])
    t_par = load("par", PT[:, :], D["params"])
    load("sm", posf[:, :].bitcast(I32), D["positions_t"])
    load("sm", bf[0:8, :], D["fox_b_t"])
    t_sm = load("sm", snk, D["sink_2"].broadcast_to([128, 8]))
    t_ga = [load("ga", GA[:, g, :], D["b_ada_2"][0:1, 2048 + 3072 * g:3072 + 3072 * g].broadcast_to([128, 1024]))
            for g in range(2)][1]
    PO.do(lambda e: e.memset(half, 0.5))
    PO.do(lambda e: e.memset(mhalf, -0.5))
    PO.do(lambda e: e.memset(zero, 0.0))
    t_set = PO.do(lambda e: e.memset(flat(BD[:, :, :]), 0.0))
    DV.wait(t_set)
    AC.wait(t_set)

    def power(o, i, which, n, *toks):
        e = which if n == 1 else which.broadcast_to([128, n])
        return tt(o, i, e, ALU.pow, t_set, *toks, q=PO)

    def rstd(o, tiles, n, *toks, scr=None):
        t = None
        parts = len(tiles[0])
        for a, tile in enumerate(tiles):
            for b, part in enumerate(tile):
                w = part.shape[-1]
                tk = toks[a] if a < len(toks) else None
                t = act(scr[:, 0:w], part, ACT.Square, tk, accum_out=ss4[:, parts * a + b:parts * a + b + 1],
                        *[]) if False else AC.do(
                    lambda e, part=part, w=w, c=parts * a + b: e.activation(scr[:, 0:w], part, ACT.Square,
                                                                          accum_out=ss4[:, c:c + 1]),
                    tk, (AC.key, AC.n) if AC.n else None, ss_free[0])
        if parts == 2:
            t = tt(ms, ss4[:, 0:4:2], ss4[:, 1:4:2], ALU.add, t)
            t = ts(ms, ms, 1.0 / n, EPS, ALU.mult, ALU.add, t)
        else:
            t = ts(ms, ss4[:, 0:2], 1.0 / n, EPS, ALU.mult, ALU.add, t)
        ss_free[0] = t
        return power(o, ms, mhalf, 2, t)

    ss_free = [None]

    def turn(srcs, dst, chunks, gain, bias, *toks):
        PE.wait(t_cst)
        last = []
        for k0 in range(0, chunks, 2):
            b, ps, freed = banks.take()
            ps = two(ps)
            PE.wait(freed, list(toks))
            for k in (0, 1):
                for t in range(2):
                    tk = tr(ps[:, k, 128 * t:128 * t + 128], srcs[t][:, 128 * (k0 + k):128 * (k0 + k) + 128],
                            inc=(k == 1 and t == 1))
            e = []
            for k in (0, 1):
                o, i = dst[:, k0 + k, :], ps[:, k, :]
                g = gain[:, k0 + k:k0 + k + 1] if gain is not None else 1.0
                z = bias[:, k0 + k:k0 + k + 1] if bias is not None else 0.0
                if k0 % 4:
                    e.append(act(o, i, ACT.Identity, tk, t_par, scale=g, bias=z))
                elif gain is None:
                    e.append(copy(o, i, tk))
                else:
                    e.append(ts(o, i, g, z, ALU.mult, ALU.add, tk, t_par))
            banks.free(b, *e)
            last += e
        return last

    def pre_norm(gain, bias, *toks, src=X, dst=HT):
        r = rstd(rs, [[src[:, 0, :]], [src[:, 1, :]]], 1024, list(toks), scr=JK)
        a = [ts(XN[:, t, :], src[:, t, :], rs[:, t:t + 1], None, ALU.mult, None, r, list(toks)) for t in range(2)]
        xn_free[0] = a[1]
        return turn([XN[:, 0, :], XN[:, 1, :]], dst, 8, gain, bias, a[1])

    xn_free = [None]

    def post_norm(toks, gain, g_tok, src=None):
        src = src or [[PS[:, 2 * t + h, :] for h in range(2)] for t in range(2)]
        r = rstd(rs2, src, 1024, *toks, scr=JK)
        done = []
        for t in range(2):
            for h in range(2):
                o = XN[:, t, 512 * h:512 * h + 512]
                a = stt(o, src[t][h], rs2[:, t:t + 1], gain[:, 512 * h:512 * h + 512], ALU.mult, ALU.mult, r, g_tok)
                yfree[2 * t + h] = a
                xs = X[:, t, 512 * h:512 * h + 512]
                done.append(tt(xs, xs, o, ALU.add, a))
        return done[-1]

    gb_free = [None]

    def load_gain(row):
        return load("gb", GB[:, :], row.broadcast_to([128, 1024]), gb_free[0])

    AC.wait(t_par)
    DV.wait(t_par)
    for l in range(2):
        a = ts(sp1[:, 2 * l:2 * l + 2], par(f"lam{l}", 0, 2), -1.0, 0.0, ALU.mult, ALU.max)
        b = act(sp2[:, 2 * l:2 * l + 2], par(f"lam{l}", 0, 2), ACT.Abs)
    b = act(sp2, sp2, ACT.Exp, b, scale=-1.0)
    c = ts(sp3, sp2, 1.0, None, ALU.add, None, b)
    d = act(sp4, sp3, ACT.Ln, c)
    e = ts(sp5, sp3, -1.0, None, ALU.add, None, c)
    e = tt(sp5, sp2, sp5, ALU.subtract, e)
    e = tt(sp4, sp4, sp5, ALU.add, d, e)
    e = tt(sp4, sp4, sp1, ALU.add, e)
    t_spl = ts(spl, sp4, -4.0, None, ALU.mult, None, e)
    for l in range(2):
        ts(hb[:, 4 * l:4 * l + 2], par(f"b_rg{l}", 0, 2), 0.5, None, ALU.mult, None)
        t_hb = ts(hb[:, 4 * l + 2:4 * l + 4], par(f"b_ig{l}", 0, 2), 0.5, None, ALU.mult, None)
    a = act(cs, par("c", 0, 8), ACT.Tanh, scale=0.5)
    a = stt(cs, cs, 1.0, par("c", 0, 8), ALU.add, ALU.mult, a)
    a = ts(cs, cs, 0.5, None, ALU.mult, None, a)
    t_cb = copy(CB[:, :, :], cs.unsqueeze(2).broadcast_to([128, 8, 32]), a)
    ps_ = S[:, 0:64].rearrange("p (t f) -> p t f", t=2)
    n_ = S[:, 64:128].rearrange("p (t f) -> p t f", t=2)
    r_ = S[:, 128:256].rearrange("p (s t f) -> p s t f", s=2, t=2)
    a = copy(amx, posf.bitcast(I32), t_sm)
    DV.wait(t_cst)
    for t in range(2):
        b = ts(ps_[:, t, :], CST[:, 2560:2592], amx[:, t:t + 1], None, ALU.mult, None, a)
    TWO_PI = 2 * np.pi
    C1 = 6.28125
    C2 = float(np.float32(TWO_PI - C1))
    C2 = float(np.frombuffer((np.frombuffer(np.float32(C2).tobytes(), np.uint32) & np.uint32(0xFFFFF000)).tobytes(), np.float32)[0])
    C3 = float(TWO_PI - C1 - C2)
    BIG = 12582912.0
    for s in range(2):
        a = ts(n_, ps_, float(1 / TWO_PI), 0.25 * (1 - s), ALU.mult, ALU.add, b)
        a = ts(n_, n_, BIG, None, ALU.add, None, a)
        a = ts(n_, n_, -BIG, None, ALU.add, None, a)
        r = r_[:, s]
        a = stt(r, n_, -C1, ps_, ALU.mult, ALU.add, a)
        a = stt(r, n_, -C2, r, ALU.mult, ALU.add, a)
        a = stt(r, n_, -C3, r, ALU.mult, ALU.add, a)
        a = ts(r, r, (1 - s) * np.pi / 2, -3.1415925, ALU.add, ALU.max, a)
        b = a = ts(r, r, 3.1415925, None, ALU.min, None, a)
    t_rot = act(CSN[:, :, :].rearrange("p (s t) f -> p s t f", s=2), r_, ACT.Sin, a)

    memT = MX
    t_memT = pre_norm(par("mem", 0, 8), None, t_mem, src=XN, dst=memT)

    kv_free = [None, None]
    MEMT = sb("MEMT", [128, 8, 256])
    t_mc = copy(MEMT[:, :, :], MX[:, :, :], t_memT, t_memT)

    kv_tok = {}

    def fill_k(l, n):
        b, ps, t = proj_t(D["w_ck"][l], 256 * n, MEMT, t_mc)
        kv_tok[l, "k", n] = e = act(CK[:, 2 * n:2 * n + 2, :], ps, ACT.Copy, t, kv_free[0])
        banks.free(b, e)

    def fill_v(l, n):
        b, ps, t = proj_r(D["w_cv"][l], 256 * n, MEMT, t_mc)
        kv_tok[l, "v", n] = e = act(CV[:, :, 256 * n:256 * n + 256], ps, ACT.Copy, t, kv_free[1])
        banks.free(b, e)

    ad_free = [None]
    ada_tok = {}

    def fill_ada(n):
        i, u, got = cols(D["w_ada_2"][0], 256 * n)
        b, ps, freed = banks.take()
        PE.wait(got, freed, t_cb)
        for kk in range(2):
            for q in range(4):
                k = 4 * kk + q
                t = mm(ps[32 * q:32 * q + 32, 0:256], CB[:, k, :], u[:, k, :], kk == 0, kk == 1, inc=(k == 7))
        ring.free(i, t)
        e = act(AD[:, :], ps[:, 0:256], ACT.Copy, t, ad_free[0])
        sec, j = n // 4, n % 4
        if sec in (2, 5):
            t = mm(ps[:, 256:512], CST[:, 2432:2560], AD[:, :], True, True, e, t_cst, inc=True)
            o = GA[:, sec // 3, 256 * j:256 * j + 256]
            f = tt(o, ps[:, 256:512], o, ALU.add, t, t_ga)
        else:
            for m in range(2):
                t = mm(ps[:, 256 + m:257 + m], AD[:, 128 * m:128 * m + 128], CST[:, 2432:2433], True, True, e, t_cst,
                       inc=(m == 1))
            s = {0: 0, 1: 8, 3: 16, 4: 24}[sec] + 2 * j
            f = tt(MT[:, s:s + 2], ps[:, 256:258], par("b_ada", 8 * sec + 2 * j, 2), ALU.add, t)
            if sec in (1, 4):
                f = ts(MT[:, s:s + 2], MT[:, s:s + 2], 1.0, None, ALU.add, None, f)
        ad_free[0] = t
        ada_tok["last"] = f
        banks.free(b, f)

    filler = []

    def fill(n):
        for _ in range(min(n, len(filler))):
            filler.pop(0)()

    def view(a, shape):
        n = int(np.prod(shape))
        v = S[:, a:a + n]
        if len(shape) == 2:
            v = v.rearrange("p (a b) -> p a b", a=shape[0])
        elif len(shape) == 3:
            v = v.rearrange("p (a b c) -> p a b c", a=shape[0], b=shape[1])
        return v

    def gelu2(o, y, t1, t2, *toks, q=None):
        q = q or DV
        a = tt(t1, y, y, ALU.mult, *toks, q=q)
        a = ts(t1, t1, 0.044715, 1.0, ALU.mult, ALU.add, a, q=q)
        a = tt(t1, t1, y, ALU.mult, a, q=q)
        a = act(t2, t1, ACT.Tanh, a, scale=float(np.sqrt(2 / np.pi)))
        return stt(o, t2, 1.0, y, ALU.add, ALU.mult, a)

    def softmax_turn(src, n_tiles, widths):
        pass

    def mixer(l, t_h):
        w = D["w_in"][l]
        QT, KT = view(0, (4, 256)), view(1024, (4, 256))
        V = view(2048, (2, 512))
        XC, LY = view(3072, (2, 256)), view(3584, (2, 256))
        A1, A2, A3, A4 = (view(4096 + 512 * i, (2, 256)) for i in range(4))
        LX = view(5120, (2, 259))
        RQ, RK, RV, RG = (view(6144 + 512 * i, (2, 256)) for i in range(4))
        QR, KR = view(8192, (2, 256)), view(8704, (2, 256))
        S1 = view(9216, (2, 256))
        R1, R2 = (JK[:, 256 * i:256 * i + 256].rearrange("p (t h f) -> p t h f", t=2, h=4) for i in range(2))
        ZF = [JK[0:8, 256 * i:256 * i + 256] for i in range(4)] + [S[0:8, 9728 + 256 * i:9984 + 256 * i] for i in range(2)]
        f_w = load("wf", WF[:, :, :], w[:, 2048:2056].rearrange("(k p) n -> p k n", p=128), t_h)
        b, ps, freed = banks.take()
        PE.wait(f_w, freed, t_h)
        for k in range(8):
            t = mm(ps[0:8, 0:256], WF[:, k, :], HT[:, k, :], k == 0, k == 7, inc=(k == 7))
        z = ts(ZF[0], ps[0:8, 0:256], bf[0:8, l:l + 1], None, ALU.add, None, t, t_sm)
        banks.free(b, z)
        a = act(ZF[1], ZF[0], ACT.Abs, z)
        a = act(ZF[1], ZF[1], ACT.Exp, a, scale=-1.0)
        c = ts(ZF[2], ZF[1], 1.0, None, ALU.add, None, a)
        d = act(ZF[3], ZF[2], ACT.Ln, c)
        e = ts(ZF[2], ZF[2], -1.0, None, ALU.add, None, c, d)
        e = tt(ZF[2], ZF[1], ZF[2], ALU.subtract, e)
        e = tt(ZF[3], ZF[3], ZF[2], ALU.add, e, d)
        e = stt(ZF[2], ZF[0], 0.0, ZF[3], ALU.min, ALU.subtract, e)
        e = DV.do(lambda g: g.tensor_tensor_scan(ZF[4], ZF[2], zero[0:8, :].broadcast_to([8, 256]), 0.0, ALU.add, ALU.add), e)
        t_c = ts(ZF[5], ZF[4], -1.0, None, ALU.mult, None, e)
        for n in range(2):
            b, ps, t = proj_t(w, 512 + 256 * n, HT)
            t_q = act(QT[:, 2 * n:2 * n + 2, :], ps, ACT.Copy, t, scale=0.125)
            banks.free(b, t_q)
            b, ps, t = proj_t(w, 1024 + 256 * n, HT)
            t_k = act(KT[:, 2 * n:2 * n + 2, :], ps, ACT.Copy, t)
            banks.free(b, t_k)
            b, ps, t = proj_r(w, 1536 + 256 * n, HT)
            t_v = act(V[:, :, 256 * n:256 * n + 256], ps, ACT.Copy, t)
            banks.free(b, t_v)
        b, ps, t = proj_t(w, 0, HT)
        DV.do(lambda e: e.memset(LX[:, :, 0:3], 0.0), t)
        e = copy(LX[:, :, 3:259], ps, t)
        banks.free(b, e)
        for c in range(2):
            cw = lambda j: par(f"conv_w{l}", 2 * j + c)
            o = XC[:, c, :]
            a = ts(o, LX[:, c, 3:259], cw(3), par(f"conv_b{l}", c), ALU.mult, ALU.add, e)
            for j in range(3):
                a = stt(o, LX[:, c, j:j + 256], cw(j), o, ALU.mult, ALU.add, a)
        t_xc = a
        b, ps, t = proj_t(w, 256, HT)
        e = act(LY, ps, ACT.Copy, t)
        banks.free(b, e)
        t_g = gelu2(flat(LY), flat(LY), flat(A1), flat(A2), e)
        w_bd = []
        for g, wg in enumerate(("w_rg", "w_ig")):
            for c in range(2):
                for h in range(2):
                    w_bd = load("bd", BD[64 * h:64 * h + 64, 2 * g + c, 64 * h:64 * h + 64], D[wg][l, 2 * c + h], t_h, t_set)
        gates = []
        for g in range(2):
            b, ps, freed = banks.take()
            ps = two(ps)
            PE.wait(freed, w_bd, t_xc)
            for c in range(2):
                t = mm(ps[:, c, :], BD[:, 2 * g + c, :], XC[:, c, :], True, True, inc=(c == 1))
            for c in range(2):
                o = (A3, A4)[g][:, c, :]
                a = act(o, ps[:, c, :], ACT.Tanh, t, t_hb, scale=0.5, bias=hb[:, 4 * l + 2 * g + c:4 * l + 2 * g + c + 1])
            banks.free(b, a)
            gates.append(a)
        t_bd[0] = t
        for c in range(2):
            a = ts(A3[:, c, :], A3[:, c, :], 1.0, spl[:, 2 * l + c:2 * l + c + 1], ALU.add, ALU.mult, gates[1], t_spl)
        b1 = act(flat(A1), flat(A3), ACT.Exp, a, t_g)
        b2 = act(flat(A2), flat(A3), ACT.Tanh, a, t_g, scale=-1.0)
        c1 = tt(flat(A3), flat(A1), flat(A1), ALU.mult, b1, b2)
        c1 = stt(flat(A3), flat(A3), 1.0, flat(A2), ALU.add, ALU.mult, c1)
        c2 = act(flat(A3), flat(A3), ACT.Sqrt, c1)
        d1 = stt(flat(A4), flat(A4), 1.0, flat(XC), ALU.add, ALU.mult, gates[1])
        d1 = stt(flat(A4), flat(A4), 0.5, flat(A3), ALU.mult, ALU.mult, d1, c2)
        for c in range(2):
            a = DV.do(lambda e, c=c: e.tensor_tensor_scan(A2[:, c, :], A1[:, c, :], A4[:, c, :], 0.0, ALU.mult, ALU.add), d1)
        t_lru = stt(flat(MX[:, 0:2, :]), flat(A2), 0.5, flat(LY), ALU.mult, ALU.mult, a, t_g, mx_free[0])
        rot = []
        for n, (raw, res) in enumerate(((A3, RQ), (A4, RK))):
            b, ps, t = proj_r(w, 2056 + 256 * n, HT)
            raw = (S1, QR)[n]
            e = act(raw, ps, ACT.Copy, t)
            banks.free(b, e)
            x = raw.rearrange("p t (h s f) -> p t h s f", h=4, s=2)
            o = res.rearrange("p t (h s f) -> p t h s f", h=4, s=2)
            cos = CSN[:, 0:2, :].unsqueeze(2).broadcast_to([128, 2, 4, 32])
            sin = CSN[:, 2:4, :].unsqueeze(2).broadcast_to([128, 2, 4, 32])
            for s, op in ((0, ALU.subtract), (1, ALU.add)):
                c1, c2 = (cos, sin) if s == 0 else (sin, cos)
                a1 = tt(R1, x[:, :, :, 0], c1, ALU.mult, e, t_rot, t_c, rot[-1:], q=PO)
                a2 = tt(R2, x[:, :, :, 1], c2, ALU.mult, e, rot[-1:], q=PO)
                rot.append(tt(o[:, :, :, s], R1, R2, op, a1, a2, q=PO))
        b, ps, t = proj_r(w, 2568, HT)
        t_rv = act(RV, ps, ACT.Copy, t)
        banks.free(b, t_rv)
        b, ps, t = proj_r(w, 2824, HT)
        t_th = act(S1, ps, ACT.Tanh, t, rot[1], scale=0.5)
        t_rg = stt(flat(RG), flat(S1), 1.0, flat(ps), ALU.add, ALU.mult, t_th)
        banks.free(b, t_rg)
        sc, pt, outs = {}, {}, {}

        def scores(h):
            c, po = h // 2, 64 * (h % 2)
            b, ps, freed = banks.take()
            PE.wait(freed, t_q, t_k, t_c, t_cst)
            one = ID[0:8, h:h + 1]
            for t in range(2):
                o = ps[:, 0:128] if t == 0 else ps[:, 128:384]
                nk = 128 * (t + 1)
                mm(o, QT[po:po + 64, c, 128 * t:128 * t + 128], KT[po:po + 64, c, 0:nk], True, False)
                mm(o, ZF[4][:, 128 * t:128 * t + 128], one.broadcast_to([8, nk]), False, False)
                tk = mm(o, one.broadcast_to([8, 128]), ZF[5][:, 0:nk], False, True, inc=(t == 1))
            i, P, pf = pp.take()
            col = 2 * h
            for t in range(2):
                o = P[:, 0:128] if t == 0 else P[:, 128:384]
                s_ = ps[:, 0:128] if t == 0 else ps[:, 128:384]
                m_ = CST[:, 256:384] if t == 0 else CST[:, 128:384]
                a = DV.do(lambda e, o=o, s_=s_, m_=m_, cc=mxx[:, col + t:col + t + 1]: e.tensor_tensor_reduce(
                    o, s_, m_, 1.0, NEG, ALU.add, ALU.max, cc), tk, pf, sm_free[0])
            banks.free(b, a)
            a = ts(nmx[:, col:col + 2], mxx[:, col:col + 2], -1.0, None, ALU.mult, None, a)
            for t in range(2):
                o = P[:, 0:128] if t == 0 else P[:, 128:384]
                a2 = act(o, o, ACT.Exp, a, bias=nmx[:, col + t:col + t + 1], accum_out=sms[:, col + t:col + t + 1])
            r = DV.do(lambda e: e.reciprocal(rcp[:, col:col + 2], sms[:, col:col + 2]), a2)
            for t in range(2):
                o = P[:, 0:128] if t == 0 else P[:, 128:384]
                r2 = ts(o, o, rcp[:, col + t:col + t + 1], None, ALU.mult, None, r)
            sc[h] = (i, P, r2)

        def turned(h):
            i, P, tok = sc[h]
            b, ps, freed = banks.take()
            PE.wait(freed, tok)
            for j in range(3):
                tk = tr(ps[:, 128 * j:128 * j + 128], P[:, 128 * j:128 * j + 128], inc=(j == 2))
            pp.free(i, tk)
            i2, Q, qf = pq.take()
            e = act(Q[:, 0:384], ps[:, 0:384], ACT.Copy, tk, qf)
            banks.free(b, e)
            pt[h] = (i2, Q, e)

        def values(h):
            c, po = h // 2, 64 * (h % 2)
            i, Q, tok = pt[h]
            if h % 2 == 0:
                outs[c] = banks.take()
                PE.wait(outs[c][2])
            ps = outs[c][1]
            PE.wait(tok, t_v)
            mm(ps[po:po + 64, 0:256], V[:, 0, 64 * h:64 * h + 64], Q[:, 0:256], True, False)
            t = mm(ps[po:po + 64, 128:256], V[:, 1, 64 * h:64 * h + 64], Q[:, 256:384], False, True, inc=True)
            pq.free(i, t)
            if h % 2:
                mx = copy(MX[:, 2 + c, :], ps[:, 0:256], t, mx_free[0])
                banks.free(outs[c][0], mx)
                outs["last"] = mx

        for i in range(10):
            if i < 8:
                scores(i)
            if 0 <= i - 1 < 8:
                turned(i - 1)
            if 0 <= i - 2:
                values(i - 2)
        res = []
        for src, dst in ((RQ, QR), (RK, KR)):
            res += turn([src[:, 0, :], src[:, 1, :]], dst, 2, None, None, rot[-1])
        bY, psY, freed = banks.take()
        psY = two(psY)
        PE.wait(freed)
        hold = []

        def ret_s(h):
            c, po = h // 2, 64 * (h % 2)
            b, ps, freed = banks.take()
            PE.wait(freed, res)
            mm(ps[:, 0:256], KR[po:po + 64, c, 0:128], QR[po:po + 64, c, :], True, True)
            t = mm(ps[:, 256:384], KR[po:po + 64, c, 128:256], QR[po:po + 64, c, 128:256], True, True, inc=True)
            i, P, pf = pp.take()
            a = tt(P[:, 0:384], ps[:, 0:384], CST[:, 384 + 384 * h:768 + 384 * h], ALU.mult, t, pf)
            banks.free(b, a)
            hold.append((i, P, a))

        def ret_v(h):
            i, P, a = hold[h]
            v = lambda t: RV[:, t, 64 * h:64 * h + 64]
            PE.wait(a, t_rv)
            mm(psY[:, 0, 64 * h:64 * h + 64], P[:, 0:128], v(0), True, True)
            mm(psY[:, 1, 64 * h:64 * h + 64], P[:, 128:256], v(0), True, False)
            t = mm(psY[:, 1, 64 * h:64 * h + 64], P[:, 256:384], v(1), False, True, inc=True)
            pp.free(i, t)
            return t

        for i in range(5):
            if i < 4:
                ret_s(i)
            if i:
                t_y = ret_v(i - 1)
        y8 = psY.rearrange("p t (h d) -> p (t h) d", h=4)
        s3 = lambda v: flat(v).rearrange("p (g d) -> p g d", g=8)
        a = red(s8[0], y8, ALU.add, t_y)
        a = ts(s8[1], s8[0], 1.0 / 64, None, ALU.mult, None, a)
        a = tt(s3(A3), y8, s8[1].unsqueeze(2).broadcast_to([128, 8, 64]), ALU.subtract, a, d1)
        banks.free(bY, a)
        b = act(flat(A4), flat(A3), ACT.Square, a, d1, t_lru)
        b = red(s8[2], s3(A4), ALU.add, b)
        b = ts(s8[3], s8[2], 1.0 / 64, EPS, ALU.mult, ALU.add, b)
        b = power(s8[4], s8[3], mhalf, 8, b)
        b = tt(s3(A3), s3(A3), s8[4].unsqueeze(2).broadcast_to([128, 8, 64]), ALU.mult, b)
        b = stt(flat(A3), flat(A3), 0.5, flat(RG), ALU.mult, ALU.mult, b, t_rg)
        fin = turn([A3[:, 0, :], A3[:, 1, :]], MX[:, 6:8, :], 2, None, None, b)
        return [t_lru, outs["last"]] + fin

    mx_free = [None]
    sm_free = [None]
    t_bd = [None]

    def cross(l, t_h):
        CQ = view(0, (8, 256))
        for n in range(4):
            b, ps, t = proj_t(D["w_cq"][l], 256 * n, HT, t_h)
            tq = act(CQ[:, 2 * n:2 * n + 2, :], ps, ACT.Copy, t, scale=1.0 / 16)
            banks.free(b, tq)
        sc, pt = {}, {}
        done = []

        def scores(h):
            b, ps, freed = banks.take()
            ps = two(ps)
            PE.wait(freed, tq, kv_tok[l, "k", h])
            for t in range(2):
                for d in range(2):
                    tk = mm(ps[:, t, :], CQ[:, 2 * h + d, 128 * t:128 * t + 128], CK[:, 2 * h + d, :], d == 0, d == 1,
                            inc=(t == 1 and d == 1))
            if h == 3:
                kv_free[0] = tk
            i, P, pf = pp.take()
            col = 2 * h
            a = red(mxx[:, col:col + 2], ps, ALU.max, tk)
            a = ts(nmx[:, col:col + 2], mxx[:, col:col + 2], -1.0, None, ALU.mult, None, a)
            for t in range(2):
                a2 = act(P[:, 256 * t:256 * t + 256], ps[:, t, :], ACT.Exp, a, pf, bias=nmx[:, col + t:col + t + 1],
                         accum_out=sms[:, col + t:col + t + 1])
            banks.free(b, a2)
            r = DV.do(lambda e: e.reciprocal(rcp[:, col:col + 2], sms[:, col:col + 2]), a2)
            for t in range(2):
                o = P[:, 256 * t:256 * t + 256]
                r2 = ts(o, o, rcp[:, col + t:col + t + 1], None, ALU.mult, None, r)
            sc[h] = (i, P, r2)

        def turned(h):
            i, P, tok = sc[h]
            b, ps, freed = banks.take()
            PE.wait(freed, tok)
            for m in range(2):
                for t in range(2):
                    tk = tr(ps[:, 256 * m + 128 * t:256 * m + 128 * t + 128], P[:, 256 * t + 128 * m:256 * t + 128 * m + 128],
                            inc=(m == 1 and t == 1))
            pp.free(i, tk)
            i2, Q, qf = pq.take()
            e = act(Q[:, :], ps, ACT.Copy, tk, qf)
            banks.free(b, e)
            pt[h] = (i2, Q, e)

        def values(h):
            i, Q, tok = pt[h]
            b, ps, freed = banks.take()
            ps = two(ps)
            PE.wait(freed, tok, [kv_tok[l, "v", n] for n in range(4)])
            for d in range(2):
                for m in range(2):
                    t = mm(ps[:, d, :], CV[:, m, 256 * h + 128 * d:256 * h + 128 * d + 128], Q[:, 256 * m:256 * m + 256],
                           m == 0, m == 1, inc=(d == 1 and m == 1))
            pq.free(i, t)
            if h == 3:
                kv_free[1] = t
            mx = copy(MX[:, 2 * h:2 * h + 2, :], ps, t, mx_free[0])
            banks.free(b, mx)
            done.append(mx)

        for i in range(6):
            if i < 4:
                scores(i)
            if 0 <= i - 1 < 4:
                turned(i - 1)
            if 0 <= i - 2:
                values(i - 2)
        return done

    def ffn(l, t_h):
        HID = view(0, (22, 256))
        A = [view(5632 + 512 * i, (2, 256)) for i in range(2)]
        af = [None, None]
        last = None
        for n in range(11):
            b1, g, t1 = proj_t(D["w_gate"][l], 256 * n, HT, t_h)
            b2, u, t2 = proj_t(D["w_up"][l], 256 * n, HT, t_h)
            a = A[n % 2]
            e = act(flat(a), flat(g), ACT.Tanh, t1, af[n % 2], scale=0.5)
            e = stt(flat(a), flat(a), 1.0, flat(g), ALU.add, ALU.mult, e)
            banks.free(b1, e)
            last = stt(flat(HID[:, 2 * n:2 * n + 2, :]), flat(a), 0.5, flat(u), ALU.mult, ALU.mult, e, t2)
            af[n % 2] = last
            banks.free(b2, last)
        return proj_y(D["w_down"][l], 11, HID, last)

    def finish_at(n):
        return stage <= n

    def store(src, *toks):
        for t in range(2):
            o = SP.dma(count, "out", lambda e, t=t: e.dma_start(out[0, 128 * t:128 * t + 128, :], src[:, t, :]), *toks)
        SP.wait(o)

    def run():
        filler.extend([lambda n=n: fill_k(0, n) for n in range(4)] + [lambda n=n: fill_v(0, n) for n in range(4)])
        filler.extend([lambda n=n: fill_ada(n) for n in range(24)])
        t_xx = t_x
        for l in range(2):
            if l == 1:
                filler[0:0] = [lambda n=n: fill_k(1, n) for n in range(4)] + [lambda n=n: fill_v(1, n) for n in range(4)]
            fill(2)
            t_h = pre_norm(par(f"pre_mix{l}", 0, 8), None, t_xx)
            t_m = mixer(l, t_h)
            t_g = load_gain(D["post_mix_g"][l:l + 1, :])
            fill(2)
            y = proj_y(D["w_out"][l], 4, MX, t_m)
            mx_free[0] = y
            t_xx = post_norm(y, GB, t_g)
            gb_free[0] = t_xx
            if finish_at(3 * l + 1):
                return store(X, t_xx)
            fill(4)
            t_h = pre_norm(par(f"pre_cross{l}", 0, 8), None, t_xx)
            t_m = cross(l, t_h)
            t_g = load_gain(D["post_cross_g"][l:l + 1, :])
            y = proj_y(D["w_co"][l], 4, MX, t_m)
            mx_free[0] = y
            t_xx = post_norm(y, GB, t_g)
            gb_free[0] = t_xx
            if finish_at(3 * l + 2):
                return store(X, t_xx)
            fill(4)
            t_h = pre_norm(par(f"pre_ffn{l}", 0, 8), None, t_xx)
            t_g = load_gain(D["post_ffn_g"][l:l + 1, :])
            y = ffn(l, t_h)
            t_xx = post_norm(y, GB, t_g)
            gb_free[0] = t_xx
            if finish_at(3 * l + 3):
                return store(X, t_xx)
        second(t_xx)

    def second(t_xx):
        fill(99)
        t_mod = ada_tok["last"]
        t_g = load_gain(D["norm_post_mix_2"][0:1, :])
        a = tt(gs[:, 0:8], par("npm2", 0, 8), MT[:, 8:16], ALU.mult, t_mod)
        b = tt(gs[:, 8:16], par("npf2", 0, 8), MT[:, 24:32], ALU.mult, t_mod)
        t_h = pre_norm(gs[:, 0:8], MT[:, 0:8], t_xx, a, b)
        ga = tt(GA[:, 0, :], GA[:, 0, :], GB[:, :], ALU.mult, t_g)
        t_g = load("gb", GB[:, :], D["norm_post_ffn_2"][0:1, :].broadcast_to([128, 1024]), ga)
        ga = tt(GA[:, 1, :], GA[:, 1, :], GB[:, :], ALU.mult, t_g, ga)
        w = D["w_in_2"][0]
        QT, K2 = view(0, (4, 256)), view(1024, (2, 256))
        V2 = view(1536, (2, 128))
        VG, UG = view(1792, (2, 512)), view(2816, (2, 512))
        G1, G2 = view(3840, (2, 512)), view(4864, (2, 512))
        WS = view(5888, (8, 128))
        LN = view(6912, (2, 512))
        AT = view(7936, (2, 512))
        GM = view(8960, (2, 512))
        for n in range(2):
            b, ps, t = proj_t(w, 256 * n, HT, t_h)
            t_q = act(QT[:, 2 * n:2 * n + 2, :], ps, ACT.Copy, t, scale=0.125)
            banks.free(b, t_q)
        t_ws = load("ws", WS, D["w_st"], t_h)
        load("ln", LN[:, 0, :], D["sgu_ln_g_2"][0:1, :].broadcast_to([128, 512]), t_h)
        t_ln = load("ln", LN[:, 1, :], D["sgu_ln_b_2"][0:1, :].broadcast_to([128, 512]), t_h)
        i, u, got = cols(w, 512)
        b, ps, freed = banks.take()
        PE.wait(got, freed)
        for k in range(8):
            mm(ps[:, 0:256], u[:, k, 0:128], HT[:, k, :], k == 0, k == 7)
        for t in range(2):
            for k in range(8):
                tk = mm(ps[:, 256 + 128 * t:384 + 128 * t], HT[:, k, 128 * t:128 * t + 128], u[:, k, 128:256], k == 0, k == 7,
                        inc=(t == 1 and k == 7))
        ring.free(i, tk)
        for j in range(2):
            for h in range(2):
                t_k = copy(K2[64 * h:64 * h + 64, j, :], ps[64 * j:64 * j + 64, 0:256], tk)
        t_v = act(V2, two(ps[:, 256:512]), ACT.Copy, tk, t_k)
        banks.free(b, t_k, t_v)
        g_free = None
        for name, dst, base in (("v", VG, 1280), ("u", UG, 768)):
            for n in range(2):
                b, ps, t = proj_r(w, base + 256 * n, HT)
                y = dst[:, :, 256 * n:256 * n + 256]
                e = act(y, ps, ACT.Copy, t)
                banks.free(b, e)
                t1, t2 = G1[:, :, 256 * n:256 * n + 256], G2[:, :, 256 * n:256 * n + 256]
                g = gelu2(y, y, t1, t2, e, g_free)
                if n == 1:
                    g_free = g
                f = ts(y, y, 0.5, None, ALU.mult, None, g)
                if name == "v":
                    t_vg = f
                else:
                    t_ug = f
            if name == "v":
                for t in range(2):
                    a = DV.do(lambda e, t=t: e.bn_stats(st6[:, 6 * t:6 * t + 6], VG[:, t, :]), t_vg)
                    a = DV.do(lambda e, t=t: e.bn_aggr(mv[:, 2 * t:2 * t + 2], st6[:, 6 * t:6 * t + 6]), a)
                a = ts(ms, mv[:, 1:4:2], EPS, None, ALU.add, None, a)
                a = power(rs, ms, mhalf, 2, a)
                for t in range(2):
                    v = VG[:, t, :]
                    c = ts(v, v, mv[:, 2 * t:2 * t + 1], rs[:, t:t + 1], ALU.subtract, ALU.mult, a)
                    c = tt(v, v, LN[:, 0, :], ALU.mult, c, t_ln)
                    t_vn = tt(v, v, LN[:, 1, :], ALU.add, c)
        sc, pt = {}, {}
        done = []

        def scores(h):
            c, po, j = h // 2, 64 * (h % 2), h // 4
            b, ps, freed = banks.take()
            PE.wait(freed, t_q, t_k)
            for t in range(2):
                tk = mm(ps[:, 256 * t:256 * t + 256], QT[po:po + 64, c, 128 * t:128 * t + 128], K2[po:po + 64, j, :], True, True,
                        inc=(t == 1))
            i, P, pf = pp.take()
            col = 2 * h
            a = stt(P[:, :], CST[:, 1920:2432], float(2.0 ** -(h + 1)), ps, ALU.mult, ALU.add, tk, pf)
            banks.free(b, a)
            a = red(mxx[:, col:col + 2], two(P[:, :]), ALU.max, a)
            a = ts(nmx[:, col:col + 2], mxx[:, col:col + 2], snk[:, h:h + 1], -1.0, ALU.max, ALU.mult, a)
            for t in range(2):
                o = P[:, 256 * t:256 * t + 256]
                a2 = act(o, o, ACT.Exp, a, bias=nmx[:, col + t:col + t + 1], accum_out=sms[:, col + t:col + t + 1])
            a3 = act(esk[:, col:col + 2], nmx[:, col:col + 2], ACT.Exp, a, bias=snk[:, h:h + 1])
            r = tt(esk[:, col:col + 2], esk[:, col:col + 2], sms[:, col:col + 2], ALU.add, a3)
            r = DV.do(lambda e: e.reciprocal(rcp[:, col:col + 2], esk[:, col:col + 2]), r)
            sc[h] = (i, P, a2, r)

        def turned(h):
            i, P, tok, r = sc[h]
            b, ps, freed = banks.take()
            PE.wait(freed, tok)
            for m in range(2):
                for t in range(2):
                    tk = tr(ps[:, 256 * m + 128 * t:256 * m + 128 * t + 128], P[:, 256 * t + 128 * m:256 * t + 128 * m + 128],
                            inc=(m == 1 and t == 1))
            pp.free(i, tk)
            i2, Q, qf = pq.take()
            e = act(Q[:, :], ps, ACT.Copy, tk, qf)
            banks.free(b, e)
            pt[h] = (i2, Q, e, r)

        def values(h):
            j = h // 4
            i, Q, tok, r = pt[h]
            b, ps, freed = banks.take()
            PE.wait(freed, tok, t_v)
            for t in range(2):
                for m in range(2):
                    tk = mm(ps[:, 64 * t:64 * t + 64], Q[:, 256 * m + 128 * t:256 * m + 128 * t + 128],
                            V2[:, m, 64 * j:64 * j + 64], m == 0, m == 1, inc=(t == 1 and m == 1))
            pq.free(i, tk)
            for t in range(2):
                a = ts(AT[:, t, 64 * h:64 * h + 64], ps[:, 64 * t:64 * t + 64], rcp[:, 2 * h + t:2 * h + t + 1], None,
                       ALU.mult, None, tk, r)
            banks.free(b, a)
            done.append(a)

        for i in range(10):
            if i < 8:
                scores(i)
            if 0 <= i - 1 < 8:
                turned(i - 1)
            if 0 <= i - 2:
                values(i - 2)
        gm = []
        for t in range(2):
            b, ps, freed = banks.take()
            PE.wait(freed, t_vn, t_ws)
            for g in range(8):
                tk = mm(ps[:, 64 * g:64 * g + 64], WS[:, g, :], VG[:, t, 64 * g:64 * g + 64], True, True, inc=(g == 7))
            o = GM[:, t, :]
            a = tt(o.rearrange("p (g c) -> p g c", g=8), ps.rearrange("p (g c) -> p g c", g=8),
                   par("b_s", 0, 8).unsqueeze(2).broadcast_to([128, 8, 64]), ALU.add, tk)
            banks.free(b, a)
            gm.append(tt(o, o, UG[:, t, :], ALU.mult, a, t_ug))
        r = rstd(rs, [[AT[:, 0, :]], [AT[:, 1, :]]], 512, done, scr=JK)
        for t in range(2):
            a = ts(AT[:, t, :], AT[:, t, :], rs[:, t:t + 1], None, ALU.mult, None, r)
        f1 = turn([AT[:, 0, :], AT[:, 1, :]], MX[:, 0:4, :], 4, par("noa2", 0, 4), None, a)
        r = rstd(rs2, [[GM[:, 0, :]], [GM[:, 1, :]]], 512, gm, scr=JK)
        for t in range(2):
            a = ts(GM[:, t, :], GM[:, t, :], rs2[:, t:t + 1], None, ALU.mult, None, r)
        f2 = turn([GM[:, 0, :], GM[:, 1, :]], MX[:, 4:8, :], 4, par("nog2", 0, 4), None, a)
        y = proj_y(D["w_out_2"][0], 4, MX, f1, f2)
        t_xx = post_norm(y, GA[:, 0, :], ga)
        if finish_at(7):
            return store(X, t_xx)
        experts(t_xx)

    def experts(t_xx):
        old = ring.freed
        big = Slots([W[:, 2816 * i:2816 * (i + 1)] for i in range(6)])
        for i in range(6):
            lo, hi = 2816 * i, 2816 * (i + 1)
            big.free(i, [old[j] for j in range(8) if 2048 * j < hi and 2048 * (j + 1) > lo])
        WR = view(0, (8, 16))
        t_wr = load("wr", WR, D["w_router_2"][0].rearrange("(k p) n -> p k n", p=128), t_xx)
        SEL, SLG = view(128, (2, 512)), view(1152, (2, 512))
        HD = [view(2176 + 704 * i, (1, 704))[:, 0, :] for i in range(2)]
        HH = [view(3584 + 896 * i, (7, 128)) for i in range(2)]
        DN = [view(5376 + 1024 * i, (2, 512)) for i in range(2)]
        SG = [view(7424 + 256 * i, (1, 256))[:, 0, :] for i in range(2)]
        W1 = view(7936, (4, 256))
        R4 = view(8960, (2, 128))
        XS = [HT, MX, CK, CV]
        YA = CV

        t_h = pre_norm(gs[:, 8:16], MT[:, 16:24], t_xx)
        b, ps, freed = banks.take()
        lg = ps[:, 0:32].rearrange("p (t e) -> p t e", t=2)
        PE.wait(freed, t_h, t_wr)
        for t in range(2):
            for k in range(8):
                tk = mm(lg[:, t, :], HT[:, k, 128 * t:128 * t + 128], WR[:, k, :], k == 0, k == 7, inc=(t == 1 and k == 7))
        t_router = tk
        a = red(amx, lg, ALU.max, tk)
        a = ts(amx, amx, -1.0, None, ALU.mult, None, a)
        for t in range(2):
            a2 = act(aff[:, 16 * t:16 * t + 16], lg[:, t, :], ACT.Exp, a, bias=amx[:, t:t + 1], accum_out=asm[:, t:t + 1])
        banks.free(b, a2)
        a = DV.do(lambda e: e.reciprocal(asm, asm), a2)
        for t in range(2):
            a = ts(aff[:, 16 * t:16 * t + 16], aff[:, 16 * t:16 * t + 16], asm[:, t:t + 1], None, ALU.mult, None, a)
        t_aff = a
        b, ps, freed = banks.take()
        PE.wait(freed, t_aff)
        for t in range(2):
            tk = tr(ps[0:16, 128 * t:128 * t + 128], aff[:, 16 * t:16 * t + 16], inc=(t == 1))
        wk = W1[0:16, 0, :]
        a = copy(wk, ps[0:16, 0:256], tk)
        banks.free(b, a)
        m8 = W1[0:16, 1, 0:8]
        for _ in range(4):
            a = DV.do(lambda e: e.max(m8, wk), a)
            a = DV.do(lambda e: e.match_replace(wk, m8, wk, -1.0), a)
        msk, pos = W1[0:16, 2, :], W1[0:16, 3, :]
        a = ts(msk, wk, 0.0, None, ALU.is_lt, None, a)
        a = DV.do(lambda e: e.tensor_tensor_scan(pos, msk, zero[0:16, :].broadcast_to([16, 256]), 0.0, ALU.add, ALU.add), a)
        a = tt(pos, pos, msk, ALU.mult, a)
        b, ps, freed = banks.take()
        PE.wait(freed, a)
        for t in range(2):
            tk = PE.do(lambda e, t=t, ps=ps: e.transpose(ps[:, 16 * t:16 * t + 16], pos[:, 128 * t:128 * t + 128], ID[0:16, 0:16]))
        sel = []
        for t in range(2):
            s3 = SEL[:, t, :].rearrange("p (e c) -> p e c", e=16)
            g3 = SLG[:, t, :].rearrange("p (e c) -> p e c", e=16)
            a = tt(s3, ps[:, 16 * t:16 * t + 16].unsqueeze(2).broadcast_to([128, 16, 32]),
                   CST[:, 2592:2624].unsqueeze(1).broadcast_to([128, 16, 32]), ALU.is_equal, tk)
            sel.append(a)
        banks.free(b, a)
        for t in range(2):
            s3 = SEL[:, t, :].rearrange("p (e c) -> p e c", e=16)
            g3 = SLG[:, t, :].rearrange("p (e c) -> p e c", e=16)
            t_slg = tt(g3, s3, aff[:, 16 * t:16 * t + 16].unsqueeze(2).broadcast_to([128, 16, 32]), ALU.mult, sel[t])

        def xs(k):
            return (HT, MX)[k // 4][:, 2 * (k % 4):2 * (k % 4) + 2, :].rearrange("p a b -> p (a b)")

        xst = []
        for k in range(8):
            b, ps, freed = banks.take()
            PE.wait(freed, sel)
            for t in range(2):
                tk = mm(ps, XN[:, t, 128 * k:128 * k + 128], SEL[:, t, :], t == 0, t == 1, inc=(t == 1))
            g, z = gs[:, 8 + k:9 + k], MT[:, 16 + k:17 + k]
            if k % 2:
                e = ts(xs(k), ps, g, z, ALU.mult, ALU.add, tk, t_router)
            else:
                e = act(xs(k), ps, ACT.Identity, tk, t_router, scale=g, bias=z)
            banks.free(b, e)
            xst.append(e)

        free_y = list(yfree)
        gate_free, down_free = [free_y[0], free_y[1], None, None], [None, None]
        rest = Slots([PS[:, 6, :], PS[:, 7, :]])
        old_free = list(banks.freed)
        rest.free(0, old_free[2])
        rest.free(1, old_free[3])
        dn_free = [old_free[0], old_free[1]]
        gu_free = [list(free_y[0:2]), list(free_y[2:4])]
        hd_free, hh_free, dn2_free, sg_free = [None, None], [None, None], [None, None], [None, None]
        done = None
        ya = [[None, None], [None, None]]
        for ex in range(16):
            e2 = ex % 2
            tok_gu = []
            for m, wname in enumerate(("w_gate_2", "w_up_2")):
                for k in range(8):
                    i, buf, freed = big.take()
                    got = load(f"w{i}", buf, D[wname][0, ex, 128 * k:128 * k + 128, :], freed)
                    PE.wait(got, xst[k])
                    if k == 0:
                        PE.wait(gu_free[m])
                    lhs = xs(k)[:, 32 * ex:32 * ex + 32]
                    for hf in range(2):
                        for q in range(4):
                            c0 = 704 * q + 352 * hf
                            t = mm(PS[32 * q:32 * q + 32, 2 * m + hf, 0:352], lhs, buf[:, c0:c0 + 352], k == 0, k == 7,
                                   inc=(hf == 1 and q == 3))
                    big.free(i, t)
                tok_gu.append(t)
            bi, ps, freed = rest.take()
            for t in range(2):
                src = SLG[:, t, 32 * ex:32 * ex + 32].unsqueeze(1).broadcast_to([128, 4, 32])
                r4 = copy(R4[:, t, :].rearrange("p (q c) -> p q c", q=4), src, t_slg, sg_free[0], q=PO)
            PE.wait(freed, r4)
            for t in range(2):
                tk = tr(ps[:, 128 * t:128 * t + 128], R4[:, t, :], inc=(t == 1))
            sg_free[0] = tk
            sgt = act(SG[e2], ps[:, 0:256], ACT.Copy, tk, dn2_free[e2])
            rest.free(bi, sgt)
            hd = HD[e2]
            for hf in range(2):
                o = hd[:, 352 * hf:352 * hf + 352]
                g, u = PS[:, hf, 0:352], PS[:, 2 + hf, 0:352]
                a = act(o, g, ACT.Tanh, tok_gu[0], hd_free[e2], scale=0.5)
                a = stt(o, o, 1.0, g, ALU.add, ALU.mult, a)
                gu_free[0] = a
                a = stt(o, o, 0.5, u, ALU.mult, ALU.mult, a, tok_gu[1])
                gu_free[1] = a
            hh = HH[e2]
            starts = [0, 128, 256, 384, 512, 640, 576]
            evac = {}
            for grp in ((0, 1, 2, 3), (4, 5, 6)):
                bi, ps, freed = rest.take()
                PE.wait(freed, a)
                for n, j in enumerate(grp):
                    s0 = starts[j]
                    wd = 64 if j == 5 else 128
                    tk = tr(ps[0:wd, 128 * n:128 * n + 128], hd[:, s0:s0 + wd], inc=(j == grp[-1]))
                if grp[0] == 0:
                    ev = act(hh[:, 0:4, :], ps.rearrange("p (a b) -> p a b", a=4), ACT.Copy, tk, hh_free[e2])
                    evac[0] = ev
                    rest.free(bi, ev)
                else:
                    v1 = copy(hh[:, 4, :], ps[:, 0:128], tk, hh_free[e2])
                    v1 = copy(hh[0:64, 5, :], ps[0:64, 128:256], tk, hh_free[e2])
                    v2 = copy(hh[64:128, 5, :], ps[64:128, 256:384], tk, hh_free[e2])
                    evac[1] = v2
                    rest.free(bi, v2)
            hd_free[e2] = tk
            wd_ = D["w_down_2"][0, ex].rearrange("(q j) d -> j q d", q=4)
            for jt in range(6):
                for nh in range(2 if jt < 5 else 1):
                    i, buf, freed = big.take()
                    if jt < 5:
                        v = buf[:, 0:2048].rearrange("p (q d) -> p q d", q=4)
                        got = load(f"w{i}", v, wd_[128 * jt:128 * jt + 128, :, 512 * nh:512 * nh + 512], freed)
                        PE.wait(got, evac[jt // 4])
                        if jt == 0:
                            PE.wait(dn_free[nh])
                        for q in range(4):
                            t = mm(PS[32 * q:32 * q + 32, 4 + nh, :], hh[:, jt, 32 * q:32 * q + 32], v[:, q, :], jt == 0, False,
                                   inc=(q == 3))
                    else:
                        v = buf[:, 0:2048].rearrange("p (q d) -> p q d", q=2)
                        load(f"w{i}", v[0:64], wd_[640:704, 0:2, :], freed)
                        got = load(f"w{i}", v[64:128], wd_[640:704, 2:4, :], freed)
                        PE.wait(got)
                        for hf in range(2):
                            for q in range(4):
                                r0 = 64 * (q // 2)
                                t = mm(PS[32 * q:32 * q + 32, 4 + hf, :], hh[r0:r0 + 64, 5, 32 * q:32 * q + 32],
                                       v[r0:r0 + 64, q % 2, 512 * hf:512 * hf + 512], False, True, inc=(q == 3 and hf == 1))
                    big.free(i, t)
            hh_free[e2] = t
            dn = DN[e2]
            d1 = act(dn[:, 0, :], PS[:, 4, :], ACT.Copy, t, dn2_free[e2])
            d2 = copy(dn[:, 1, :], PS[:, 5, :], t, dn2_free[e2])
            dn_free = [d1, d2]
            for t in range(2):
                for hf in range(2):
                    bi, ps, freed = rest.take()
                    tk = mm(ps, SG[e2][:, 128 * t:128 * t + 128], dn[:, hf, :], True, True, freed, d1, d2, sgt, inc=True)
                    o = YA[:, t, 512 * hf:512 * hf + 512]
                    if ex == 0:
                        a = copy(o, ps, tk)
                    else:
                        a = tt(o, o, ps, ALU.add, tk, ya[t][hf])
                    ya[t][hf] = a
                    rest.free(bi, a)
            dn2_free[e2] = tk
        y = [[YA[:, t, 0:512], YA[:, t, 512:1024]] for t in range(2)]
        t_xx = post_norm([ya[0], ya[1]], GA[:, 1, :], None, src=y)
        store(X, t_xx)

    run()

    block = ctx.enter_context(nc.Block())

    def play(queue, eng):
        for key, v, fn in queue.items:
            if fn is None:
                eng.wait_ge(sems[key], v)
            else:
                ins = fn(eng)
                if key is not None:
                    ins.then_inc(sems[key], v)

    @block.sync
    def _(e):
        play(SP, e)

    @block.tensor
    def _(e):
        play(PE, e)

    @block.scalar
    def _(e):
        play(AC, e)

    @block.vector
    def _(e):
        play(DV, e)

    @block.gpsimd
    def _(e):
        play(PO, e)


_DIRECT = ["x", "mem", "post_mix_g", "w_in", "w_rg", "w_ig", "w_out", "post_cross_g", "w_cq",
           "w_ck", "w_cv", "w_co", "w_gate", "w_up", "w_down", "post_ffn_g", "w_ada_2", "b_ada_2", "norm_post_mix_2",
           "w_in_2", "sink_2", "sgu_ln_g_2", "sgu_ln_b_2", "w_out_2", "norm_post_ffn_2", "w_router_2", "w_gate_2",
           "w_up_2", "w_down_2"]


def layout(inputs):
    g = {k: np.ascontiguousarray(inputs[k]) for k in _DIRECT}

    def rows(a):
        return np.asarray(a).reshape(-1, 128)

    parts = []
    for l in range(2):
        parts += [rows(inputs[n][l]) for n in ("pre_mix_g", "pre_cross_g", "pre_ffn_g", "conv_w", "conv_b", "b_rg", "b_ig",
                                               "lru_lambda")]
    parts += [rows(inputs["mem_norm_g"]), rows(inputs["norm_pre_mix_2"]), rows(inputs["norm_out_attn_2"]),
              rows(inputs["norm_out_gmlp_2"]), rows(inputs["norm_pre_ffn_2"]), rows(inputs["b_ada_2"]),
              rows(inputs["b_s_2"]), rows(inputs["c_2"])]
    g["params"] = np.ascontiguousarray(np.concatenate(parts, 0).T)
    g["w_st"] = np.ascontiguousarray(np.transpose(np.asarray(inputs["w_s_2"])[0], (2, 0, 1)))
    g["positions_t"] = np.ascontiguousarray(np.asarray(inputs["positions"]).reshape(2, 128).T)
    g["fox_b_t"] = np.ascontiguousarray(np.asarray(inputs["fox_b_f"]).T)
    g["consts"] = constants()
    return g


def kernel(**inputs):
    import concourse.bacc as _bacc
    from concourse.bass_utils import run_bass_kernel_spmd as _run

    nc = _bacc.Bacc("TRN2", target_bir_lowering=False, num_devices=1)
    arrays, D = {}, {}
    for name, a in layout(inputs).items():
        arrays[f"in_{name}"] = a
        D[name] = nc.dram_tensor(f"in_{name}", a.shape, mybir.dt.from_np(a.dtype), kind="ExternalInput").ap()
    out = nc.dram_tensor("out_0", (1, 256, 1024), F32, kind="ExternalOutput").ap()
    program(nc, D, out)
    r = _run(nc, [arrays], core_ids=[0])
    return r.results[0]["out_0"]
```

```python
from contextlib import ExitStack

import numpy as np

import concourse.bass as bass
from concourse import mybir

F32 = mybir.dt.float32
I32 = mybir.dt.int32
F32R = mybir.dt.float32r
ALU = mybir.AluOpType
ACT = mybir.ActivationFunctionType
AX = mybir.AxisListType
EPS = 1e-6
NEG = -1e30

PC = {}


def _col(name, n):
    PC[name] = (PC["n"], PC["n"] + n)
    PC["n"] += n


PC["n"] = 0
for _l in range(2):
    for _n, _k in (("pre_mix", 8), ("pre_cross", 8), ("pre_ffn", 8), ("conv_w", 8), ("conv_b", 2),
                   ("b_rg", 2), ("b_ig", 2), ("lam", 2)):
        _col(f"{_n}{_l}", _k)
for _n, _k in (("mem", 8), ("npm2", 8), ("noa2", 4), ("nog2", 4), ("npf2", 8), ("b_ada", 48), ("b_s", 8),
               ("c", 8)):
    _col(_n, _k)

CC = {"ident": (0, 128), "mask": (128, 384), "dec": (384, 1920), "dist": (1920, 2432), "rows": (2432, 2560),
      "freq": (2560, 2592), "iota": (2592, 2624)}
NCONST = 2624


def constants():
    c = np.zeros((128, NCONST), np.float32)
    p = np.arange(128)
    c[:, 0:128] = np.eye(128)
    c[:, 256:384] = np.where(p[None, :] <= p[:, None], 0.0, NEG)
    gamma = np.log1p(-np.exp2(-5.0 - np.arange(4)))
    diff = p[None, :] - p[:, None]
    for h in range(4):
        own = np.where(diff >= 0, np.exp(gamma[h] * np.maximum(diff, 0)), 0.0) / 8
        c[:, 384 + 384 * h:512 + 384 * h] = own
        c[:, 512 + 384 * h:640 + 384 * h] = np.exp(gamma[h] * (diff + 128)) / 8
        c[:, 640 + 384 * h:768 + 384 * h] = own
    for t in range(2):
        d = np.abs(128 * t + p[:, None] - np.arange(256)[None, :])
        c[:, 1920 + 256 * t:2176 + 256 * t] = np.where(d <= 128, -d, -1e33)
    c[:, 2432:2560] = (p % 32 == 0)[:, None]
    c[:, 2560:2592] = (10000.0 ** (-np.arange(32, dtype=np.float32) / np.float32(32))).astype(np.float32)
    c[:, 2592:2624] = 1 + np.arange(32)
    return c


class Queue:

    def __init__(self, key):
        self.key, self.items, self.n, self.seen = key, [], 0, {}

    def wait(self, *toks):
        for t in toks:
            if t is None:
                continue
            if isinstance(t, list):
                self.wait(*t)
            elif self.seen.get(t[0], 0) < t[1]:
                self.seen[t[0]] = t[1]
                self.items.append((t[0], t[1], None))

    def do(self, fn, *toks):
        self.wait(*toks)
        self.n += 1
        self.items.append((self.key, 1, fn))
        return (self.key, self.n)

    def quiet(self, fn, *toks):
        self.wait(*toks)
        self.items.append((None, 0, fn))

    def dma(self, count, key, fn, *toks):
        self.wait(*toks)
        count[key] = count.get(key, 0) + 16
        self.items.append((key, 16, fn))
        return (key, count[key])


class Slots:

    def __init__(self, bufs):
        self.bufs, self.at, self.freed, self.held = bufs, 0, [None] * len(bufs), set()

    def take(self):
        i = self.at % len(self.bufs)
        while i in self.held:
            i = (i + 1) % len(self.bufs)
        self.at = i + 1
        self.held.add(i)
        return i, self.bufs[i], self.freed[i]

    def free(self, i, *toks):
        self.freed[i] = list(toks)
        self.held.discard(i)


KEYS = ["pe", "act", "dve", "pool", "x", "mem", "cst", "par", "sm", "gb", "ga", "ln", "bd", "wf", "ws", "wr", "out"]
KEYS += [f"w{i}" for i in range(8)]
NW = 4
NB = 7


class Memory:
    pass


def memory(nc, ctx):
    M = Memory()

    def sb(name, shape, dt=F32, at=ctx):
        return at.enter_context(nc.sbuf_tensor(name, shape, dt))

    M.PS = ctx.enter_context(nc.psum_tensor("PS", [128, 8, 512], F32))
    M.CST = sb("CST", [128, NCONST])
    M.PT = sb("PT", [128, PC["n"]])
    M.X = sb("X", [128, 2, 1024])
    M.XN = sb("XN", [128, 2, 1024])
    M.GA = sb("GA", [128, 2, 1024])
    M.S = sb("S", [128, 10240])
    M.T = sb("T", [128, 288])
    M.CB = sb("CB", [128, 8, 32])
    M.AD = sb("AD", [128, 256])
    M.CSN = sb("CSN", [128, 4, 32])
    M.BD = sb("BD", [128, 4, 128])
    M.WF = sb("WF", [128, 8, 8])
    M.JK = sb("JK", [128, 1024])
    M.PP = [sb(f"PP{i}", [128, 512]) for i in range(3)]
    M.PQ = [sb(f"PQ{i}", [128, 512]) for i in range(2)]
    with ExitStack() as first:
        M.W = sb("W", [128, 2048 * NW], F32, first)
        M.MEMh = sb("MEMh", [128, 8, 256], F32R, first)
        M.MEMl = sb("MEMl", [128, 8, 256], F32R, first)
        M.WH = [sb(f"WH{i}", [128, 2048], F32R, first) for i in range(2)]
        M.WL = [sb(f"WL{i}", [128, 2048], F32R, first) for i in range(2)]
        M.MXh = sb("MXh", [128, 8, 256], F32R, first)
        M.MXl = sb("MXl", [128, 8, 256], F32R, first)
        M.HTh = sb("HTh", [128, 8, 256], F32R, first)
        M.HTl = sb("HTl", [128, 8, 256], F32R, first)
    M.WB = sb("WB", [128, 2816 * NB])
    M.XS = sb("XS", [128, 8, 512])
    M.HF = sb("HF", [128, 8, 256])
    M.YA = sb("YA", [128, 2, 1024])
    return M


def program(nc, D, out, stage=99):
    with ExitStack() as ctx:
        M = memory(nc, ctx)
        sems = {k: ctx.enter_context(nc.semaphore("s_" + k)) for k in KEYS}
        _, order = emit(M, D, out, None, stage)
        queues, _ = emit(M, D, out, order, stage)
        block = ctx.enter_context(nc.Block())

        def play(queue, eng):
            for key, v, fn in queue.items:
                if fn is None:
                    eng.wait_ge(sems[key], v)
                else:
                    ins = fn(eng)
                    if key is not None:
                        ins.then_inc(sems[key], v)

        @block.sync
        def _(e):
            play(queues[0], e)

        @block.tensor
        def _(e):
            play(queues[1], e)

        @block.scalar
        def _(e):
            play(queues[2], e)

        @block.vector
        def _(e):
            play(queues[3], e)

        @block.gpsimd
        def _(e):
            play(queues[4], e)


def emit(M, D, out, order, stage):
    PE, AC, DV, PO, SP = Queue("pe"), Queue("act"), Queue("dve"), Queue("pool"), Queue("sp")
    count = {}
    CST, PT, X, XN, GA, S, T, PS, JK = M.CST, M.PT, M.X, M.XN, M.GA, M.S, M.T, M.PS, M.JK
    CB, AD, CSN, BD, WF = M.CB, M.AD, M.CSN, M.BD, M.WF
    HT, MX, MEM = (M.HTh, M.HTl), (M.MXh, M.MXl), (M.MEMh, M.MEMl)
    GB = S[:, 9216:10240]

    place = [0]

    def small(n):
        place[0] += n
        assert place[0] <= 288, place
        return T[:, place[0] - n:place[0]]

    ID = CST[:, 0:128]

    def par(name, i=0, n=None):
        a, b = PC[name]
        return PT[:, a + i:a + i + (n or 1)]

    def flat(ap):
        return ap.rearrange("p a b -> p (a b)")

    def mm(o, l, r, start, stop, *toks, inc=False):
        fn = lambda e: e.matmul(o, l, r, start=start, stop=stop, skip_group_check=True)
        return PE.do(fn, *toks) if inc else PE.quiet(fn, *toks)

    def tr(o, i, *toks, inc=False):
        fn = lambda e: e.transpose(o, i, ID)
        return PE.do(fn, *toks) if inc else PE.quiet(fn, *toks)

    def act(o, i, f, *toks, **kw):
        return AC.do(lambda e: e.activation(o, i, f, **kw), *toks)

    def ts(o, i, s1, s2, o1, o2, *toks, q=DV):
        if s2 is None:
            return q.do(lambda e: e.tensor_scalar(o, i, s1, None, o1), *toks)
        return q.do(lambda e: e.tensor_scalar(o, i, s1, s2, o1, o2), *toks)

    def tt(o, a, b, op, *toks, q=DV):
        return q.do(lambda e: e.tensor_tensor(o, a, b, op), *toks)

    def stt(o, a, s, b, o1, o2, *toks):
        return DV.do(lambda e: e.scalar_tensor_tensor(out=o, in0=a, scalar=s, in1=b, op0=o1, op1=o2), *toks)

    def copy(o, i, *toks, q=DV):
        return q.do(lambda e: e.tensor_copy(o, i), *toks)

    def red(o, i, op, *toks, ax=AX.X):
        return DV.do(lambda e: e.tensor_reduce(o, i, ax, op), *toks)

    def load(key, o, i, *toks):
        return SP.dma(count, key, lambda e: e.dma_start(o, i), *toks)

    def load_late(key, o, i, *toks):
        return PO.dma(count, key, lambda e: e.dma_start(o, i), *toks)

    used = []
    wfree, wgot, halves = {}, {}, {}
    hfree = [None, None]
    nsplit = [0]

    def unit_src(u):
        name, l, kind, n, split = u
        w = D[name][l]
        if kind == "cols":
            return w[:, 256 * n[0] + n[1]:256 * n[0] + n[1] + 256].rearrange("(k p) n -> p k n", p=128), 8
        return w[256 * n:256 * n + 256, :].rearrange("(k p) n -> p k n", p=128), 2

    def slot(m):
        return M.W[:, 2048 * (m % NW):2048 * (m % NW) + 2048]

    def load_unit(m, u):
        src, a = unit_src(u)
        wgot[m] = load(f"w{m % NW}", slot(m).rearrange("p (a b) -> p a b", a=a), src, wfree.get(m - NW))

    def split_unit(m):
        i = nsplit[0] % 2
        nsplit[0] += 1
        h, l, w = M.WH[i][:, :], M.WL[i][:, :], slot(m)
        a = act(h, w, ACT.Copy, wgot[m], hfree[i])
        b = tt(l, w, h.bitcast(F32), ALU.subtract, a)
        wfree[m] = b
        halves[m] = (i, b)

    def get_unit(u):
        m = len(used)
        used.append(u)
        todo = [u] if order is None else order[m:m + NW - 1]
        for j, v in enumerate(todo):
            if m + j not in wgot and (m + j < NW or m + j - NW in wfree):
                load_unit(m + j, v)
        ahead = 0
        for j, v in enumerate(todo):
            if v[4] and m + j in wgot and ahead < (2 if u[4] else 1):
                ahead += 1
                if m + j not in halves:
                    split_unit(m + j)
        return m

    def raw_unit(name, l, n):
        u = (name, l, "cols", (n, 0), False)
        m = get_unit(u)
        return m, slot(m).rearrange("p (a b) -> p a b", a=8), wgot[m]

    def split_cols(name, l, n, off=0):
        m = get_unit((name, l, "cols", (n, off), True))
        i, t = halves[m]
        return i, [x[i][:, :].rearrange("p (a b) -> p a b", a=8) for x in (M.WH, M.WL)], t

    def split_rows(name, l, n):
        m = get_unit((name, l, "rows", n, True))
        i, t = halves[m]
        return i, [x[i][:, :].rearrange("p (a b) -> p a b", a=2) for x in (M.WH, M.WL)], t

    banks = Slots([PS[:, i, :] for i in range(4, 8)])

    def two(b):
        return b.rearrange("p (a b) -> p a b", a=2)

    def mm3(o, l, r, start, stop, inc=False):
        mm(o, l[0], r[0], start, False)
        mm(o, l[0], r[1], False, False)
        return mm(o, l[1], r[0], False, stop, inc=inc)

    def part(pair, *ix):
        return [x[ix] for x in pair]

    def proj_t(name, l, n, src, *toks, off=0):
        i, u, got = split_cols(name, l, n, off)
        b, ps, freed = banks.take()
        ps = two(ps)
        PE.wait(got, freed, list(toks))
        for m in range(2):
            for k in range(8):
                t = mm3(ps[:, m, :], part(u, slice(None), k, slice(128 * m, 128 * m + 128)), part(src, slice(None), k),
                        k == 0, k == 7, inc=(m == 1 and k == 7))
        hfree[i] = t
        return b, ps, t

    def proj_r(name, l, n, src, *toks, off=0):
        i, u, got = split_cols(name, l, n, off)
        b, ps, freed = banks.take()
        ps = two(ps)
        PE.wait(got, freed, list(toks))
        for m in range(2):
            for k in range(8):
                t = mm3(ps[:, m, :], part(src, slice(None), k, slice(128 * m, 128 * m + 128)), part(u, slice(None), k),
                        k == 0, k == 7, inc=(m == 1 and k == 7))
        hfree[i] = t
        return b, ps, t

    yfree = [None] * 4

    def y_unit(name, l, n, last, src, *toks):
        i, u, got = split_rows(name, l, n)
        PE.wait(got, list(toks))
        for t in range(2):
            for kk in range(2):
                for h in range(2):
                    if n == 0 and kk == 0:
                        PE.wait(yfree[2 * t + h])
                    tok = mm3(PS[:, 2 * t + h, :], part(src, slice(None), kk, slice(128 * t, 128 * t + 128)),
                              part(u, slice(None), kk, slice(512 * h, 512 * h + 512)), n == 0 and kk == 0, last and kk == 1,
                              inc=(kk == 1 and h == 1))
            if t == 0:
                first = tok
        hfree[i] = tok
        return [first, tok]

    def proj_y(name, l, n_units, src, *toks):
        for n in range(n_units):
            r = y_unit(name, l, n, n == n_units - 1, part(src, slice(None), slice(2 * n, 2 * n + 2)), *toks)
        return r

    def split(dst, src, *toks):
        a = act(dst[0], src, ACT.Copy, *toks)
        return tt(dst[1], src, dst[0].bitcast(F32), ALU.subtract, a)

    half = small(1)
    mhalf = small(1)
    zero = small(1)
    junk_free = [None]
    ss4 = small(4)
    ms = small(2)
    rs = small(2)
    rs2 = small(2)
    spl = small(4)
    sp1, sp2, sp3, sp4, sp5 = small(4), small(4), small(4), small(4), small(4)
    hb = small(8)
    cs = small(8)
    MT = small(32)
    gs = small(16)
    bf = small(2)
    snk = small(8)
    nmx = small(16)
    mxx = small(16)
    sms = small(16)
    rcp = small(16)
    esk = small(16)
    st6 = small(12)
    mv = small(4)
    s8 = [small(8) for _ in range(5)]
    posf = small(2)
    aff = small(32)
    amx = small(2)
    asm = small(2)

    pp, pq = Slots(M.PP), Slots(M.PQ)

    t_x = [load("x", X[:, t, :], D["x"][0, 128 * t:128 * t + 128, :]) for t in range(2)][1]
    t_mem = [load("mem", XN[:, t, :], D["mem"][0, 128 * t:128 * t + 128, :]) for t in range(2)][1]
    t_cst = load("cst", CST[:, :], D["consts"])
    t_par = load("par", PT[:, :], D["params"])
    load("sm", posf[:, :].bitcast(I32), D["positions_t"])
    load("sm", bf[0:8, :], D["fox_b_t"])
    t_sm = load("sm", snk, D["sink_2"].broadcast_to([128, 8]))
    t_ga = [load("ga", GA[:, g, :], D["b_ada_2"][0:1, 2048 + 3072 * g:3072 + 3072 * g].broadcast_to([128, 1024]))
            for g in range(2)][1]
    PO.do(lambda e: e.memset(half, 0.5))
    PO.do(lambda e: e.memset(mhalf, -0.5))
    PO.do(lambda e: e.memset(zero, 0.0))
    t_set = PO.do(lambda e: e.memset(flat(BD[:, :, :]), 0.0))
    DV.wait(t_set)
    AC.wait(t_set)

    def power(o, i, which, n, *toks):
        e = which if n == 1 else which.broadcast_to([128, n])
        return tt(o, i, e, ALU.pow, t_set, *toks, q=PO)

    def rstd(o, tiles, n, *toks, scr=None):
        t = None
        parts = len(tiles[0])
        for a, tile in enumerate(tiles):
            for b, part in enumerate(tile):
                w = part.shape[-1]
                tk = toks[a] if a < len(toks) else None
                t = act(scr[:, 0:w], part, ACT.Square, tk, accum_out=ss4[:, parts * a + b:parts * a + b + 1],
                        *[]) if False else AC.do(
                    lambda e, part=part, w=w, c=parts * a + b: e.activation(scr[:, 0:w], part, ACT.Square,
                                                                          accum_out=ss4[:, c:c + 1]),
                    tk, (AC.key, AC.n) if AC.n else None, ss_free[0])
        if parts == 2:
            t = tt(ms, ss4[:, 0:4:2], ss4[:, 1:4:2], ALU.add, t)
            t = ts(ms, ms, 1.0 / n, EPS, ALU.mult, ALU.add, t)
        else:
            t = ts(ms, ss4[:, 0:2], 1.0 / n, EPS, ALU.mult, ALU.add, t)
        ss_free[0] = t
        return power(o, ms, mhalf, 2, t)

    ss_free = [None]

    temp = Slots([JK[:, 256 * i:256 * i + 256] for i in range(4)])

    def turn(srcs, dst, chunks, gain, bias, *toks, at=0):
        PE.wait(t_cst)
        last = []
        for k0 in range(0, chunks, 2):
            b, ps, freed = banks.take()
            ps = two(ps)
            PE.wait(freed, list(toks))
            for k in (0, 1):
                for t in range(2):
                    tk = tr(ps[:, k, 128 * t:128 * t + 128], srcs[t][:, 128 * (k0 + k):128 * (k0 + k) + 128],
                            inc=(k == 1 and t == 1))
            e = []
            for k in (0, 1):
                i = ps[:, k, :]
                g = gain[:, k0 + k:k0 + k + 1] if gain is not None else 1.0
                z = bias[:, k0 + k:k0 + k + 1] if bias is not None else 0.0
                if not isinstance(dst, tuple):
                    e.append(ts(dst[:, at + k0 + k, :], i, g, z, ALU.mult, ALU.add, tk, t_par))
                elif bias is None:
                    h, l = dst[0][:, at + k0 + k, :], dst[1][:, at + k0 + k, :]
                    a = act(h, i, ACT.Identity, tk, e, t_par, scale=g)
                    e.append(stt(l, i, g, h.bitcast(F32), ALU.mult, ALU.subtract, a))
                else:
                    h, l = dst[0][:, at + k0 + k, :], dst[1][:, at + k0 + k, :]
                    j, v, vf = temp.take()
                    a = ts(v, i, g, z, ALU.mult, ALU.add, tk, t_par, vf)
                    e.append(a)
                    a = split((h, l), v, a)
                    temp.free(j, a)
                    e.append(a)
            banks.free(b, *e)
            last += e
        return last

    def pre_norm(gain, bias, *toks, src=X, dst=None):
        dst = dst or HT
        r = rstd(rs, [[src[:, 0, :]], [src[:, 1, :]]], 1024, list(toks), scr=JK)
        a = [ts(XN[:, t, :], src[:, t, :], rs[:, t:t + 1], None, ALU.mult, None, r, list(toks)) for t in range(2)]
        xn_free[0] = a[1]
        return turn([XN[:, 0, :], XN[:, 1, :]], dst, 8, gain, bias, a[1])

    xn_free = [None]

    def post_norm(toks, gain, g_tok, src=None):
        src = src or [[PS[:, 2 * t + h, :] for h in range(2)] for t in range(2)]
        r = rstd(rs2, src, 1024, *toks, scr=JK)
        done = []
        for t in range(2):
            for h in range(2):
                o = XN[:, t, 512 * h:512 * h + 512]
                a = stt(o, src[t][h], rs2[:, t:t + 1], gain[:, 512 * h:512 * h + 512], ALU.mult, ALU.mult, r, g_tok)
                yfree[2 * t + h] = a
                xs = X[:, t, 512 * h:512 * h + 512]
                done.append(tt(xs, xs, o, ALU.add, a))
        return done[-1]

    gb_free = [None]

    def load_gain(row, *toks):
        return load_late("gb", GB, row.broadcast_to([128, 1024]), gb_free[0], *toks)

    AC.wait(t_par)
    DV.wait(t_par)
    for l in range(2):
        a = ts(sp1[:, 2 * l:2 * l + 2], par(f"lam{l}", 0, 2), -1.0, 0.0, ALU.mult, ALU.max)
        b = act(sp2[:, 2 * l:2 * l + 2], par(f"lam{l}", 0, 2), ACT.Abs)
    b = act(sp2, sp2, ACT.Exp, b, scale=-1.0)
    c = ts(sp3, sp2, 1.0, None, ALU.add, None, b)
    d = act(sp4, sp3, ACT.Ln, c)
    e = ts(sp5, sp3, -1.0, None, ALU.add, None, c)
    e = tt(sp5, sp2, sp5, ALU.subtract, e)
    e = tt(sp4, sp4, sp5, ALU.add, d, e)
    e = tt(sp4, sp4, sp1, ALU.add, e)
    t_spl = ts(spl, sp4, -4.0, None, ALU.mult, None, e)
    for l in range(2):
        ts(hb[:, 4 * l:4 * l + 2], par(f"b_rg{l}", 0, 2), 0.5, None, ALU.mult, None)
        t_hb = ts(hb[:, 4 * l + 2:4 * l + 4], par(f"b_ig{l}", 0, 2), 0.5, None, ALU.mult, None)
    a = act(cs, par("c", 0, 8), ACT.Tanh, scale=0.5)
    a = stt(cs, cs, 1.0, par("c", 0, 8), ALU.add, ALU.mult, a)
    a = ts(cs, cs, 0.5, None, ALU.mult, None, a)
    t_cb = copy(CB[:, :, :], cs.unsqueeze(2).broadcast_to([128, 8, 32]), a)
    ps_ = S[:, 0:64].rearrange("p (t f) -> p t f", t=2)
    n_ = S[:, 64:128].rearrange("p (t f) -> p t f", t=2)
    r_ = S[:, 128:256].rearrange("p (s t f) -> p s t f", s=2, t=2)
    a = copy(amx, posf.bitcast(I32), t_sm)
    DV.wait(t_cst)
    for t in range(2):
        b = ts(ps_[:, t, :], CST[:, 2560:2592], amx[:, t:t + 1], None, ALU.mult, None, a)
    TWO_PI = 2 * np.pi
    C1 = 6.28125
    C2 = float(np.float32(TWO_PI - C1))
    C2 = float(np.frombuffer((np.frombuffer(np.float32(C2).tobytes(), np.uint32) & np.uint32(0xFFFFF000)).tobytes(), np.float32)[0])
    C3 = float(TWO_PI - C1 - C2)
    BIG = 12582912.0
    for s in range(2):
        a = ts(n_, ps_, float(1 / TWO_PI), 0.25 * (1 - s), ALU.mult, ALU.add, b)
        a = ts(n_, n_, BIG, None, ALU.add, None, a)
        a = ts(n_, n_, -BIG, None, ALU.add, None, a)
        r = r_[:, s]
        a = stt(r, n_, -C1, ps_, ALU.mult, ALU.add, a)
        a = stt(r, n_, -C2, r, ALU.mult, ALU.add, a)
        a = stt(r, n_, -C3, r, ALU.mult, ALU.add, a)
        a = ts(r, r, (1 - s) * np.pi / 2, -3.1415925, ALU.add, ALU.max, a)
        b = a = ts(r, r, 3.1415925, None, ALU.min, None, a)
    t_rot = act(CSN[:, :, :].rearrange("p (s t) f -> p s t f", s=2), r_, ACT.Sin, a)

    t_mc = pre_norm(par("mem", 0, 8), None, t_mem, src=XN, dst=MEM)
    CK = S[:, 2048:4096].rearrange("p (a b) -> p a b", a=8)
    CV = S[:, 4096:6144].rearrange("p (a b) -> p a b", a=2)
    kv_last = [None]

    kv_tok = {}

    def fill_k(l, n):
        b, ps, t = proj_t("w_ck", l, n, MEM, t_mc)
        kv_tok[l, "k", n] = e = act(CK[:, 2 * n:2 * n + 2, :], ps, ACT.Copy, t)
        banks.free(b, e)

    def fill_v(l, n):
        b, ps, t = proj_r("w_cv", l, n, MEM, t_mc)
        kv_tok[l, "v", n] = e = act(CV[:, :, 256 * n:256 * n + 256], ps, ACT.Copy, t)
        kv_last[0] = t
        banks.free(b, e)

    ad_free = [None]
    ada_tok = {}

    def fill_ada(n):
        i, u, got = raw_unit("w_ada_2", 0, n)
        b, ps, freed = banks.take()
        PE.wait(got, freed, t_cb)
        for kk in range(2):
            for q in range(4):
                k = 4 * kk + q
                t = mm(ps[32 * q:32 * q + 32, 0:256], CB[:, k, :], u[:, k, :], kk == 0, kk == 1, inc=(k == 7))
        wfree[i] = t
        e = act(AD[:, :], ps[:, 0:256], ACT.Copy, t, ad_free[0])
        sec, j = n // 4, n % 4
        if sec in (2, 5):
            t = mm(ps[:, 256:512], CST[:, 2432:2560], AD[:, :], True, True, e, t_cst, inc=True)
            o = GA[:, sec // 3, 256 * j:256 * j + 256]
            f = tt(o, ps[:, 256:512], o, ALU.add, t, t_ga)
        else:
            for m in range(2):
                t = mm(ps[:, 256 + m:257 + m], AD[:, 128 * m:128 * m + 128], CST[:, 2432:2433], True, True, e, t_cst,
                       inc=(m == 1))
            s = {0: 0, 1: 8, 3: 16, 4: 24}[sec] + 2 * j
            f = tt(MT[:, s:s + 2], ps[:, 256:258], par("b_ada", 8 * sec + 2 * j, 2), ALU.add, t)
            if sec in (1, 4):
                f = ts(MT[:, s:s + 2], MT[:, s:s + 2], 1.0, None, ALU.add, None, f)
        ad_free[0] = t
        ada_tok["last"] = f
        banks.free(b, f)

    filler = []

    def fill(n):
        for _ in range(min(n, len(filler))):
            filler.pop(0)()

    def view(a, shape):
        n = int(np.prod(shape))
        v = S[:, a:a + n]
        if len(shape) == 2:
            v = v.rearrange("p (a b) -> p a b", a=shape[0])
        elif len(shape) == 3:
            v = v.rearrange("p (a b c) -> p a b c", a=shape[0], b=shape[1])
        return v

    def gelu2(o, y, t1, t2, *toks, q=None):
        q = q or DV
        a = tt(t1, y, y, ALU.mult, *toks, q=q)
        a = ts(t1, t1, 0.044715, 1.0, ALU.mult, ALU.add, a, q=q)
        a = tt(t1, t1, y, ALU.mult, a, q=q)
        a = act(t2, t1, ACT.Tanh, a, scale=float(np.sqrt(2 / np.pi)))
        return stt(o, t2, 1.0, y, ALU.add, ALU.mult, a)

    def softmax_turn(src, n_tiles, widths):
        pass

    def mixer(l, t_h):
        w = "w_in"
        QT, KT = view(0, (4, 256)), view(1024, (4, 256))
        V = view(2048, (2, 512))
        XC, LY = view(3072, (2, 256)), view(3584, (2, 256))
        A1, A2, A3, A4 = (view(4096 + 512 * i, (2, 256)) for i in range(4))
        LX = view(5120, (2, 259))
        RQ, RK, RV, RG = (view(6144 + 512 * i, (2, 256)) for i in range(4))
        QR, KR = view(8192, (2, 256)), view(8704, (2, 256))
        S1 = view(9216, (2, 256))
        R1, R2 = (JK[:, 256 * i:256 * i + 256].rearrange("p (t h f) -> p t h f", t=2, h=4) for i in range(2))
        ZF = [JK[0:8, 256 * i:256 * i + 256] for i in range(4)] + [S[0:8, 9728 + 256 * i:9984 + 256 * i] for i in range(2)]
        f_w = load_late("wf", WF[:, :, :], D["w_in"][l][:, 2048:2056].rearrange("(k p) n -> p k n", p=128), t_h)
        b, ps, freed = banks.take()
        PE.wait(f_w, freed, t_h)
        for j in range(2):
            for k in range(8):
                t = mm(ps[0:8, 0:256], WF[:, k, :], HT[j][:, k, :].bitcast(F32), j == k == 0, j == 1 and k == 7,
                       inc=(j == 1 and k == 7))
        z = ts(ZF[0], ps[0:8, 0:256], bf[0:8, l:l + 1], None, ALU.add, None, t, t_sm)
        banks.free(b, z)
        a = act(ZF[1], ZF[0], ACT.Abs, z)
        a = act(ZF[1], ZF[1], ACT.Exp, a, scale=-1.0)
        c = ts(ZF[2], ZF[1], 1.0, None, ALU.add, None, a)
        d = act(ZF[3], ZF[2], ACT.Ln, c)
        e = ts(ZF[2], ZF[2], -1.0, None, ALU.add, None, c, d)
        e = tt(ZF[2], ZF[1], ZF[2], ALU.subtract, e)
        e = tt(ZF[3], ZF[3], ZF[2], ALU.add, e, d)
        e = stt(ZF[2], ZF[0], 0.0, ZF[3], ALU.min, ALU.subtract, e)
        e = DV.do(lambda g: g.tensor_tensor_scan(ZF[4], ZF[2], zero[0:8, :].broadcast_to([8, 256]), 0.0, ALU.add, ALU.add), e)
        t_c = ts(ZF[5], ZF[4], -1.0, None, ALU.mult, None, e)
        for n in range(2):
            b, ps, t = proj_t(w, l, 2 + n, HT)
            t_q = act(QT[:, 2 * n:2 * n + 2, :], ps, ACT.Copy, t, scale=0.125)
            banks.free(b, t_q)
            b, ps, t = proj_t(w, l, 4 + n, HT)
            t_k = act(KT[:, 2 * n:2 * n + 2, :], ps, ACT.Copy, t)
            banks.free(b, t_k)
            b, ps, t = proj_r(w, l, 6 + n, HT)
            t_v = act(V[:, :, 256 * n:256 * n + 256], ps, ACT.Copy, t)
            banks.free(b, t_v)
        b, ps, t = proj_t(w, l, 0, HT)
        DV.do(lambda e: e.memset(LX[:, :, 0:3], 0.0), t)
        e = copy(LX[:, :, 3:259], ps, t)
        banks.free(b, e)
        for c in range(2):
            cw = lambda j: par(f"conv_w{l}", 2 * j + c)
            o = XC[:, c, :]
            a = ts(o, LX[:, c, 3:259], cw(3), par(f"conv_b{l}", c), ALU.mult, ALU.add, e)
            for j in range(3):
                a = stt(o, LX[:, c, j:j + 256], cw(j), o, ALU.mult, ALU.add, a)
        t_xc = a
        b, ps, t = proj_t(w, l, 1, HT)
        e = act(LY, ps, ACT.Copy, t)
        banks.free(b, e)
        t_g = gelu2(flat(LY), flat(LY), flat(A1), flat(A2), e)
        w_bd = []
        for g, wg in enumerate(("w_rg", "w_ig")):
            for c in range(2):
                for h in range(2):
                    w_bd = load_late("bd", BD[64 * h:64 * h + 64, 2 * g + c, 64 * h:64 * h + 64], D[wg][l, 2 * c + h], t_h, t_set)
        gates = []
        for g in range(2):
            b, ps, freed = banks.take()
            ps = two(ps)
            PE.wait(freed, w_bd, t_xc)
            for c in range(2):
                t = mm(ps[:, c, :], BD[:, 2 * g + c, :], XC[:, c, :], True, True, inc=(c == 1))
            for c in range(2):
                o = (A3, A4)[g][:, c, :]
                a = act(o, ps[:, c, :], ACT.Tanh, t, t_hb, scale=0.5, bias=hb[:, 4 * l + 2 * g + c:4 * l + 2 * g + c + 1])
            banks.free(b, a)
            gates.append(a)
        t_bd[0] = t
        for c in range(2):
            a = ts(A3[:, c, :], A3[:, c, :], 1.0, spl[:, 2 * l + c:2 * l + c + 1], ALU.add, ALU.mult, gates[1], t_spl)
        b1 = act(flat(A1), flat(A3), ACT.Exp, a, t_g)
        b2 = act(flat(A2), flat(A3), ACT.Tanh, a, t_g, scale=-1.0)
        c1 = tt(flat(A3), flat(A1), flat(A1), ALU.mult, b1, b2)
        c1 = stt(flat(A3), flat(A3), 1.0, flat(A2), ALU.add, ALU.mult, c1)
        c2 = act(flat(A3), flat(A3), ACT.Sqrt, c1)
        d1 = stt(flat(A4), flat(A4), 1.0, flat(XC), ALU.add, ALU.mult, gates[1])
        d1 = stt(flat(A4), flat(A4), 0.5, flat(A3), ALU.mult, ALU.mult, d1, c2)
        for c in range(2):
            a = DV.do(lambda e, c=c: e.tensor_tensor_scan(A2[:, c, :], A1[:, c, :], A4[:, c, :], 0.0, ALU.mult, ALU.add), d1)
        t_lru = stt(flat(A2), flat(A2), 0.5, flat(LY), ALU.mult, ALU.mult, a, t_g)
        t_lru = split((MX[0][:, 0:2, :], MX[1][:, 0:2, :]), A2, t_lru, mx_free[0])
        rot = []
        for n, (raw, res) in enumerate(((A3, RQ), (A4, RK))):
            b, ps, t = proj_r(w, l, 8 + n, HT, off=8)
            raw = (S1, QR)[n]
            e = act(raw, ps, ACT.Copy, t)
            banks.free(b, e)
            x = raw.rearrange("p t (h s f) -> p t h s f", h=4, s=2)
            o = res.rearrange("p t (h s f) -> p t h s f", h=4, s=2)
            cos = CSN[:, 0:2, :].unsqueeze(2).broadcast_to([128, 2, 4, 32])
            sin = CSN[:, 2:4, :].unsqueeze(2).broadcast_to([128, 2, 4, 32])
            for s, op in ((0, ALU.subtract), (1, ALU.add)):
                c1, c2 = (cos, sin) if s == 0 else (sin, cos)
                a1 = tt(R1, x[:, :, :, 0], c1, ALU.mult, e, t_rot, t_c, rot[-1:], q=PO)
                a2 = tt(R2, x[:, :, :, 1], c2, ALU.mult, e, rot[-1:], q=PO)
                rot.append(tt(o[:, :, :, s], R1, R2, op, a1, a2, q=PO))
        b, ps, t = proj_r(w, l, 10, HT, off=8)
        t_rv = act(RV, ps, ACT.Copy, t)
        banks.free(b, t_rv)
        b, ps, t = proj_r(w, l, 11, HT, off=8)
        t_th = act(S1, ps, ACT.Tanh, t, rot[1], scale=0.5)
        t_rg = stt(flat(RG), flat(S1), 1.0, flat(ps), ALU.add, ALU.mult, t_th)
        banks.free(b, t_rg)
        sc, pt, outs = {}, {}, {}

        def scores(h):
            c, po = h // 2, 64 * (h % 2)
            b, ps, freed = banks.take()
            PE.wait(freed, t_q, t_k, t_c, t_cst)
            one = ID[0:8, h:h + 1]
            for t in range(2):
                o = ps[:, 0:128] if t == 0 else ps[:, 128:384]
                nk = 128 * (t + 1)
                mm(o, QT[po:po + 64, c, 128 * t:128 * t + 128], KT[po:po + 64, c, 0:nk], True, False)
                mm(o, ZF[4][:, 128 * t:128 * t + 128], one.broadcast_to([8, nk]), False, False)
                tk = mm(o, one.broadcast_to([8, 128]), ZF[5][:, 0:nk], False, True, inc=(t == 1))
            i, P, pf = pp.take()
            col = 2 * h
            for t in range(2):
                o = P[:, 0:128] if t == 0 else P[:, 128:384]
                s_ = ps[:, 0:128] if t == 0 else ps[:, 128:384]
                m_ = CST[:, 256:384] if t == 0 else CST[:, 128:384]
                a = DV.do(lambda e, o=o, s_=s_, m_=m_, cc=mxx[:, col + t:col + t + 1]: e.tensor_tensor_reduce(
                    o, s_, m_, 1.0, NEG, ALU.add, ALU.max, cc), tk, pf, sm_free[0])
            banks.free(b, a)
            a = ts(nmx[:, col:col + 2], mxx[:, col:col + 2], -1.0, None, ALU.mult, None, a)
            for t in range(2):
                o = P[:, 0:128] if t == 0 else P[:, 128:384]
                a2 = act(o, o, ACT.Exp, a, bias=nmx[:, col + t:col + t + 1], accum_out=sms[:, col + t:col + t + 1])
            r = DV.do(lambda e: e.reciprocal(rcp[:, col:col + 2], sms[:, col:col + 2]), a2)
            for t in range(2):
                o = P[:, 0:128] if t == 0 else P[:, 128:384]
                r2 = ts(o, o, rcp[:, col + t:col + t + 1], None, ALU.mult, None, r)
            sc[h] = (i, P, r2)

        def turned(h):
            i, P, tok = sc[h]
            b, ps, freed = banks.take()
            PE.wait(freed, tok)
            for j in range(3):
                tk = tr(ps[:, 128 * j:128 * j + 128], P[:, 128 * j:128 * j + 128], inc=(j == 2))
            pp.free(i, tk)
            i2, Q, qf = pq.take()
            e = act(Q[:, 0:384], ps[:, 0:384], ACT.Copy, tk, qf)
            banks.free(b, e)
            pt[h] = (i2, Q, e)

        def values(h):
            c, po = h // 2, 64 * (h % 2)
            i, Q, tok = pt[h]
            if h % 2 == 0:
                outs[c] = banks.take()
                PE.wait(outs[c][2])
            ps = outs[c][1]
            PE.wait(tok, t_v)
            mm(ps[po:po + 64, 0:256], V[:, 0, 64 * h:64 * h + 64], Q[:, 0:256], True, False)
            t = mm(ps[po:po + 64, 128:256], V[:, 1, 64 * h:64 * h + 64], Q[:, 256:384], False, True, inc=True)
            pq.free(i, t)
            if h % 2:
                mx = split((MX[0][:, 2 + c, :], MX[1][:, 2 + c, :]), ps[:, 0:256], t, mx_free[0])
                banks.free(outs[c][0], mx)
                outs["last"] = mx

        for i in range(10):
            if i < 8:
                scores(i)
            if 0 <= i - 1 < 8:
                turned(i - 1)
            if 0 <= i - 2:
                values(i - 2)
        res = []
        for src, dst in ((RQ, QR), (RK, KR)):
            res += turn([src[:, 0, :], src[:, 1, :]], dst, 2, None, None, rot[-1])
        bY, psY, freed = banks.take()
        psY = two(psY)
        PE.wait(freed)
        hold = []

        def ret_s(h):
            c, po = h // 2, 64 * (h % 2)
            b, ps, freed = banks.take()
            PE.wait(freed, res)
            mm(ps[:, 0:256], KR[po:po + 64, c, 0:128], QR[po:po + 64, c, :], True, True)
            t = mm(ps[:, 256:384], KR[po:po + 64, c, 128:256], QR[po:po + 64, c, 128:256], True, True, inc=True)
            i, P, pf = pp.take()
            a = tt(P[:, 0:384], ps[:, 0:384], CST[:, 384 + 384 * h:768 + 384 * h], ALU.mult, t, pf)
            banks.free(b, a)
            hold.append((i, P, a))

        def ret_v(h):
            i, P, a = hold[h]
            v = lambda t: RV[:, t, 64 * h:64 * h + 64]
            PE.wait(a, t_rv)
            mm(psY[:, 0, 64 * h:64 * h + 64], P[:, 0:128], v(0), True, True)
            mm(psY[:, 1, 64 * h:64 * h + 64], P[:, 128:256], v(0), True, False)
            t = mm(psY[:, 1, 64 * h:64 * h + 64], P[:, 256:384], v(1), False, True, inc=True)
            pp.free(i, t)
            return t

        for i in range(5):
            if i < 4:
                ret_s(i)
            if i:
                t_y = ret_v(i - 1)
        y8 = psY.rearrange("p t (h d) -> p (t h) d", h=4)
        s3 = lambda v: flat(v).rearrange("p (g d) -> p g d", g=8)
        a = red(s8[0], y8, ALU.add, t_y)
        a = ts(s8[1], s8[0], 1.0 / 64, None, ALU.mult, None, a)
        a = tt(s3(A3), y8, s8[1].unsqueeze(2).broadcast_to([128, 8, 64]), ALU.subtract, a, d1)
        banks.free(bY, a)
        b = act(flat(A4), flat(A3), ACT.Square, a, d1, t_lru)
        b = red(s8[2], s3(A4), ALU.add, b)
        b = ts(s8[3], s8[2], 1.0 / 64, EPS, ALU.mult, ALU.add, b)
        b = power(s8[4], s8[3], mhalf, 8, b)
        b = tt(s3(A3), s3(A3), s8[4].unsqueeze(2).broadcast_to([128, 8, 64]), ALU.mult, b)
        b = stt(flat(A3), flat(A3), 0.5, flat(RG), ALU.mult, ALU.mult, b, t_rg)
        fin = turn([A3[:, 0, :], A3[:, 1, :]], MX, 2, None, None, b, at=6)
        return [t_lru, outs["last"]] + fin

    mx_free = [None]
    sm_free = [None]
    t_bd = [None]

    def cross(l, t_h):
        CQ = view(0, (8, 256))
        for n in range(4):
            b, ps, t = proj_t("w_cq", l, n, HT, t_h)
            tq = act(CQ[:, 2 * n:2 * n + 2, :], ps, ACT.Copy, t, scale=1.0 / 16)
            banks.free(b, tq)
        sc, pt = {}, {}
        done = []

        def scores(h):
            b, ps, freed = banks.take()
            ps = two(ps)
            PE.wait(freed, tq, kv_tok[l, "k", h])
            for t in range(2):
                for d in range(2):
                    tk = mm(ps[:, t, :], CQ[:, 2 * h + d, 128 * t:128 * t + 128], CK[:, 2 * h + d, :], d == 0, d == 1,
                            inc=(t == 1 and d == 1))
            i, P, pf = pp.take()
            col = 2 * h
            a = red(mxx[:, col:col + 2], ps, ALU.max, tk)
            a = ts(nmx[:, col:col + 2], mxx[:, col:col + 2], -1.0, None, ALU.mult, None, a)
            for t in range(2):
                a2 = act(P[:, 256 * t:256 * t + 256], ps[:, t, :], ACT.Exp, a, pf, bias=nmx[:, col + t:col + t + 1],
                         accum_out=sms[:, col + t:col + t + 1])
            banks.free(b, a2)
            r = DV.do(lambda e: e.reciprocal(rcp[:, col:col + 2], sms[:, col:col + 2]), a2)
            for t in range(2):
                o = P[:, 256 * t:256 * t + 256]
                r2 = ts(o, o, rcp[:, col + t:col + t + 1], None, ALU.mult, None, r)
            sc[h] = (i, P, r2)

        def turned(h):
            i, P, tok = sc[h]
            b, ps, freed = banks.take()
            PE.wait(freed, tok)
            for m in range(2):
                for t in range(2):
                    tk = tr(ps[:, 256 * m + 128 * t:256 * m + 128 * t + 128], P[:, 256 * t + 128 * m:256 * t + 128 * m + 128],
                            inc=(m == 1 and t == 1))
            pp.free(i, tk)
            i2, Q, qf = pq.take()
            e = act(Q[:, :], ps, ACT.Copy, tk, qf)
            banks.free(b, e)
            pt[h] = (i2, Q, e)

        def values(h):
            i, Q, tok = pt[h]
            b, ps, freed = banks.take()
            ps = two(ps)
            PE.wait(freed, tok, [kv_tok[l, "v", n] for n in range(4)])
            for d in range(2):
                for m in range(2):
                    t = mm(ps[:, d, :], CV[:, m, 256 * h + 128 * d:256 * h + 128 * d + 128], Q[:, 256 * m:256 * m + 256],
                           m == 0, m == 1, inc=(d == 1 and m == 1))
            pq.free(i, t)
            mx = split((MX[0][:, 2 * h:2 * h + 2, :], MX[1][:, 2 * h:2 * h + 2, :]), ps, t, mx_free[0])
            banks.free(b, mx)
            done.append(mx)

        for i in range(6):
            if i < 4:
                scores(i)
            if 0 <= i - 1 < 4:
                turned(i - 1)
            if 0 <= i - 2:
                values(i - 2)
        return done

    def ffn(l, t_h):
        A = [view(512 * i, (2, 256)) for i in range(2)]
        hid = Slots([part(MX, slice(None), slice(2 * i, 2 * i + 2)) for i in range(4)])
        for i in range(4):
            hid.free(i, mx_free[0])
        af = [None, None]
        ready = None

        def down(n):
            i, d, tok = ready
            y = y_unit("w_down", l, n, n == 10, d, tok)
            hid.free(i, y)
            return y

        for n in range(11):
            b1, g, t1 = proj_t("w_gate", l, n, HT, t_h)
            b2, u, t2 = proj_t("w_up", l, n, HT, t_h)
            a = A[n % 2]
            e = act(flat(a), flat(g), ACT.Tanh, t1, af[n % 2], scale=0.5)
            e = stt(flat(a), flat(a), 1.0, flat(g), ALU.add, ALU.mult, e)
            banks.free(b1, e)
            if n:
                down(n - 1)
            e = stt(flat(a), flat(a), 0.5, flat(u), ALU.mult, ALU.mult, e, t2)
            banks.free(b2, e)
            i, d, df = hid.take()
            e = split(d, a, e, df)
            af[n % 2] = e
            ready = (i, d, e)
        return down(10)

    def finish_at(n):
        return stage <= n

    def store(src, *toks):
        for t in range(2):
            o = SP.dma(count, "out", lambda e, t=t: e.dma_start(out[0, 128 * t:128 * t + 128, :], src[:, t, :]), *toks)
        SP.wait(o)

    def run():
        filler.extend([lambda n=n: fill_ada(n) for n in range(24)])
        fill(4)
        t_xx = t_x
        for l in range(2):
            if l:
                fill(4)
            t_h = pre_norm(par(f"pre_mix{l}", 0, 8), None, t_xx)
            t_m = mixer(l, t_h)
            t_g = load_gain(D["post_mix_g"][l:l + 1, :], t_m)
            y = proj_y("w_out", l, 4, MX, t_m)
            mx_free[0] = y
            t_xx = post_norm(y, GB, t_g)
            gb_free[0] = t_xx
            if finish_at(3 * l + 1):
                return store(X, t_xx)
            for n in range(4):
                fill_k(l, n)
            for n in range(4):
                fill_v(l, n)
            t_h = pre_norm(par(f"pre_cross{l}", 0, 8), None, t_xx)
            t_m = cross(l, t_h)
            t_g = load_gain(D["post_cross_g"][l:l + 1, :])
            y = proj_y("w_co", l, 4, MX, t_m)
            mx_free[0] = y
            t_xx = post_norm(y, GB, t_g)
            gb_free[0] = t_xx
            if finish_at(3 * l + 2):
                return store(X, t_xx)
            fill(4)
            t_h = pre_norm(par(f"pre_ffn{l}", 0, 8), None, t_xx)
            t_g = load_gain(D["post_ffn_g"][l:l + 1, :])
            y = ffn(l, t_h)
            mx_free[0] = y
            t_xx = post_norm(y, GB, t_g)
            gb_free[0] = t_xx
            if finish_at(3 * l + 3):
                return store(X, t_xx)
        second(t_xx)

    def second(t_xx):
        fill(4)
        t_mod = ada_tok["last"]
        t_g = load_gain(D["norm_post_mix_2"][0:1, :])
        a = tt(gs[:, 0:8], par("npm2", 0, 8), MT[:, 8:16], ALU.mult, t_mod)
        b = tt(gs[:, 8:16], par("npf2", 0, 8), MT[:, 24:32], ALU.mult, t_mod)
        t_h = pre_norm(gs[:, 0:8], MT[:, 0:8], t_xx, a, b)
        gb_free[0] = ga = tt(GA[:, 0, :], GA[:, 0, :], GB, ALU.mult, t_g)
        QT, K2 = view(0, (4, 256)), view(1024, (2, 256))
        V2 = view(1536, (2, 128))
        VG, UG = view(1792, (2, 512)), view(2816, (2, 512))
        G1, G2 = view(3840, (2, 512)), view(4864, (2, 512))
        WS = view(5888, (8, 128))
        LN = view(6912, (2, 512))
        AT = view(7936, (2, 512))
        GM = view(8960, (2, 512))
        for n in range(2):
            b, ps, t = proj_t("w_in_2", 0, n, HT, t_h)
            t_q = act(QT[:, 2 * n:2 * n + 2, :], ps, ACT.Copy, t, scale=0.125)
            banks.free(b, t_q)
        t_ws = load_late("ws", WS, D["w_st"], t_h)
        load_late("ln", LN[:, 0, :], D["sgu_ln_g_2"][0:1, :].broadcast_to([128, 512]), t_h)
        t_ln = load_late("ln", LN[:, 1, :], D["sgu_ln_b_2"][0:1, :].broadcast_to([128, 512]), t_h)
        i, u, got = split_cols("w_in_2", 0, 2)
        b, ps, freed = banks.take()
        PE.wait(got, freed)
        for k in range(8):
            mm3(ps[:, 0:256], part(u, slice(None), k, slice(0, 128)), part(HT, slice(None), k), k == 0, k == 7)
        for t in range(2):
            for k in range(8):
                tk = mm3(ps[:, 256 + 128 * t:384 + 128 * t], part(HT, slice(None), k, slice(128 * t, 128 * t + 128)),
                         part(u, slice(None), k, slice(128, 256)), k == 0, k == 7, inc=(t == 1 and k == 7))
        hfree[i] = tk
        for j in range(2):
            for h in range(2):
                t_k = copy(K2[64 * h:64 * h + 64, j, :], ps[64 * j:64 * j + 64, 0:256], tk)
        t_v = act(V2, two(ps[:, 256:512]), ACT.Copy, tk, t_k)
        banks.free(b, t_k, t_v)
        g_free = None
        for name, dst, base in (("v", VG, 5), ("u", UG, 3)):
            for n in range(2):
                b, ps, t = proj_r("w_in_2", 0, base + n, HT)
                y = dst[:, :, 256 * n:256 * n + 256]
                e = act(y, ps, ACT.Copy, t)
                banks.free(b, e)
                t1, t2 = G1[:, :, 256 * n:256 * n + 256], G2[:, :, 256 * n:256 * n + 256]
                g = gelu2(y, y, t1, t2, e, g_free)
                if n == 1:
                    g_free = g
                f = ts(y, y, 0.5, None, ALU.mult, None, g)
                if name == "v":
                    t_vg = f
                else:
                    t_ug = f
            if name == "v":
                for t in range(2):
                    a = DV.do(lambda e, t=t: e.bn_stats(st6[:, 6 * t:6 * t + 6], VG[:, t, :]), t_vg)
                    a = DV.do(lambda e, t=t: e.bn_aggr(mv[:, 2 * t:2 * t + 2], st6[:, 6 * t:6 * t + 6]), a)
                a = ts(ms, mv[:, 1:4:2], EPS, None, ALU.add, None, a)
                a = power(rs, ms, mhalf, 2, a)
                for t in range(2):
                    v = VG[:, t, :]
                    c = ts(v, v, mv[:, 2 * t:2 * t + 1], rs[:, t:t + 1], ALU.subtract, ALU.mult, a)
                    c = tt(v, v, LN[:, 0, :], ALU.mult, c, t_ln)
                    t_vn = tt(v, v, LN[:, 1, :], ALU.add, c)
        sc, pt = {}, {}
        done = []

        def scores(h):
            c, po, j = h // 2, 64 * (h % 2), h // 4
            b, ps, freed = banks.take()
            PE.wait(freed, t_q, t_k)
            for t in range(2):
                tk = mm(ps[:, 256 * t:256 * t + 256], QT[po:po + 64, c, 128 * t:128 * t + 128], K2[po:po + 64, j, :], True, True,
                        inc=(t == 1))
            i, P, pf = pp.take()
            col = 2 * h
            a = stt(P[:, :], CST[:, 1920:2432], float(2.0 ** -(h + 1)), ps, ALU.mult, ALU.add, tk, pf)
            banks.free(b, a)
            a = red(mxx[:, col:col + 2], two(P[:, :]), ALU.max, a)
            a = ts(nmx[:, col:col + 2], mxx[:, col:col + 2], snk[:, h:h + 1], -1.0, ALU.max, ALU.mult, a)
            for t in range(2):
                o = P[:, 256 * t:256 * t + 256]
                a2 = act(o, o, ACT.Exp, a, bias=nmx[:, col + t:col + t + 1], accum_out=sms[:, col + t:col + t + 1])
            a3 = act(esk[:, col:col + 2], nmx[:, col:col + 2], ACT.Exp, a, bias=snk[:, h:h + 1])
            r = tt(esk[:, col:col + 2], esk[:, col:col + 2], sms[:, col:col + 2], ALU.add, a3)
            r = DV.do(lambda e: e.reciprocal(rcp[:, col:col + 2], esk[:, col:col + 2]), r)
            sc[h] = (i, P, a2, r)

        def turned(h):
            i, P, tok, r = sc[h]
            b, ps, freed = banks.take()
            PE.wait(freed, tok)
            for m in range(2):
                for t in range(2):
                    tk = tr(ps[:, 256 * m + 128 * t:256 * m + 128 * t + 128], P[:, 256 * t + 128 * m:256 * t + 128 * m + 128],
                            inc=(m == 1 and t == 1))
            pp.free(i, tk)
            i2, Q, qf = pq.take()
            e = act(Q[:, :], ps, ACT.Copy, tk, qf)
            banks.free(b, e)
            pt[h] = (i2, Q, e, r)

        def values(h):
            j = h // 4
            i, Q, tok, r = pt[h]
            b, ps, freed = banks.take()
            PE.wait(freed, tok, t_v)
            for t in range(2):
                for m in range(2):
                    tk = mm(ps[:, 64 * t:64 * t + 64], Q[:, 256 * m + 128 * t:256 * m + 128 * t + 128],
                            V2[:, m, 64 * j:64 * j + 64], m == 0, m == 1, inc=(t == 1 and m == 1))
            pq.free(i, tk)
            for t in range(2):
                a = ts(AT[:, t, 64 * h:64 * h + 64], ps[:, 64 * t:64 * t + 64], rcp[:, 2 * h + t:2 * h + t + 1], None,
                       ALU.mult, None, tk, r)
            banks.free(b, a)
            done.append(a)

        for i in range(10):
            if i < 8:
                scores(i)
            if 0 <= i - 1 < 8:
                turned(i - 1)
            if 0 <= i - 2:
                values(i - 2)
        gm = []
        for t in range(2):
            b, ps, freed = banks.take()
            PE.wait(freed, t_vn, t_ws)
            for g in range(8):
                tk = mm(ps[:, 64 * g:64 * g + 64], WS[:, g, :], VG[:, t, 64 * g:64 * g + 64], True, True, inc=(g == 7))
            o = GM[:, t, :]
            a = tt(o.rearrange("p (g c) -> p g c", g=8), ps.rearrange("p (g c) -> p g c", g=8),
                   par("b_s", 0, 8).unsqueeze(2).broadcast_to([128, 8, 64]), ALU.add, tk)
            banks.free(b, a)
            gm.append(tt(o, o, UG[:, t, :], ALU.mult, a, t_ug))
        r = rstd(rs, [[AT[:, 0, :]], [AT[:, 1, :]]], 512, done, scr=JK)
        for t in range(2):
            a = ts(AT[:, t, :], AT[:, t, :], rs[:, t:t + 1], None, ALU.mult, None, r)
        f1 = turn([AT[:, 0, :], AT[:, 1, :]], MX, 4, par("noa2", 0, 4), None, a)
        r = rstd(rs2, [[GM[:, 0, :]], [GM[:, 1, :]]], 512, gm, scr=JK)
        for t in range(2):
            a = ts(GM[:, t, :], GM[:, t, :], rs2[:, t:t + 1], None, ALU.mult, None, r)
        f2 = turn([GM[:, 0, :], GM[:, 1, :]], MX, 4, par("nog2", 0, 4), None, a, at=4)
        y = proj_y("w_out_2", 0, 4, MX, f1, f2)
        mx_free[0] = y
        t_xx = post_norm(y, GA[:, 0, :], ga)
        if finish_at(7):
            return store(X, t_xx)
        experts(t_xx)

    def experts(t_xx):
        fill(4)
        t_g = load_gain(D["norm_post_ffn_2"][0:1, :], mx_free[0])
        tt(GA[:, 1, :], GA[:, 1, :], GB, ALU.mult, t_g, ada_tok["last"])
        n = len(used)
        big = Slots([M.WB[:, 2816 * i:2816 * (i + 1)] for i in range(NB)])
        for i in range(NB):
            lo, hi = 2816 * i, 2816 * (i + 1)
            f = [wfree[m] for m in range(n - NW, n) if 2048 * (m % NW) < hi and 2048 * (m % NW + 1) > lo]
            if hi > 2048 * NW:
                f.append(kv_last[0])
            if hi > 2048 * NW + 4096:
                f.append(mx_free[0])
            big.free(i, f)
        HF, YA = M.HF, M.YA
        WR = view(0, (8, 16))
        t_wr = load_late("wr", WR, D["w_router_2"][0].rearrange("(k p) n -> p k n", p=128), t_xx)
        SEL, SLG = view(128, (2, 512)), view(1152, (2, 512))
        HD = [view(2176 + 704 * i, (1, 704))[:, 0, :] for i in range(2)]
        HH = [view(3584 + 896 * i, (7, 128)) for i in range(2)]
        DN = [view(5376 + 1024 * i, (2, 512)) for i in range(2)]
        SG = [view(7424 + 256 * i, (1, 256))[:, 0, :] for i in range(2)]
        W1 = view(7936, (4, 256))
        R4 = view(8960, (2, 128))

        t_h = pre_norm(gs[:, 8:16], MT[:, 16:24], t_xx, dst=HF)
        b, ps, freed = banks.take()
        lg = ps[:, 0:32].rearrange("p (t e) -> p t e", t=2)
        PE.wait(freed, t_h, t_wr)
        for t in range(2):
            for k in range(8):
                tk = mm(lg[:, t, :], HF[:, k, 128 * t:128 * t + 128], WR[:, k, :], k == 0, k == 7, inc=(t == 1 and k == 7))
        t_router = tk
        a = red(amx, lg, ALU.max, tk)
        a = ts(amx, amx, -1.0, None, ALU.mult, None, a)
        for t in range(2):
            a2 = act(aff[:, 16 * t:16 * t + 16], lg[:, t, :], ACT.Exp, a, bias=amx[:, t:t + 1], accum_out=asm[:, t:t + 1])
        banks.free(b, a2)
        a = DV.do(lambda e: e.reciprocal(asm, asm), a2)
        for t in range(2):
            a = ts(aff[:, 16 * t:16 * t + 16], aff[:, 16 * t:16 * t + 16], asm[:, t:t + 1], None, ALU.mult, None, a)
        t_aff = a
        b, ps, freed = banks.take()
        PE.wait(freed, t_aff)
        for t in range(2):
            tk = tr(ps[0:16, 128 * t:128 * t + 128], aff[:, 16 * t:16 * t + 16], inc=(t == 1))
        wk = W1[0:16, 0, :]
        a = copy(wk, ps[0:16, 0:256], tk)
        banks.free(b, a)
        m8 = W1[0:16, 1, 0:8]
        for _ in range(4):
            a = DV.do(lambda e: e.max(m8, wk), a)
            a = DV.do(lambda e: e.match_replace(wk, m8, wk, -1.0), a)
        msk, pos = W1[0:16, 2, :], W1[0:16, 3, :]
        a = ts(msk, wk, 0.0, None, ALU.is_lt, None, a)
        a = DV.do(lambda e: e.tensor_tensor_scan(pos, msk, zero[0:16, :].broadcast_to([16, 256]), 0.0, ALU.add, ALU.add), a)
        a = tt(pos, pos, msk, ALU.mult, a)
        b, ps, freed = banks.take()
        PE.wait(freed, a)
        for t in range(2):
            tk = PE.do(lambda e, t=t, ps=ps: e.transpose(ps[:, 16 * t:16 * t + 16], pos[:, 128 * t:128 * t + 128], ID[0:16, 0:16]))
        sel = []
        for t in range(2):
            s3 = SEL[:, t, :].rearrange("p (e c) -> p e c", e=16)
            g3 = SLG[:, t, :].rearrange("p (e c) -> p e c", e=16)
            a = tt(s3, ps[:, 16 * t:16 * t + 16].unsqueeze(2).broadcast_to([128, 16, 32]),
                   CST[:, 2592:2624].unsqueeze(1).broadcast_to([128, 16, 32]), ALU.is_equal, tk)
            sel.append(a)
        banks.free(b, a)
        for t in range(2):
            s3 = SEL[:, t, :].rearrange("p (e c) -> p e c", e=16)
            g3 = SLG[:, t, :].rearrange("p (e c) -> p e c", e=16)
            t_slg = tt(g3, s3, aff[:, 16 * t:16 * t + 16].unsqueeze(2).broadcast_to([128, 16, 32]), ALU.mult, sel[t])

        def xs(k):
            return M.XS[:, k, :]

        xst = []
        for k in range(8):
            b, ps, freed = banks.take()
            PE.wait(freed, sel)
            for t in range(2):
                tk = mm(ps, XN[:, t, 128 * k:128 * k + 128], SEL[:, t, :], t == 0, t == 1, inc=(t == 1))
            g, z = gs[:, 8 + k:9 + k], MT[:, 16 + k:17 + k]
            if k % 2:
                e = ts(xs(k), ps, g, z, ALU.mult, ALU.add, tk, t_router)
            else:
                e = act(xs(k), ps, ACT.Identity, tk, t_router, scale=g, bias=z)
            banks.free(b, e)
            xst.append(e)

        free_y = list(yfree)
        gate_free, down_free = [free_y[0], free_y[1], None, None], [None, None]
        rest = Slots([PS[:, 6, :], PS[:, 7, :]])
        old_free = list(banks.freed)
        rest.free(0, old_free[2])
        rest.free(1, old_free[3])
        dn_free = [old_free[0], old_free[1]]
        gu_free = [list(free_y[0:2]), list(free_y[2:4])]
        hd_free, hh_free, dn2_free, sg_free = [None, None], [None, None], [None, None], [None, None]
        done = None
        ya = [[None, None], [None, None]]
        for ex in range(16):
            e2 = ex % 2
            tok_gu = []
            for m, wname in enumerate(("w_gate_2", "w_up_2")):
                for k in range(8):
                    i, buf, freed = big.take()
                    got = load(f"w{i}", buf, D[wname][0, ex, 128 * k:128 * k + 128, :], freed)
                    PE.wait(got, xst[k])
                    if k == 0:
                        PE.wait(gu_free[m])
                    lhs = xs(k)[:, 32 * ex:32 * ex + 32]
                    for hf in range(2):
                        for q in range(4):
                            c0 = 704 * q + 352 * hf
                            t = mm(PS[32 * q:32 * q + 32, 2 * m + hf, 0:352], lhs, buf[:, c0:c0 + 352], k == 0, k == 7,
                                   inc=(hf == 1 and q == 3))
                    big.free(i, t)
                tok_gu.append(t)
            bi, ps, freed = rest.take()
            for t in range(2):
                src = SLG[:, t, 32 * ex:32 * ex + 32].unsqueeze(1).broadcast_to([128, 4, 32])
                r4 = copy(R4[:, t, :].rearrange("p (q c) -> p q c", q=4), src, t_slg, sg_free[0], q=PO)
            PE.wait(freed, r4)
            for t in range(2):
                tk = tr(ps[:, 128 * t:128 * t + 128], R4[:, t, :], inc=(t == 1))
            sg_free[0] = tk
            sgt = act(SG[e2], ps[:, 0:256], ACT.Copy, tk, dn2_free[e2])
            rest.free(bi, sgt)
            hd = HD[e2]
            for hf in range(2):
                o = hd[:, 352 * hf:352 * hf + 352]
                g, u = PS[:, hf, 0:352], PS[:, 2 + hf, 0:352]
                a = act(o, g, ACT.Tanh, tok_gu[0], hd_free[e2], scale=0.5)
                a = stt(o, o, 1.0, g, ALU.add, ALU.mult, a)
                gu_free[0] = a
                a = stt(o, o, 0.5, u, ALU.mult, ALU.mult, a, tok_gu[1])
                gu_free[1] = a
            hh = HH[e2]
            starts = [0, 128, 256, 384, 512, 640, 576]
            evac = {}
            for grp in ((0, 1, 2, 3), (4, 5, 6)):
                bi, ps, freed = rest.take()
                PE.wait(freed, a)
                for n, j in enumerate(grp):
                    s0 = starts[j]
                    wd = 64 if j == 5 else 128
                    tk = tr(ps[0:wd, 128 * n:128 * n + 128], hd[:, s0:s0 + wd], inc=(j == grp[-1]))
                if grp[0] == 0:
                    ev = act(hh[:, 0:4, :], ps.rearrange("p (a b) -> p a b", a=4), ACT.Copy, tk, hh_free[e2])
                    evac[0] = ev
                    rest.free(bi, ev)
                else:
                    v1 = copy(hh[:, 4, :], ps[:, 0:128], tk, hh_free[e2])
                    v1 = copy(hh[0:64, 5, :], ps[0:64, 128:256], tk, hh_free[e2])
                    v2 = copy(hh[64:128, 5, :], ps[64:128, 256:384], tk, hh_free[e2])
                    evac[1] = v2
                    rest.free(bi, v2)
            hd_free[e2] = tk
            wd_ = D["w_down_2"][0, ex].rearrange("(q j) d -> j q d", q=4)
            for jt in range(6):
                for nh in range(2 if jt < 5 else 1):
                    i, buf, freed = big.take()
                    if jt < 5:
                        v = buf[:, 0:2048].rearrange("p (q d) -> p q d", q=4)
                        got = load(f"w{i}", v, wd_[128 * jt:128 * jt + 128, :, 512 * nh:512 * nh + 512], freed)
                        PE.wait(got, evac[jt // 4])
                        if jt == 0:
                            PE.wait(dn_free[nh])
                        for q in range(4):
                            t = mm(PS[32 * q:32 * q + 32, 4 + nh, :], hh[:, jt, 32 * q:32 * q + 32], v[:, q, :], jt == 0, False,
                                   inc=(q == 3))
                    else:
                        v = buf[:, 0:2048].rearrange("p (q d) -> p q d", q=2)
                        load(f"w{i}", v[0:64], wd_[640:704, 0:2, :], freed)
                        got = load(f"w{i}", v[64:128], wd_[640:704, 2:4, :], freed)
                        PE.wait(got)
                        for hf in range(2):
                            for q in range(4):
                                r0 = 64 * (q // 2)
                                t = mm(PS[32 * q:32 * q + 32, 4 + hf, :], hh[r0:r0 + 64, 5, 32 * q:32 * q + 32],
                                       v[r0:r0 + 64, q % 2, 512 * hf:512 * hf + 512], False, True, inc=(q == 3 and hf == 1))
                    big.free(i, t)
            hh_free[e2] = t
            dn = DN[e2]
            d1 = act(dn[:, 0, :], PS[:, 4, :], ACT.Copy, t, dn2_free[e2])
            d2 = copy(dn[:, 1, :], PS[:, 5, :], t, dn2_free[e2])
            dn_free = [d1, d2]
            for t in range(2):
                for hf in range(2):
                    bi, ps, freed = rest.take()
                    tk = mm(ps, SG[e2][:, 128 * t:128 * t + 128], dn[:, hf, :], True, True, freed, d1, d2, sgt, inc=True)
                    o = YA[:, t, 512 * hf:512 * hf + 512]
                    if ex == 0:
                        a = copy(o, ps, tk)
                    else:
                        a = tt(o, o, ps, ALU.add, tk, ya[t][hf])
                    ya[t][hf] = a
                    rest.free(bi, a)
            dn2_free[e2] = tk
        y = [[YA[:, t, 0:512], YA[:, t, 512:1024]] for t in range(2)]
        t_xx = post_norm([ya[0], ya[1]], GA[:, 1, :], None, src=y)
        store(X, t_xx)

    run()
    return (SP, PE, AC, DV, PO), used


_DIRECT = ["x", "mem", "post_mix_g", "w_in", "w_rg", "w_ig", "w_out", "post_cross_g", "w_cq",
           "w_ck", "w_cv", "w_co", "w_gate", "w_up", "w_down", "post_ffn_g", "w_ada_2", "b_ada_2", "norm_post_mix_2",
           "w_in_2", "sink_2", "sgu_ln_g_2", "sgu_ln_b_2", "w_out_2", "norm_post_ffn_2", "w_router_2", "w_gate_2",
           "w_up_2", "w_down_2"]


def layout(inputs):
    g = {k: np.ascontiguousarray(inputs[k]) for k in _DIRECT}

    def rows(a):
        return np.asarray(a).reshape(-1, 128)

    parts = []
    for l in range(2):
        parts += [rows(inputs[n][l]) for n in ("pre_mix_g", "pre_cross_g", "pre_ffn_g", "conv_w", "conv_b", "b_rg", "b_ig",
                                               "lru_lambda")]
    parts += [rows(inputs["mem_norm_g"]), rows(inputs["norm_pre_mix_2"]), rows(inputs["norm_out_attn_2"]),
              rows(inputs["norm_out_gmlp_2"]), rows(inputs["norm_pre_ffn_2"]), rows(inputs["b_ada_2"]),
              rows(inputs["b_s_2"]), rows(inputs["c_2"])]
    g["params"] = np.ascontiguousarray(np.concatenate(parts, 0).T)
    g["w_st"] = np.ascontiguousarray(np.transpose(np.asarray(inputs["w_s_2"])[0], (2, 0, 1)))
    g["positions_t"] = np.ascontiguousarray(np.asarray(inputs["positions"]).reshape(2, 128).T)
    g["fox_b_t"] = np.ascontiguousarray(np.asarray(inputs["fox_b_f"]).T)
    g["consts"] = constants()
    return g


def kernel(**inputs):
    import concourse.bacc as _bacc
    from concourse.bass_utils import run_bass_kernel_spmd as _run

    nc = _bacc.Bacc("TRN2", target_bir_lowering=False, num_devices=1)
    arrays, D = {}, {}
    for name, a in layout(inputs).items():
        arrays[f"in_{name}"] = a
        D[name] = nc.dram_tensor(f"in_{name}", a.shape, mybir.dt.from_np(a.dtype), kind="ExternalInput").ap()
    out = nc.dram_tensor("out_0", (1, 256, 1024), F32, kind="ExternalOutput").ap()
    program(nc, D, out)
    r = _run(nc, [arrays], core_ids=[0])
    return r.results[0]["out_0"]
```

```python
from contextlib import ExitStack

import numpy as np

import concourse.bass as bass
from concourse import mybir

F32 = mybir.dt.float32
I32 = mybir.dt.int32
F32R = mybir.dt.float32r
ALU = mybir.AluOpType
ACT = mybir.ActivationFunctionType
AX = mybir.AxisListType
EPS = 1e-6
NEG = -1e30

PC = {}


def _col(name, n):
    PC[name] = (PC["n"], PC["n"] + n)
    PC["n"] += n


PC["n"] = 0
for _l in range(2):
    for _n, _k in (("pre_mix", 8), ("pre_cross", 8), ("pre_ffn", 8), ("conv_w", 8), ("conv_b", 2),
                   ("b_rg", 2), ("b_ig", 2), ("lam", 2)):
        _col(f"{_n}{_l}", _k)
for _n, _k in (("mem", 8), ("npm2", 8), ("noa2", 4), ("nog2", 4), ("npf2", 8), ("b_ada", 48), ("b_s", 8),
               ("c", 8)):
    _col(_n, _k)

C_ROWS, C_FREQ, C_IOTA, C_MASK, C_DEC, C_DIST = 128, 256, 288, 320, 576, 2112
NCONST = 2624


def constants():
    c = np.zeros((128, NCONST), np.float32)
    p = np.arange(128)
    c[:, 0:128] = np.eye(128)
    c[:, C_MASK + 128:C_MASK + 256] = np.where(p[None, :] <= p[:, None], 0.0, NEG)
    gamma = np.log1p(-np.exp2(-5.0 - np.arange(4)))
    diff = p[None, :] - p[:, None]
    for h in range(4):
        own = np.where(diff >= 0, np.exp(gamma[h] * np.maximum(diff, 0)), 0.0) / 8
        c[:, C_DEC + 384 * h:C_DEC + 128 + 384 * h] = own
        c[:, C_DEC + 128 + 384 * h:C_DEC + 256 + 384 * h] = np.exp(gamma[h] * (diff + 128)) / 8
        c[:, C_DEC + 256 + 384 * h:C_DEC + 384 + 384 * h] = own
    for t in range(2):
        d = np.abs(128 * t + p[:, None] - np.arange(256)[None, :])
        c[:, C_DIST + 256 * t:C_DIST + 256 + 256 * t] = np.where(d <= 128, -d, -1e33)
    c[:, C_ROWS:C_ROWS + 128] = (p % 32 == 0)[:, None]
    c[:, C_FREQ:C_FREQ + 32] = (10000.0 ** (-np.arange(32, dtype=np.float32) / np.float32(32))).astype(np.float32)
    c[:, C_IOTA:C_IOTA + 32] = 1 + np.arange(32)
    return c


class Queue:

    def __init__(self, key):
        self.key, self.items, self.n, self.seen = key, [], 0, {}

    def wait(self, *toks):
        for t in toks:
            if t is None:
                continue
            if isinstance(t, list):
                self.wait(*t)
            elif self.seen.get(t[0], 0) < t[1]:
                self.seen[t[0]] = t[1]
                self.items.append((t[0], t[1], None))

    def do(self, fn, *toks):
        self.wait(*toks)
        self.n += 1
        self.items.append((self.key, 1, fn))
        return (self.key, self.n)

    def quiet(self, fn, *toks):
        self.wait(*toks)
        self.items.append((None, 0, fn))

    def dma(self, count, key, fn, *toks):
        self.wait(*toks)
        count[key] = count.get(key, 0) + 16
        self.items.append((key, 16, fn))
        return (key, count[key])


class Slots:

    def __init__(self, bufs):
        self.bufs, self.at, self.freed, self.held = bufs, 0, [None] * len(bufs), set()

    def take(self):
        i = self.at % len(self.bufs)
        while i in self.held:
            i = (i + 1) % len(self.bufs)
        self.at = i + 1
        self.held.add(i)
        return i, self.bufs[i], self.freed[i]

    def free(self, i, *toks):
        self.freed[i] = list(toks)
        self.held.discard(i)


NW = 4
NB = 7

KEYS = ["id", "pe", "act", "dve", "pool", "x0", "x1", "mem0", "mem1", "cst", "par", "sm", "gb", "ga", "ln", "bd", "wf", "ws", "wr", "out"]
KEYS += [f"w{i}" for i in range(4)] + [f"b{i}" for i in range(NB + 3)]

class Memory:
    pass


def memory(nc, ctx):
    M = Memory()

    def sb(name, shape, dt=F32, at=ctx):
        return at.enter_context(nc.sbuf_tensor(name, shape, dt))

    M.PS = ctx.enter_context(nc.psum_tensor("PS", [128, 8, 512], F32))
    C1, N1, J1 = sb("C1", [128, NCONST + 512]), sb("N1", [128, 4096]), sb("J1", [128, 3584])
    M.CST, M.CB, M.AD = C1[:, 0:NCONST], C1[:, NCONST:NCONST + 256].rearrange("p (a b) -> p a b", a=8), C1[:, NCONST + 256:]
    M.XN, M.GA = (N1[:, 2048 * i:2048 * i + 2048].rearrange("p (a b) -> p a b", a=2) for i in range(2))
    M.JK = J1[:, 0:1024]
    M.PP = [J1[:, 1024 + 512 * i:1536 + 512 * i] for i in range(3)]
    M.PQ = [J1[:, 2560 + 512 * i:3072 + 512 * i] for i in range(2)]
    M.MORE = [J1[:, 768:3584], C1[:, NCONST + 512 - 2816:NCONST + 512], N1[:, 0:2816]]
    M.PT = sb("PT", [128, PC["n"]])
    M.X = sb("X", [128, 2, 1024])
    M.WR = sb("WR", [128, 8, 16])
    M.T = sb("T", [128, 288])
    M.CSN = sb("CSN", [128, 4, 32])
    M.WF = sb("WF", [128, 8, 8])
    M.ONE = sb("ONE", [128, 8], F32R)
    M.FH, M.FL = sb("FH", [128, 64], F32R), sb("FL", [128, 64], F32R)
    with ExitStack() as first:
        M.S = sb("S", [128, 10240], F32, first)
        M.BD = sb("BD", [128, 4, 128], F32, first)
        M.MEMh = sb("MEMh", [128, 8, 256], F32R, first)
        M.MEMl = sb("MEMl", [128, 8, 256], F32R, first)
        M.HTh = sb("HTh", [128, 8, 256], F32R, first)
        M.HTl = sb("HTl", [128, 8, 256], F32R, first)
        M.W = sb("W", [128, 2048 * NW], F32, first)
        M.WH = [sb(f"WH{i}", [128, 2048], F32R, first) for i in range(2)]
        M.WL = [sb(f"WL{i}", [128, 2048], F32R, first) for i in range(2)]
        M.MXh = sb("MXh", [128, 8, 256], F32R, first)
        M.MXl = sb("MXl", [128, 8, 256], F32R, first)
    sb("under0", [128, 128])
    M.SEL = sb("SEL", [128, 2, 512], F32R)
    sb("under1", [128, 3584 - 1152])
    M.XP = [sb(f"XP{i}", [128, 2, 1024], F32R) for i in range(2)]
    sb("under2", [128, 10240 - 3584 - 4096])
    M.WB = sb("WB", [128, 2816 * NB])
    M.XS = sb("XS", [128, 8, 512])
    M.HF = sb("HF", [128, 8, 256])
    M.YA = sb("YA", [128, 2, 1024])
    return M


def program(nc, D, out):
    with ExitStack() as ctx:
        M = memory(nc, ctx)
        sems = {k: ctx.enter_context(nc.semaphore("s_" + k)) for k in KEYS}
        _, order = emit(M, D, out, None)
        queues, _ = emit(M, D, out, order)
        block = ctx.enter_context(nc.Block())

        def play(queue, eng):
            for key, v, fn in queue.items:
                if fn is None:
                    eng.wait_ge(sems[key], v)
                else:
                    ins = fn(eng)
                    if key is not None:
                        ins.then_inc(sems[key], v)

        @block.sync
        def _(e):
            play(queues[0], e)

        @block.tensor
        def _(e):
            play(queues[1], e)

        @block.scalar
        def _(e):
            play(queues[2], e)

        @block.vector
        def _(e):
            play(queues[3], e)

        @block.gpsimd
        def _(e):
            play(queues[4], e)


def emit(M, D, out, order):
    PE, AC, DV, PO, SP = Queue("pe"), Queue("act"), Queue("dve"), Queue("pool"), Queue("sp")
    count = {}
    CST, PT, X, XN, GA, S, T, PS, JK = M.CST, M.PT, M.X, M.XN, M.GA, M.S, M.T, M.PS, M.JK
    CB, AD, CSN, BD, WF = M.CB, M.AD, M.CSN, M.BD, M.WF
    HT, MX, MEM = (M.HTh, M.HTl), (M.MXh, M.MXl), (M.MEMh, M.MEMl)
    GB = S[:, 9216:10240]

    place = [0]

    def small(n):
        place[0] += n
        assert place[0] <= 288, place
        return T[:, place[0] - n:place[0]]

    ID = CST[:, 0:128]

    def par(name, i=0, n=None):
        a, b = PC[name]
        return PT[:, a + i:a + i + (n or 1)]

    def flat(ap):
        return ap.rearrange("p a b -> p (a b)")

    def mm(o, l, r, start, stop, *toks, inc=False):
        fn = lambda e: e.matmul(o, l, r, start=start, stop=stop, skip_group_check=True)
        return PE.do(fn, *toks) if inc else PE.quiet(fn, *toks)

    def tr(o, i, *toks, inc=False):
        fn = lambda e: e.transpose(o, i, ID)
        return PE.do(fn, *toks) if inc else PE.quiet(fn, *toks)

    def act(o, i, f, *toks, **kw):
        return AC.do(lambda e: e.activation(o, i, f, **kw), *toks)

    def ts(o, i, s1, s2, o1, o2, *toks, q=DV):
        if s2 is None:
            return q.do(lambda e: e.tensor_scalar(o, i, s1, None, o1), *toks)
        return q.do(lambda e: e.tensor_scalar(o, i, s1, s2, o1, o2), *toks)

    def tt(o, a, b, op, *toks, q=DV):
        return q.do(lambda e: e.tensor_tensor(o, a, b, op), *toks)

    def stt(o, a, s, b, o1, o2, *toks):
        return DV.do(lambda e: e.scalar_tensor_tensor(out=o, in0=a, scalar=s, in1=b, op0=o1, op1=o2), *toks)

    def copy(o, i, *toks, q=DV):
        return q.do(lambda e: e.tensor_copy(o, i), *toks)

    def red(o, i, op, *toks, ax=AX.X):
        return DV.do(lambda e: e.tensor_reduce(o, i, ax, op), *toks)

    def load(key, o, i, *toks):
        return SP.dma(count, key, lambda e: e.dma_start(o, i), *toks)

    def load_late(key, o, i, *toks):
        return PO.dma(count, key, lambda e: e.dma_start(o, i), *toks)

    used = []
    wfree, wgot, halves = {}, {}, {}
    hfree = [None, None]
    nsplit = [0]

    def unit_src(u):
        name, l, kind, n, split = u
        w = D[name][l]
        if kind == "cols":
            return w[:, 256 * n[0] + n[1]:256 * n[0] + n[1] + 256].rearrange("(k p) n -> p k n", p=128), 8
        return w[256 * n:256 * n + 256, :].rearrange("(k p) n -> p k n", p=128), 2

    def slot(m):
        return M.W[:, 2048 * (m % NW):2048 * (m % NW) + 2048]

    def load_unit(m, u):
        src, a = unit_src(u)
        wgot[m] = load(f"w{m % NW}", slot(m).rearrange("p (a b) -> p a b", a=a), src, wfree.get(m - NW))

    shared = [False]

    def split_unit(m):
        i = nsplit[0] % 2
        nsplit[0] += 1
        h, l, w = M.WH[i][:, :], M.WL[i][:, :], slot(m)
        a = act(h, w, ACT.Copy, wgot[m], hfree[i])
        n = 1536 if shared[0] else 2048
        b = [tt(l[:, 0:n], w[:, 0:n], h[:, 0:n].bitcast(F32), ALU.subtract, a)]
        if shared[0]:
            b.append(tt(l[:, n:], w[:, n:], h[:, n:].bitcast(F32), ALU.subtract, a, q=PO))
        wfree[m] = b
        halves[m] = (i, b)

    early = []

    def early_high():
        m = len(used) + 1
        if m - 1 in halves and m in wgot and m not in halves and order[m][4]:
            i = nsplit[0] % 2
            nsplit[0] += 1
            early.append((m, i, act(M.WH[i][:, :], slot(m), ACT.Copy, wgot[m], hfree[i])))

    def early_low():
        if early:
            m, i, a = early.pop()
            wfree[m] = tt(M.WL[i][:, :], slot(m), M.WH[i][:, :].bitcast(F32), ALU.subtract, a, q=PO)
            halves[m] = (i, wfree[m])

    def get_unit(u):
        m = len(used)
        used.append(u)
        todo = [u] if order is None else order[m:m + NW - 1]
        for j, v in enumerate(todo):
            if m + j not in wgot and (m + j < NW or m + j - NW in wfree):
                load_unit(m + j, v)
        ahead = 0
        for j, v in enumerate(todo):
            if v[4] and m + j in wgot and ahead < (2 if u[4] else 1):
                ahead += 1
                if m + j not in halves:
                    split_unit(m + j)
        return m

    def raw_unit(name, l, n):
        u = (name, l, "cols", (n, 0), False)
        m = get_unit(u)
        return m, slot(m).rearrange("p (a b) -> p a b", a=8), wgot[m]

    def split_cols(name, l, n, off=0):
        m = get_unit((name, l, "cols", (n, off), True))
        i, t = halves[m]
        return i, [x[i][:, :].rearrange("p (a b) -> p a b", a=8) for x in (M.WH, M.WL)], t

    def split_rows(name, l, n):
        m = get_unit((name, l, "rows", n, True))
        i, t = halves[m]
        return i, [x[i][:, :].rearrange("p (a b) -> p a b", a=2) for x in (M.WH, M.WL)], t

    banks = Slots([PS[:, i, :] for i in range(4, 8)])

    def two(b):
        return b.rearrange("p (a b) -> p a b", a=2)

    def mm3(o, l, r, start, stop, inc=False):
        mm(o, l[0], r[0], start, False)
        mm(o, l[0], r[1], False, False)
        return mm(o, l[1], r[0], False, stop, inc=inc)

    def part(pair, *ix):
        return [x[ix] for x in pair]

    beside = []

    def step(n=1):
        for _ in range(n):
            if beside:
                try:
                    next(beside[0])
                except StopIteration:
                    beside.pop(0)

    def finish_gen(g):
        for _ in g:
            pass

    def finish(g):
        while g in beside:
            step()

    norms = {}

    def chunk(src, k):
        return norms[id(src)][k] if id(src) in norms else None

    def proj_t(name, l, n, src, *toks, off=0):
        i, u, got = split_cols(name, l, n, off)
        b, ps, freed = banks.take()
        ps = two(ps)
        PE.wait(got, freed, list(toks))
        for m in range(2):
            for k in range(8):
                PE.wait(chunk(src, k))
                t = mm3(ps[:, m, :], part(u, slice(None), k, slice(128 * m, 128 * m + 128)), part(src, slice(None), k),
                        k == 0, k == 7, inc=(m == 1 and k == 7))
            if m:
                hfree[i] = t
            step()
        return b, ps, t

    def proj_r(name, l, n, src, *toks, off=0):
        i, u, got = split_cols(name, l, n, off)
        b, ps, freed = banks.take()
        ps = two(ps)
        PE.wait(got, freed, list(toks))
        for m in range(2):
            for k in range(8):
                PE.wait(chunk(src, k))
                t = mm3(ps[:, m, :], part(src, slice(None), k, slice(128 * m, 128 * m + 128)), part(u, slice(None), k),
                        k == 0, k == 7, inc=(m == 1 and k == 7))
            if m:
                hfree[i] = t
            step()
        return b, ps, t

    yfree = [None] * 4

    def y_unit(name, l, n, src, *toks, start=False, last=False):
        i, u, got = split_rows(name, l, n)
        both = []
        PE.wait(got, list(toks))
        for t in range(2):
            parts_ = []
            for h in range(2):
                for kk in range(2):
                    if start and kk == 0:
                        PE.wait(yfree[2 * t + h])
                    tok = mm3(PS[:, 2 * t + h, :], part(src, slice(None), kk, slice(128 * t, 128 * t + 128)),
                              part(u, slice(None), kk, slice(512 * h, 512 * h + 512)), start and kk == 0, last and kk == 1,
                              inc=kk == 1)
                parts_.append(tok)
            both.append(parts_)
            if t:
                hfree[i] = tok
            step()
        return both

    def out_unit(name, l, n, *toks, **kw):
        return y_unit(name, l, n, part(MX, slice(None), slice(2 * n, 2 * n + 2)), *toks, **kw)

    def split(dst, src, *toks):
        a = act(dst[0], src, ACT.Copy, *toks)
        return tt(dst[1], src, dst[0].bitcast(F32), ALU.subtract, a)

    mhalf = small(1)
    warm = small(1)
    zero = small(1)
    ss4 = small(4)
    ms = small(2)
    rs = small(2)
    rs2 = small(2)
    spl = small(4)
    sp1, sp2, sp3, sp4, sp5 = small(4), small(4), small(4), small(4), small(4)
    hb = small(8)
    cs = small(8)
    MT = small(32)
    gs = small(16)
    bf = small(2)
    snk = small(8)
    nmx = small(16)
    mxx = small(16)
    sms = small(16)
    rcp = small(16)
    esk = small(16)
    st6 = small(12)
    mv = small(4)
    s8 = [small(8) for _ in range(5)]
    posf = small(2)
    aff = small(32)
    amx = small(2)
    asm = small(2)

    pp, pq = Slots(M.PP), Slots(M.PQ)

    PO.do(lambda e: e.memset(mhalf, -0.5))
    PO.do(lambda e: e.memset(zero, 0.0))
    t_set = PO.do(lambda e: e.memset(flat(BD[:, :, :]), 0.0))
    t_x = [load(f"x{t}", X[:, t, :], D["x"][0, 128 * t:128 * t + 128, :]) for t in range(2)]
    t_x = [[t, t] for t in t_x]
    t_id = load("id", CST[:, 0:128], D["consts"][:, 0:128])
    t_par = load("par", PT[:, :], D["params"])
    if order is not None:
        for m in range(NW - 1):
            load_unit(m, order[m])
    load("sm", posf[:, :].bitcast(I32), D["positions_t"])
    load("sm", bf[0:8, :], D["fox_b_t"])
    t_sm = load("sm", snk, D["sink_2"].broadcast_to([128, 8]))
    t_cst = load("cst", CST[:, 128:NCONST], D["consts"][:, 128:NCONST])
    t_mem = [[load(f"mem{t}", XN[:, t, :], D["mem"][0, 128 * t:128 * t + 128, :])] * 2 for t in range(2)]
    DV.wait(t_set)
    AC.wait(t_set)
    act(warm, zero, ACT.Square)

    def power(o, i, which, n, *toks):
        e = which if n == 1 else which.broadcast_to([128, n])
        return tt(o, i, e, ALU.pow, t_set, *toks, q=PO)

    def rstd(o, a, tile, n, scr, *toks, q=AC):
        parts = len(tile)
        for b, part in enumerate(tile):
            c = ss4[:, 2 * a + b:2 * a + b + 1]
            junk = scr[:, 0:part.shape[-1]]
            wait = [toks[b], (q.key, q.n) if q.n else None, ss_free[a]]
            if q is AC:
                t = q.do(lambda e, part=part, c=c: e.activation(junk, part, ACT.Square, accum_out=c), *wait)
            else:
                t = q.do(lambda e, part=part, c=c: e.tensor_tensor_reduce(
                    junk, part, part, 1.0, 0.0, ALU.mult, ALU.add, c), *wait)
        m = ms[:, a:a + 1]
        if parts == 2:
            t = tt(m, ss4[:, 2 * a:2 * a + 1], ss4[:, 2 * a + 1:2 * a + 2], ALU.add, t)
            t = ts(m, m, 1.0 / n, EPS, ALU.mult, ALU.add, t)
        else:
            t = ts(m, ss4[:, 2 * a:2 * a + 1], 1.0 / n, EPS, ALU.mult, ALU.add, t)
        ss_free[a] = t
        return power(o[:, a:a + 1], m, mhalf, 1, t)

    def diagonal(dst, r, rows, n, scr, *toks):
        rt = [rstd(r, t, rows[t], n, scr[t], *toks[t], q=AC if len(rows[t]) == 2 else (AC, DV)[t]) for t in range(2)]
        for t in range(2):
            a = ts(dst[:, 128 * t:128 * t + 128], ID, r[:, t:t + 1], None, ALU.mult, None, rt[t], t_id)
        return a

    ss_free = [None, None]

    temp = Slots([JK[:, 256 * i:256 * i + 256] for i in range(1, 4)])
    DG = JK[:, 0:256]

    def turning(srcs, dst, chunks, gain, bias, *toks, at=0, by=None, got):
        PE.wait(t_id)
        for k0 in range(0, chunks, 2):
            b, ps, freed = banks.take()
            ps = two(ps)
            PE.wait(freed, list(toks))
            for k in (0, 1):
                for t in range(2):
                    o, i = ps[:, k, 128 * t:128 * t + 128], srcs[t][:, 128 * (k0 + k):128 * (k0 + k) + 128]
                    if by is None:
                        tk = tr(o, i, inc=(k == 1 and t == 1))
                    else:
                        tk = mm(o, i, by[:, 128 * t:128 * t + 128], True, True, inc=(k == 1 and t == 1))
            g = [gain[:, k0 + k:k0 + k + 1] if gain is not None else 1.0 for k in (0, 1)]
            z = [bias[:, k0 + k:k0 + k + 1] if bias is not None else 0.0 for k in (0, 1)]
            if not isinstance(dst, tuple):
                for k in (0, 1):
                    o = dst[:, at + k0 + k, :]
                    if k0 % 4:
                        a = act(o, ps[:, k, :], ACT.Identity, tk, t_par, scale=g[k], bias=z[k])
                    else:
                        a = ts(o, ps[:, k, :], g[k], z[k], ALU.mult, ALU.add, tk, t_par)
                    got.append(a)
                e = [a]
            else:
                hl = [[x[:, at + k0 + k, :] for x in dst] for k in (0, 1)]
                if bias is None:
                    for k in (0, 1):
                        a = act(hl[k][0], ps[:, k, :], ACT.Identity, tk, t_par, scale=g[k])
                    for k in (0, 1):
                        c = stt(hl[k][1], ps[:, k, :], g[k], hl[k][0].bitcast(F32), ALU.mult, ALU.subtract, a)
                        got.append([a, c])
                    e = [c]
                else:
                    v = [temp.take() for k in (0, 1)]
                    c = [ts(v[k][1], ps[:, k, :], g[k], z[k], ALU.mult, ALU.add, tk, t_par, v[k][2]) for k in (0, 1)]
                    h = [act(hl[k][0], v[k][1], ACT.Copy, c[k]) for k in (0, 1)]
                    for k in (0, 1):
                        a = tt(hl[k][1], v[k][1], hl[k][0].bitcast(F32), ALU.subtract, h[k])
                        got.append(a)
                        temp.free(v[k][0], a)
                    e = [c[1]]
            banks.free(b, *e)
            yield

    def turn(*args, **kw):
        got = []
        for _ in turning(*args, got=got, **kw):
            pass
        return got

    NSCR = (S[:, 7168:8192], S[:, 8192:9216])

    def norming(gain, bias, rows, *toks, src=X, dst=None, got, scr=NSCR, dg=DG):
        norms[id(dst or HT)] = got
        a = diagonal(dg, rs, [[src[:, t, 0:512], src[:, t, 512:1024]] for t in range(2)], 1024, scr, *rows)
        early_low()
        yield
        yield from turning([src[:, 0, :], src[:, 1, :]], dst or HT, 8, gain, bias, a, list(toks), by=dg, got=got)

    def pre_norm(*args, **kw):
        got = []
        for _ in norming(*args, got=got, **kw):
            pass
        return got

    def post_norm(toks, gain, g_tok, src=None, ahead=True, tmp=XN):
        src = src or [[PS[:, 2 * t + h, :] for h in range(2)] for t in range(2)]
        done = []
        for t in range(2):
            n0 = AC.n
            r = rstd(rs2, t, src[t], 1024, PSCR[0], *toks[t])
            both = []
            for h in range(2):
                o = tmp[:, t, 512 * h:512 * h + 512]
                yfree[2 * t + h] = tt(o, src[t][h], gain[:, 512 * h:512 * h + 512], ALU.mult, (AC.key, n0 + h + 1), g_tok)
            for h in range(2):
                o, xs = tmp[:, t, 512 * h:512 * h + 512], X[:, t, 512 * h:512 * h + 512]
                both.append(stt(xs, o, rs2[:, t:t + 1], xs, ALU.mult, ALU.add, yfree[2 * t + h], r))
            done.append(both)
        if ahead:
            early_high()
        return done

    PSCR = (JK[:, 0:512], JK[:, 512:1024])

    gb_free = [None]

    def load_gain(row, *toks):
        return load_late("gb", GB, row.broadcast_to([128, 1024]), gb_free[0], *toks)

    AC.wait(t_par)
    DV.wait(t_par)
    tok = {}

    def parameters():
        for l in range(2):
            a = ts(sp1[:, 2 * l:2 * l + 2], par(f"lam{l}", 0, 2), -1.0, 0.0, ALU.mult, ALU.max)
            b = act(sp2[:, 2 * l:2 * l + 2], par(f"lam{l}", 0, 2), ACT.Abs)
        b = act(sp2, sp2, ACT.Exp, b, scale=-1.0)
        c = ts(sp3, sp2, 1.0, None, ALU.add, None, b)
        d = act(sp4, sp3, ACT.Ln, c)
        e = ts(sp5, sp3, -1.0, None, ALU.add, None, c)
        yield
        e = tt(sp5, sp2, sp5, ALU.subtract, e)
        e = tt(sp4, sp4, sp5, ALU.add, d, e)
        e = tt(sp4, sp4, sp1, ALU.add, e)
        t_spl = ts(spl, sp4, -4.0, None, ALU.mult, None, e)
        yield
        for l in range(2):
            ts(hb[:, 4 * l:4 * l + 2], par(f"b_rg{l}", 0, 2), 0.5, None, ALU.mult, None)
            t_hb = ts(hb[:, 4 * l + 2:4 * l + 4], par(f"b_ig{l}", 0, 2), 0.5, None, ALU.mult, None)
        yield
        a = act(cs, par("c", 0, 8), ACT.Tanh, scale=0.5)
        a = stt(cs, cs, 1.0, par("c", 0, 8), ALU.add, ALU.mult, a)
        a = ts(cs, cs, 0.5, None, ALU.mult, None, a)
        t_cb = copy(CB[:, :, :], cs.unsqueeze(2).broadcast_to([128, 8, 32]), a)
        yield
        ps_ = S[:, 9216:9280].rearrange("p (t f) -> p t f", t=2)
        n_ = S[:, 9280:9344].rearrange("p (t f) -> p t f", t=2)
        r_ = S[:, 9344:9472].rearrange("p (s t f) -> p s t f", s=2, t=2)
        a = copy(amx, posf.bitcast(I32), t_sm)
        DV.wait(t_cst)
        yield
        for t in range(2):
            b = ts(ps_[:, t, :], CST[:, C_FREQ:C_FREQ + 32], amx[:, t:t + 1], None, ALU.mult, None, a)
        TWO_PI = 2 * np.pi
        C1 = 6.28125
        C2 = float(np.float32(TWO_PI - C1))
        C2 = float(np.frombuffer((np.frombuffer(np.float32(C2).tobytes(), np.uint32) & np.uint32(0xFFFFF000)).tobytes(), np.float32)[0])
        C3 = float(TWO_PI - C1 - C2)
        BIG = 12582912.0
        for s in range(2):
            a = ts(n_, ps_, float(1 / TWO_PI), 0.25 * (1 - s), ALU.mult, ALU.add, b)
            a = ts(n_, n_, BIG, None, ALU.add, None, a)
            a = ts(n_, n_, -BIG, None, ALU.add, None, a)
            r = r_[:, s]
            yield
            a = stt(r, n_, -C1, ps_, ALU.mult, ALU.add, a)
            a = stt(r, n_, -C2, r, ALU.mult, ALU.add, a)
            a = stt(r, n_, -C3, r, ALU.mult, ALU.add, a)
            a = ts(r, r, (1 - s) * np.pi / 2, -3.1415925, ALU.add, ALU.max, a)
            b = a = ts(r, r, 3.1415925, None, ALU.min, None, a)
        t_rot = act(CSN[:, :, :].rearrange("p (s t) f -> p s t f", s=2), r_, ACT.Sin, a)
        yield
        tok.update(spl=t_spl, hb=t_hb, cb=t_cb, rot=t_rot)

    CK = S[:, 2048:4096].rearrange("p (a b) -> p a b", a=8)
    CV = S[:, 4096:6144].rearrange("p (a b) -> p a b", a=2)
    kv_last = [None]
    ht_last = [None]

    kv_tok = {}

    def fill_k(l, n):
        b, ps, t = proj_t("w_ck", l, n, MEM)
        yield
        kv_tok[l, "k", n] = e = act(CK[:, 2 * n:2 * n + 2, :], ps, ACT.Copy, t)
        banks.free(b, e)

    def fill_v(l, n):
        b, ps, t = proj_r("w_cv", l, n, MEM)
        kv_last[0] = t
        yield
        kv_tok[l, "v", n] = e = act(CV[:, :, 256 * n:256 * n + 256], ps, ACT.Copy, t)
        banks.free(b, e)

    ad_free = [None]
    ada_tok = {}

    def fill_ada(n):
        i, u, got = raw_unit("w_ada_2", 0, n)
        b, ps, freed = banks.take()
        PE.wait(got, freed, tok["cb"])
        for kk in range(2):
            for q in range(4):
                k = 4 * kk + q
                t = mm(ps[32 * q:32 * q + 32, 0:256], CB[:, k, :], u[:, k, :], kk == 0, kk == 1, inc=(k == 7))
        wfree[i] = t
        e = act(AD[:, :], ps[:, 0:256], ACT.Copy, t, ad_free[0])
        sec, j = n // 4, n % 4
        if sec in (2, 5):
            t = mm(ps[:, 256:512], CST[:, C_ROWS:C_ROWS + 128], AD[:, :], True, True, e, t_cst, inc=True)
            o = GA[:, sec // 3, 256 * j:256 * j + 256]
            f = tt(o, ps[:, 256:512], o, ALU.add, t, tok["ga"])
        else:
            for m in range(2):
                t = mm(ps[:, 256 + m:257 + m], AD[:, 128 * m:128 * m + 128], CST[:, C_ROWS:C_ROWS + 1], True, True, e, t_cst,
                       inc=(m == 1))
            s = {0: 0, 1: 8, 3: 16, 4: 24}[sec] + 2 * j
            f = tt(MT[:, s:s + 2], ps[:, 256:258], par("b_ada", 8 * sec + 2 * j, 2), ALU.add, t)
            if sec in (1, 4):
                f = ts(MT[:, s:s + 2], MT[:, s:s + 2], 1.0, None, ALU.add, None, f)
        ad_free[0] = t
        ada_tok["last"] = f
        banks.free(b, f)

    filler = []

    def fill(n):
        for _ in range(min(n, len(filler))):
            filler.pop(0)()

    def view(a, shape):
        n = int(np.prod(shape))
        v = S[:, a:a + n]
        if len(shape) == 2:
            v = v.rearrange("p (a b) -> p a b", a=shape[0])
        elif len(shape) == 3:
            v = v.rearrange("p (a b c) -> p a b c", a=shape[0], b=shape[1])
        return v

    def gelu2(o, y, t1, t2, *toks):
        a = act(t1, y, ACT.Square, *toks)
        a = ts(t1, t1, 0.044715, 1.0, ALU.mult, ALU.add, a)
        a = tt(t1, t1, y, ALU.mult, a)
        a = act(t2, t1, ACT.Tanh, a, scale=float(np.sqrt(2 / np.pi)))
        return stt(o, t2, 1.0, y, ALU.add, ALU.mult, a)

    def mixer(l, t_h):
        w = "w_in"
        QT, KT = view(0, (4, 256)), view(1024, (4, 256))
        V = view(2048, (2, 512))
        XC, LY = view(3072, (2, 256)), view(3584, (2, 256))
        A1, A2, A3, A4 = (view(4096 + 512 * i, (2, 256)) for i in range(4))
        LX = view(5120, (2, 259))
        RQ, RK, RV, RG = (view(6144 + 512 * i, (2, 256)) for i in range(4))
        QR, KR = view(8192, (2, 256)), view(8704, (2, 256))
        S1 = view(9216, (2, 256))
        R1, R2 = (JK[:, 256 * i:256 * i + 256].rearrange("p (t h f) -> p t h f", t=2, h=4) for i in range(2))
        ZF = [JK[0:8, 256 * i:256 * i + 256] for i in range(4)]
        CQ, CN = [MX[0][0:8, 6 + i, :] for i in range(2)], [MX[1][0:8, 6 + i, :] for i in range(2)]
        f_w = load_late("wf", WF[:, :, :], D["w_in"][l][:, 2048:2056].rearrange("(k p) n -> p k n", p=128), t_h)
        for g, wg in enumerate(("w_rg", "w_ig")):
            for c in range(2):
                for h in range(2):
                    w_bd = load_late("bd", BD[64 * h:64 * h + 64, 2 * g + c, 64 * h:64 * h + 64], D[wg][l, 2 * c + h], t_h, t_set)
        if l == 0:
            tok["wr"] = load_late("wr", M.WR[:, :, :], D["w_router_2"][0].rearrange("(k p) n -> p k n", p=128))
            tok["ga"] = [load_late("ga", GA[:, g, :], D["b_ada_2"][0:1, 2048 + 3072 * g:3072 + 3072 * g].broadcast_to([128, 1024]))
                         for g in range(2)][1]
        did = {}

        def forget():
            FH, FL = (v[:, 0:64].rearrange("p (a b) -> p a b", a=8) for v in (M.FH, M.FL))
            a = split((FH, FL), WF[:, :, :], f_w)
            yield
            b, ps, freed = banks.take()
            PE.wait(freed, a)
            for k in range(8):
                t = mm3(ps[0:8, 0:256], (FH[:, k, :], FL[:, k, :]), part(HT, slice(None), k), k == 0, k == 7, inc=k == 7)
            z = ts(ZF[0], ps[0:8, 0:256], bf[0:8, l:l + 1], None, ALU.add, None, t, t_sm)
            banks.free(b, z)
            a = act(ZF[1], ZF[0], ACT.Abs, z)
            a = act(ZF[1], ZF[1], ACT.Exp, a, scale=-1.0)
            yield
            c = ts(ZF[2], ZF[1], 1.0, None, ALU.add, None, a)
            d = act(ZF[3], ZF[2], ACT.Ln, c)
            yield
            e = ts(ZF[2], ZF[2], -1.0, None, ALU.add, None, c, d)
            e = tt(ZF[2], ZF[1], ZF[2], ALU.subtract, e)
            e = tt(ZF[3], ZF[3], ZF[2], ALU.add, e, d)
            e = stt(ZF[2], ZF[0], 0.0, ZF[3], ALU.min, ALU.subtract, e)
            yield
            e = DV.do(lambda g: g.tensor_tensor_scan(ZF[0], ZF[2], zero[0:8, :].broadcast_to([8, 256]), 0.0, ALU.add, ALU.add), e)
            e = split((CQ[0], CQ[1]), ZF[0], e, mx_free[0])
            yield
            for i in range(2):
                e = ts(CN[i], CQ[i].bitcast(F32), -1.0, None, ALU.mult, None, e)
            did["c"] = copy(M.ONE[0:8, :], ID[0:8, 0:8], e)

        def recurrence(t_lx, t_ly):
            e = t_lx
            for c in range(2):
                cw = lambda j: par(f"conv_w{l}", 2 * j + c)
                o = XC[:, c, :]
                a = ts(o, LX[:, c, 3:259], cw(3), par(f"conv_b{l}", c), ALU.mult, ALU.add, e)
                for j in range(3):
                    a = stt(o, LX[:, c, j:j + 256], cw(j), o, ALU.mult, ALU.add, a)
                yield
            t_xc = a
            y, t1, t2 = flat(LY), flat(A1), flat(A2)
            a = act(t1, y, ACT.Square, t_ly)
            a = ts(t1, t1, 0.044715, 1.0, ALU.mult, ALU.add, a)
            yield
            a = tt(t1, t1, y, ALU.mult, a)
            a = act(t2, t1, ACT.Tanh, a, scale=float(np.sqrt(2 / np.pi)))
            yield
            t_g = stt(y, t2, 1.0, y, ALU.add, ALU.mult, a)
            gates = []
            for g in range(2):
                b, ps, freed = banks.take()
                ps = two(ps)
                PE.wait(freed, w_bd, t_xc)
                for c in range(2):
                    t = mm(ps[:, c, :], BD[:, 2 * g + c, :], XC[:, c, :], True, True, inc=(c == 1))
                for c in range(2):
                    o = (A3, A4)[g][:, c, :]
                    a = act(o, ps[:, c, :], ACT.Tanh, t, tok["hb"], scale=0.5, bias=hb[:, 4 * l + 2 * g + c:4 * l + 2 * g + c + 1])
                banks.free(b, a)
                gates.append(a)
                yield
            for c in range(2):
                a = ts(A3[:, c, :], A3[:, c, :], 1.0, spl[:, 2 * l + c:2 * l + c + 1], ALU.add, ALU.mult, gates[1], tok["spl"])
            b1 = act(flat(A1), flat(A3), ACT.Exp, a, t_g)
            b2 = act(flat(A2), flat(A3), ACT.Tanh, a, t_g, scale=-1.0)
            yield
            d1 = stt(flat(A4), flat(A4), 1.0, flat(XC), ALU.add, ALU.mult, gates[1])
            c1 = tt(flat(A3), flat(A1), flat(A1), ALU.mult, b1, b2)
            yield
            c1 = stt(flat(A3), flat(A3), 1.0, flat(A2), ALU.add, ALU.mult, c1)
            c2 = act(flat(A3), flat(A3), ACT.Sqrt, c1)
            yield
            d1 = stt(flat(A4), flat(A4), 0.5, flat(A3), ALU.mult, ALU.mult, d1, c2)
            yield
            for c in range(2):
                a = DV.do(lambda e, c=c: e.tensor_tensor_scan(A2[:, c, :], A1[:, c, :], A4[:, c, :], 0.0, ALU.mult, ALU.add), d1)
                yield
            t = stt(flat(A2), flat(A2), 0.5, flat(LY), ALU.mult, ALU.mult, a, t_g)
            did["lru"] = split((MX[0][:, 0:2, :], MX[1][:, 0:2, :]), A2, t, mx_free[0])
            did["d1"] = d1

        b, ps, t = proj_t(w, l, 0, HT)
        DV.do(lambda e: e.memset(LX[:, :, 0:3], 0.0), t)
        t_lx = copy(LX[:, :, 3:259], ps, t)
        banks.free(b, t_lx)
        b, ps, t = proj_t(w, l, 1, HT)
        t_ly = act(LY, ps, ACT.Copy, t)
        banks.free(b, t_ly)
        fg = forget()
        beside.append(fg)
        if l == 0:
            junk = [flat(v[:, 0:4, :]) for v in MX]
            pars = parameters()
            beside.extend([pars, norming(par("mem", 0, 8), None, t_mem, src=XN, dst=MEM, got=[],
                                         scr=junk, dg=JK[:, 512:768])])
        rec = recurrence(t_lx, t_ly)
        beside.append(rec)
        for n in range(2):
            b, ps, t = proj_t(w, l, 2 + n, HT)
            t_q = act(QT[:, 2 * n:2 * n + 2, :], ps, ACT.Copy, t, scale=0.125)
            banks.free(b, t_q)
            b, ps, t = proj_t(w, l, 4 + n, HT)
            t_k = act(KT[:, 2 * n:2 * n + 2, :], ps, ACT.Copy, t)
            banks.free(b, t_k)
            b, ps, t = proj_r(w, l, 6 + n, HT)
            t_v = act(V[:, :, 256 * n:256 * n + 256], ps, ACT.Copy, t)
            banks.free(b, t_v)
        finish(fg)
        if l == 0:
            finish(pars)
        t_c = did["c"]
        t_rot = tok["rot"]
        rot = []
        for n, (raw, res) in enumerate(((S1, RQ), (QR, RK))):
            b, ps, t = proj_r(w, l, 8 + n, HT, off=8)
            e = act(raw, ps, ACT.Copy, t)
            banks.free(b, e)
            x = raw.rearrange("p t (h s f) -> p t h s f", h=4, s=2)
            o = res.rearrange("p t (h s f) -> p t h s f", h=4, s=2)
            cos = CSN[:, 0:2, :].unsqueeze(2).broadcast_to([128, 2, 4, 32])
            sin = CSN[:, 2:4, :].unsqueeze(2).broadcast_to([128, 2, 4, 32])
            for s, op in ((0, ALU.subtract), (1, ALU.add)):
                c1, c2 = (cos, sin) if s == 0 else (sin, cos)
                a1 = tt(R1, x[:, :, :, 0], c1, ALU.mult, e, t_rot, t_c, rot[-1:], q=PO)
                a2 = tt(R2, x[:, :, :, 1], c2, ALU.mult, e, rot[-1:], q=PO)
                rot.append(tt(o[:, :, :, s], R1, R2, op, a1, a2, q=PO))
        sc, pt, outs = {}, {}, {}

        def scores(h):
            c, po = h // 2, 64 * (h % 2)
            b, ps, freed = banks.take()
            PE.wait(freed, t_q, t_k, t_c, t_cst)
            one = M.ONE[0:8, h:h + 1]
            for t in range(2):
                o = ps[:, 0:128] if t == 0 else ps[:, 128:384]
                nk = 128 * (t + 1)
                mm(o, QT[po:po + 64, c, 128 * t:128 * t + 128], KT[po:po + 64, c, 0:nk], True, False)
                for i in range(2):
                    mm(o, CQ[i][:, 128 * t:128 * t + 128], one.broadcast_to([8, nk]), False, False)
                    tk = mm(o, one.broadcast_to([8, 128]), CN[i][:, 0:nk], False, i == 1, inc=(t == i == 1))
            i, P, pf = pp.take()
            col = 2 * h
            for t in range(2):
                o = P[:, 0:128] if t == 0 else P[:, 128:384]
                s_ = ps[:, 0:128] if t == 0 else ps[:, 128:384]
                m_ = CST[:, C_MASK + 128:C_MASK + 256] if t == 0 else CST[:, C_MASK:C_MASK + 256]
                a = DV.do(lambda e, o=o, s_=s_, m_=m_, cc=mxx[:, col + t:col + t + 1]: e.tensor_tensor_reduce(
                    o, s_, m_, 1.0, NEG, ALU.add, ALU.max, cc), tk, pf)
            banks.free(b, a)
            a = ts(nmx[:, col:col + 2], mxx[:, col:col + 2], -1.0, None, ALU.mult, None, a)
            for t in range(2):
                o = P[:, 0:128] if t == 0 else P[:, 128:384]
                a2 = act(o, o, ACT.Exp, a, bias=nmx[:, col + t:col + t + 1], accum_out=sms[:, col + t:col + t + 1])
            r = DV.do(lambda e: e.reciprocal(rcp[:, col:col + 2], sms[:, col:col + 2]), a2)
            for t in range(2):
                o = P[:, 0:128] if t == 0 else P[:, 128:384]
                r2 = ts(o, o, rcp[:, col + t:col + t + 1], None, ALU.mult, None, r)
            sc[h] = (i, P, r2)

        def turned(h):
            i, P, tok = sc[h]
            b, ps, freed = banks.take()
            PE.wait(freed, tok)
            for j in range(3):
                tk = tr(ps[:, 128 * j:128 * j + 128], P[:, 128 * j:128 * j + 128], inc=(j == 2))
            pp.free(i, tk)
            i2, Q, qf = pq.take()
            e = act(Q[:, 0:384], ps[:, 0:384], ACT.Copy, tk, qf)
            banks.free(b, e)
            pt[h] = (i2, Q, e)

        def values(h):
            c, po = h // 2, 64 * (h % 2)
            i, Q, tok = pt[h]
            if h % 2 == 0:
                outs[c] = banks.take()
                PE.wait(outs[c][2])
            ps = outs[c][1]
            PE.wait(tok, t_v)
            mm(ps[po:po + 64, 0:256], V[:, 0, 64 * h:64 * h + 64], Q[:, 0:256], True, False)
            t = mm(ps[po:po + 64, 128:256], V[:, 1, 64 * h:64 * h + 64], Q[:, 256:384], False, True, inc=True)
            pq.free(i, t)
            if h % 2:
                mx = split((MX[0][:, 2 + c, :], MX[1][:, 2 + c, :]), ps[:, 0:256], t, mx_free[0])
                banks.free(outs[c][0], mx)
                outs["last"] = mx

        def heads(i):
            if i < 8:
                scores(i)
            if 0 <= i - 1 < 8:
                turned(i - 1)
            if 0 <= i - 2:
                values(i - 2)

        heads(0)
        b, ps, t = proj_r(w, l, 10, HT, off=8)
        t_rv = act(RV, ps, ACT.Copy, t)
        banks.free(b, t_rv)
        heads(1)
        b, ps, t = proj_r(w, l, 11, HT, off=8)
        t_th = act(S1, ps, ACT.Tanh, t, rot[1], scale=0.5)
        t_rg = stt(flat(RG), flat(S1), 1.0, flat(ps), ALU.add, ALU.mult, t_th)
        banks.free(b, t_rg)
        res = []
        for i in range(2, 10):
            if i > 7:
                src, dst = ((RQ, QR), (RK, KR))[i - 8]
                res += turn([src[:, 0, :], src[:, 1, :]], dst, 2, None, None, rot[-1])
            heads(i)
            step()
        finish(rec)
        t_lru, d1 = did["lru"], did["d1"]
        bY, psY, freed = banks.take()
        psY = two(psY)
        PE.wait(freed)
        hold = []

        def ret_s(h):
            c, po = h // 2, 64 * (h % 2)
            b, ps, freed = banks.take()
            PE.wait(freed, res)
            mm(ps[:, 0:256], KR[po:po + 64, c, 0:128], QR[po:po + 64, c, :], True, True)
            t = mm(ps[:, 256:384], KR[po:po + 64, c, 128:256], QR[po:po + 64, c, 128:256], True, True, inc=True)
            i, P, pf = pp.take()
            a = tt(P[:, 0:384], ps[:, 0:384], CST[:, C_DEC + 384 * h:C_DEC + 384 + 384 * h], ALU.mult, t, pf)
            banks.free(b, a)
            hold.append((i, P, a))

        def ret_v(h):
            i, P, a = hold[h]
            v = lambda t: RV[:, t, 64 * h:64 * h + 64]
            PE.wait(a, t_rv)
            mm(psY[:, 0, 64 * h:64 * h + 64], P[:, 0:128], v(0), True, True)
            mm(psY[:, 1, 64 * h:64 * h + 64], P[:, 128:256], v(0), True, False)
            t = mm(psY[:, 1, 64 * h:64 * h + 64], P[:, 256:384], v(1), False, True, inc=True)
            pp.free(i, t)
            return t

        for i in range(5):
            if i < 4:
                ret_s(i)
            if i:
                t_y = ret_v(i - 1)
        y8 = psY.rearrange("p t (h d) -> p (t h) d", h=4)
        s3 = lambda v: flat(v).rearrange("p (g d) -> p g d", g=8)
        fin = []

        def retained():
            a = red(s8[0], y8, ALU.add, t_y)
            a = ts(s8[1], s8[0], 1.0 / 64, None, ALU.mult, None, a)
            a = tt(s3(A3), y8, s8[1].unsqueeze(2).broadcast_to([128, 8, 64]), ALU.subtract, a, d1)
            banks.free(bY, a)
            b = act(flat(A4), flat(A3), ACT.Square, a, d1, t_lru)
            b = red(s8[2], s3(A4), ALU.add, b)
            b = ts(s8[3], s8[2], 1.0 / 64, EPS, ALU.mult, ALU.add, b)
            b = power(s8[4], s8[3], mhalf, 8, b)
            yield
            b = tt(s3(A3), s3(A3), s8[4].unsqueeze(2).broadcast_to([128, 8, 64]), ALU.mult, b)
            b = stt(flat(A3), flat(A3), 0.5, flat(RG), ALU.mult, ALU.mult, b, t_rg)
            yield
            yield from turning([A3[:, 0, :], A3[:, 1, :]], MX, 2, None, None, b, at=6, got=fin)

        last = retained()
        beside.append(last)
        out_unit("w_out", l, 0, t_lru, start=True)
        out_unit("w_out", l, 1, outs["last"])
        out_unit("w_out", l, 2)
        finish(last)
        t_g = load_gain(D["post_mix_g"][l:l + 1, :], fin)
        return out_unit("w_out", l, 3, fin, last=True), t_g

    mx_free = [None]

    def cross(l):
        CQ = view(0, (8, 256))
        tq = {}

        def query(n):
            b, ps, t = proj_t("w_cq", l, n, HT)
            tq[n] = act(CQ[:, 2 * n:2 * n + 2, :], ps, ACT.Copy, t, scale=1.0 / 16)
            banks.free(b, tq[n])

        sc, pt = {}, {}
        done = []

        def scores(h):
            b, ps, freed = banks.take()
            ps = two(ps)
            PE.wait(freed, tq[h], kv_tok[l, "k", h])
            for t in range(2):
                for d in range(2):
                    tk = mm(ps[:, t, :], CQ[:, 2 * h + d, 128 * t:128 * t + 128], CK[:, 2 * h + d, :], d == 0, d == 1,
                            inc=(t == 1 and d == 1))
            i, P, pf = pp.take()
            col = 2 * h
            a = red(mxx[:, col:col + 2], ps, ALU.max, tk)
            a = ts(nmx[:, col:col + 2], mxx[:, col:col + 2], -1.0, None, ALU.mult, None, a)
            for t in range(2):
                a2 = act(P[:, 256 * t:256 * t + 256], ps[:, t, :], ACT.Exp, a, pf, bias=nmx[:, col + t:col + t + 1],
                         accum_out=sms[:, col + t:col + t + 1])
            banks.free(b, a2)
            r = DV.do(lambda e: e.reciprocal(rcp[:, col:col + 2], sms[:, col:col + 2]), a2)
            for t in range(2):
                o = P[:, 256 * t:256 * t + 256]
                r2 = ts(o, o, rcp[:, col + t:col + t + 1], None, ALU.mult, None, r)
            sc[h] = (i, P, r2)

        def turned(h):
            i, P, tok = sc[h]
            b, ps, freed = banks.take()
            PE.wait(freed, tok)
            for m in range(2):
                for t in range(2):
                    tk = tr(ps[:, 256 * m + 128 * t:256 * m + 128 * t + 128], P[:, 256 * t + 128 * m:256 * t + 128 * m + 128],
                            inc=(m == 1 and t == 1))
            pp.free(i, tk)
            i2, Q, qf = pq.take()
            e = act(Q[:, :], ps, ACT.Copy, tk, qf)
            banks.free(b, e)
            pt[h] = (i2, Q, e)

        def values(h):
            i, Q, tok = pt[h]
            b, ps, freed = banks.take()
            ps = two(ps)
            PE.wait(freed, tok, [kv_tok[l, "v", n] for n in range(4)])
            for d in range(2):
                for m in range(2):
                    t = mm(ps[:, d, :], CV[:, m, 256 * h + 128 * d:256 * h + 128 * d + 128], Q[:, 256 * m:256 * m + 256],
                           m == 0, m == 1, inc=(d == 1 and m == 1))
            pq.free(i, t)
            mx = split((MX[0][:, 2 * h:2 * h + 2, :], MX[1][:, 2 * h:2 * h + 2, :]), ps, t, mx_free[0])
            banks.free(b, mx)
            done.append(mx)

        query(0)
        for i in range(6):
            if i < 4:
                scores(i)
            if i + 1 < 4:
                query(i + 1)
            if 0 <= i - 1 < 4:
                turned(i - 1)
            if i == 4:
                out_unit("w_co", l, 0, done[0], start=True)
            if i == 5:
                out_unit("w_co", l, 1, done[1])
            if 0 <= i - 2:
                values(i - 2)
        out_unit("w_co", l, 2, done[2])
        return out_unit("w_co", l, 3, done[3], last=True)

    def ffn(l):
        A = [view(512 * i, (2, 256)) for i in range(2)]
        hid = Slots([part(MX, slice(None), slice(2 * i, 2 * i + 2)) for i in range(4)])
        for i in range(4):
            hid.free(i, mx_free[0])
        af = [None, None]
        ready = {}

        def down(n):
            i, d, tok = ready[n]
            y = y_unit("w_down", l, n, d, tok, start=n == 0, last=n == 10)
            hid.free(i, y)
            return y

        for n in range(11):
            b1, g, t1 = proj_t("w_gate", l, n, HT)
            b2, u, t2 = proj_t("w_up", l, n, HT)
            a = A[n % 2]
            e = act(flat(a), flat(g), ACT.Tanh, t1, af[n % 2], scale=0.5)
            e = stt(flat(a), flat(a), 1.0, flat(g), ALU.add, ALU.mult, e)
            banks.free(b1, e)
            if n > 1:
                down(n - 2)
            fill(2 if n == 5 else 1)
            e = stt(flat(a), flat(a), 0.5, flat(u), ALU.mult, ALU.mult, e, t2)
            banks.free(b2, e)
            i, d, df = hid.take()
            e = split(d, a, e, df)
            af[n % 2] = e
            ready[n] = (i, d, e)
        down(9)
        return down(10)

    def store(src, toks):
        for t in range(2):
            o = SP.dma(count, "out", lambda e, t=t: e.dma_start(out[0, 128 * t:128 * t + 128, :], src[:, t, :]), toks[t])
        SP.wait(o)

    def run():
        filler.extend([lambda n=n: fill_ada(n) for n in range(24)])
        t_xx = t_x
        for l in range(2):
            nrm = norming(par(f"pre_mix{l}", 0, 8), None, t_xx, got=[])
            next(nrm)
            if l == 0 and order is not None:
                split_unit(0)
                early_high()
                early_low()
            finish_gen(nrm)
            t_h = norms[id(HT)]
            y, t_g = mixer(l, t_h)
            mx_free[0] = y
            kv = [fill_k(l, n) for n in range(4)] + [fill_v(l, n) for n in range(4)]
            next(kv[0])
            t_xx = post_norm(y, GB, t_g, ahead=False)
            gb_free[0] = t_xx
            nrm = norming(par(f"pre_cross{l}", 0, 8), None, t_xx, got=[])
            finish_gen(kv[0])
            next(kv[1])
            next(nrm)
            finish_gen(kv[1])
            next(kv[2])
            finish_gen(kv[2])
            beside.append(nrm)
            for g in kv[3:]:
                finish_gen(g)
            finish(nrm)
            t_g = load_gain(D["post_cross_g"][l:l + 1, :])
            y = cross(l)
            mx_free[0] = y
            t_xx = post_norm(y, GB, t_g)
            gb_free[0] = t_xx
            t_h = pre_norm(par(f"pre_ffn{l}", 0, 8), None, t_xx)
            t_g = load_gain(D["post_ffn_g"][l:l + 1, :])
            y = ffn(l)
            mx_free[0] = y
            t_xx = post_norm(y, GB, t_g)
            gb_free[0] = t_xx
        second(t_xx)

    def second(t_xx):
        t_mod = ada_tok["last"]
        t_g = load_gain(D["norm_post_mix_2"][0:1, :])
        a = tt(gs[:, 0:8], par("npm2", 0, 8), MT[:, 8:16], ALU.mult, t_mod)
        b = tt(gs[:, 8:16], par("npf2", 0, 8), MT[:, 24:32], ALU.mult, t_mod)
        t_h = pre_norm(gs[:, 0:8], MT[:, 0:8], t_xx, a, b)
        gb_free[0] = ga = tt(GA[:, 0, :], GA[:, 0, :], GB, ALU.mult, t_g)
        QT, K2 = view(0, (4, 256)), view(1024, (2, 256))
        V2 = view(1536, (2, 128))
        VG, UG = view(1792, (2, 512)), view(2816, (2, 512))
        G1, G2 = view(3840, (2, 512)), view(4864, (2, 512))
        WS = view(5888, (8, 128))
        LN = view(6912, (2, 512))
        AT = view(7936, (2, 512))
        GM = view(8960, (2, 512))
        for n in range(2):
            b, ps, t = proj_t("w_in_2", 0, n, HT)
            t_q = act(QT[:, 2 * n:2 * n + 2, :], ps, ACT.Copy, t, scale=0.125)
            banks.free(b, t_q)
        t_ws = load_late("ws", WS, D["w_st"], t_h)
        load_late("ln", LN[:, 0, :], D["sgu_ln_g_2"][0:1, :].broadcast_to([128, 512]), t_h)
        t_ln = load_late("ln", LN[:, 1, :], D["sgu_ln_b_2"][0:1, :].broadcast_to([128, 512]), t_h)
        i, u, got = split_cols("w_in_2", 0, 2)
        b, ps, freed = banks.take()
        PE.wait(got, freed)
        for k in range(8):
            mm3(ps[:, 0:256], part(u, slice(None), k, slice(0, 128)), part(HT, slice(None), k), k == 0, k == 7)
        for t in range(2):
            for k in range(8):
                tk = mm3(ps[:, 256 + 128 * t:384 + 128 * t], part(HT, slice(None), k, slice(128 * t, 128 * t + 128)),
                         part(u, slice(None), k, slice(128, 256)), k == 0, k == 7, inc=(t == 1 and k == 7))
        hfree[i] = tk
        for j in range(2):
            for h in range(2):
                t_k = copy(K2[64 * h:64 * h + 64, j, :], ps[64 * j:64 * j + 64, 0:256], tk)
        t_v = act(V2, two(ps[:, 256:512]), ACT.Copy, tk, t_k)
        banks.free(b, t_k, t_v)
        sc, pt = {}, {}
        done = []

        def scores(h):
            c, po, j = h // 2, 64 * (h % 2), h // 4
            b, ps, freed = banks.take()
            PE.wait(freed, t_q, t_k)
            for t in range(2):
                tk = mm(ps[:, 256 * t:256 * t + 256], QT[po:po + 64, c, 128 * t:128 * t + 128], K2[po:po + 64, j, :], True, True,
                        inc=(t == 1))
            i, P, pf = pp.take()
            col = 2 * h
            a = stt(P[:, :], CST[:, C_DIST:C_DIST + 512], float(2.0 ** -(h + 1)), ps, ALU.mult, ALU.add, tk, pf)
            banks.free(b, a)
            a = red(mxx[:, col:col + 2], two(P[:, :]), ALU.max, a)
            a = ts(nmx[:, col:col + 2], mxx[:, col:col + 2], snk[:, h:h + 1], -1.0, ALU.max, ALU.mult, a)
            for t in range(2):
                o = P[:, 256 * t:256 * t + 256]
                a2 = act(o, o, ACT.Exp, a, bias=nmx[:, col + t:col + t + 1], accum_out=sms[:, col + t:col + t + 1])
            a3 = act(esk[:, col:col + 2], nmx[:, col:col + 2], ACT.Exp, a, bias=snk[:, h:h + 1])
            r = tt(esk[:, col:col + 2], esk[:, col:col + 2], sms[:, col:col + 2], ALU.add, a3)
            r = DV.do(lambda e: e.reciprocal(rcp[:, col:col + 2], esk[:, col:col + 2]), r)
            sc[h] = (i, P, a2, r)

        def turned(h):
            i, P, tok, r = sc[h]
            b, ps, freed = banks.take()
            PE.wait(freed, tok)
            for m in range(2):
                for t in range(2):
                    tk = tr(ps[:, 256 * m + 128 * t:256 * m + 128 * t + 128], P[:, 256 * t + 128 * m:256 * t + 128 * m + 128],
                            inc=(m == 1 and t == 1))
            pp.free(i, tk)
            i2, Q, qf = pq.take()
            e = act(Q[:, :], ps, ACT.Copy, tk, qf)
            banks.free(b, e)
            pt[h] = (i2, Q, e, r)

        def values(h):
            j = h // 4
            i, Q, tok, r = pt[h]
            b, ps, freed = banks.take()
            PE.wait(freed, tok, t_v)
            for t in range(2):
                for m in range(2):
                    tk = mm(ps[:, 64 * t:64 * t + 64], Q[:, 256 * m + 128 * t:256 * m + 128 * t + 128],
                            V2[:, m, 64 * j:64 * j + 64], m == 0, m == 1, inc=(t == 1 and m == 1))
            pq.free(i, tk)
            for t in range(2):
                a = ts(AT[:, t, 64 * h:64 * h + 64], ps[:, 64 * t:64 * t + 64], rcp[:, 2 * h + t:2 * h + t + 1], None,
                       ALU.mult, None, tk, r)
            banks.free(b, a)
            done.append(a)

        def attention():
            for i in range(10):
                if i < 8:
                    scores(i)
                if 0 <= i - 1 < 8:
                    turned(i - 1)
                if 0 <= i - 2:
                    values(i - 2)
                yield

        heads = attention()
        shared[0] = True
        g_free = None
        for name, dst, base in (("v", VG, 5), ("u", UG, 3)):
            for n in range(2):
                b, ps, t = proj_r("w_in_2", 0, base + n, HT)
                if (name, n) == ("v", 0):
                    beside.append(heads)
                y = dst[:, :, 256 * n:256 * n + 256]
                e = act(y, ps, ACT.Copy, t)
                banks.free(b, e)
                t1, t2 = G1[:, :, 256 * n:256 * n + 256], G2[:, :, 256 * n:256 * n + 256]
                g = gelu2(y, y, t1, t2, e, g_free)
                if n == 1:
                    g_free = g
            ht_last[0] = t
            if name == "u":
                t_ug = g
                continue
            for t in range(2):
                a = DV.do(lambda e, t=t: e.bn_stats(st6[:, 6 * t:6 * t + 6], VG[:, t, :]), g)
                a = DV.do(lambda e, t=t: e.bn_aggr(mv[:, 2 * t:2 * t + 2], st6[:, 6 * t:6 * t + 6]), a)
            a = ts(ms, mv[:, 1:4:2], 0.25, EPS, ALU.mult, ALU.add, a)
            a = power(rs, ms, mhalf, 2, a)
            a = ts(rs, rs, 0.5, None, ALU.mult, None, a)
            for t in range(2):
                v = VG[:, t, :]
                c = ts(v, v, mv[:, 2 * t:2 * t + 1], rs[:, t:t + 1], ALU.subtract, ALU.mult, a)
                c = tt(v, v, LN[:, 0, :], ALU.mult, c, t_ln, q=PO)
                t_vn = tt(v, v, LN[:, 1, :], ALU.add, c, q=PO)
        gm = []
        for t in range(2):
            b, ps, freed = banks.take()
            PE.wait(freed, t_vn, t_ws)
            for g in range(8):
                tk = mm(ps[:, 64 * g:64 * g + 64], WS[:, g, :], VG[:, t, 64 * g:64 * g + 64], True, True, inc=(g == 7))
            o = GM[:, t, :]
            a = tt(o.rearrange("p (g c) -> p g c", g=8), ps.rearrange("p (g c) -> p g c", g=8),
                   par("b_s", 0, 8).unsqueeze(2).broadcast_to([128, 8, 64]), ALU.add, tk)
            banks.free(b, a)
            gm.append(stt(o, o, 0.5, UG[:, t, :], ALU.mult, ALU.mult, a, t_ug))
        scr = (XN[:, 0, :], XN[:, 1, :])
        D2 = JK[:, 256:512]
        rows = [GM[:, 0, :], GM[:, 1, :]]
        a = diagonal(DG, rs2, [[v] for v in rows], 512, scr, [gm[0]], [gm[1]])
        finish(heads)
        f2 = turn(rows, MX, 4, par("nog2", 0, 4), None, a, at=4, by=DG)
        rows = [AT[:, 0, :], AT[:, 1, :]]
        a = diagonal(D2, rs, [[v] for v in rows], 512, scr, [done], [done])
        out_unit("w_out_2", 0, 2, f2, start=True)
        f1 = turn(rows, MX, 4, par("noa2", 0, 4), None, a, by=D2)
        out_unit("w_out_2", 0, 3, f2)
        out_unit("w_out_2", 0, 0, f1)
        y = out_unit("w_out_2", 0, 1, f1, last=True)
        mx_free[0] = y
        t_xx = post_norm(y, GA[:, 0, :], ga)
        experts(t_xx, done + f1)

    def experts(t_xx, attended):
        n = len(used)
        slots = [M.WB[:, 2816 * i:2816 * (i + 1)] for i in range(NB)]
        big = Slots(slots[0:3] + M.MORE[0:2] + slots[3:] + M.MORE[2:])
        for i in range(NB):
            lo, hi = 2816 * i, 2816 * (i + 1)
            f = [kv_last[0]]
            if hi > 4608:
                f.append(ht_last[0])
            f += [wfree[m] for m in range(n - NW, n)
                  if 8704 + 2048 * (m % NW) < hi and 8704 + 2048 * (m % NW + 1) > lo]
            if hi > 16896:
                f.append(mx_free[0])
            big.free(i if i < 3 else i + 2, f)
        big.free(3, attended)
        big.free(4, attended)
        big.free(NB + 2, t_xx)
        HF, YA = M.HF, M.YA
        WR = M.WR
        SEL, SLG, XP = M.SEL, view(1152, (2, 512)), M.XP
        HD = [view(2176 + 704 * i, (1, 704))[:, 0, :] for i in range(2)]
        HH = [view(3584 + 896 * i, (7, 128)) for i in range(2)]
        DN = [view(5376 + 1024 * i, (2, 512)) for i in range(2)]
        SG = [view(7424 + 256 * i, (1, 256))[:, 0, :] for i in range(2)]
        W1 = view(7936, (4, 256))
        R4 = view(8960, (2, 128))

        t_h = []
        nrm = norming(gs[:, 8:16], MT[:, 16:24], t_xx, dst=HF, got=t_h)
        next(nrm)
        for t in range(2):
            h, l = XP[0][:, t, :], XP[1][:, t, :]
            a = act(h, X[:, t, :], ACT.Copy, (PO.key, PO.n), t_xx, scale=rs[:, t:t + 1])
            t_xn = stt(l, X[:, t, :], rs[:, t:t + 1], h.bitcast(F32), ALU.mult, ALU.subtract, a)
        finish_gen(nrm)
        b, ps, freed = banks.take()
        lg = ps[:, 0:32].rearrange("p (t e) -> p t e", t=2)
        PE.wait(freed, t_h, tok["wr"])
        for t in range(2):
            for k in range(8):
                tk = mm(lg[:, t, :], HF[:, k, 128 * t:128 * t + 128], WR[:, k, :], k == 0, k == 7, inc=(t == 1 and k == 7))
        t_router = tk
        a = red(amx, lg, ALU.max, tk)
        a = ts(amx, amx, -1.0, None, ALU.mult, None, a)
        for t in range(2):
            a2 = act(aff[:, 16 * t:16 * t + 16], lg[:, t, :], ACT.Exp, a, bias=amx[:, t:t + 1], accum_out=asm[:, t:t + 1])
        banks.free(b, a2)
        a = DV.do(lambda e: e.reciprocal(asm, asm), a2)
        for t in range(2):
            a = ts(aff[:, 16 * t:16 * t + 16], aff[:, 16 * t:16 * t + 16], asm[:, t:t + 1], None, ALU.mult, None, a)
        t_aff = a
        b, ps, freed = banks.take()
        PE.wait(freed, t_aff)
        for t in range(2):
            tk = tr(ps[0:16, 128 * t:128 * t + 128], aff[:, 16 * t:16 * t + 16], inc=(t == 1))
        wk = W1[0:16, 0, :]
        a = copy(wk, ps[0:16, 0:256], tk)
        banks.free(b, a)
        m8 = W1[0:16, 1, 0:8]
        for _ in range(4):
            a = DV.do(lambda e: e.max(m8, wk), a)
            a = DV.do(lambda e: e.match_replace(wk, m8, wk, -1.0), a)
        msk, pos = W1[0:16, 2, :], W1[0:16, 3, :]
        a = ts(msk, wk, 0.0, None, ALU.is_lt, None, a)
        a = DV.do(lambda e: e.tensor_tensor_scan(pos, msk, zero[0:16, :].broadcast_to([16, 256]), 0.0, ALU.add, ALU.add), a)
        a = tt(pos, pos, msk, ALU.mult, a)
        b, ps, freed = banks.take()
        PE.wait(freed, a)
        for t in range(2):
            tk = PE.do(lambda e, t=t, ps=ps: e.transpose(ps[:, 16 * t:16 * t + 16], pos[:, 128 * t:128 * t + 128], ID[0:16, 0:16]))
        sel = []
        for t in range(2):
            s3 = SEL[:, t, :].rearrange("p (e c) -> p e c", e=16)
            g3 = SLG[:, t, :].rearrange("p (e c) -> p e c", e=16)
            a = tt(s3, ps[:, 16 * t:16 * t + 16].unsqueeze(2).broadcast_to([128, 16, 32]),
                   CST[:, C_IOTA:C_IOTA + 32].unsqueeze(1).broadcast_to([128, 16, 32]), ALU.is_equal, tk)
            sel.append(a)
        banks.free(b, a)
        for t in range(2):
            s3 = SEL[:, t, :].rearrange("p (e c) -> p e c", e=16)
            g3 = SLG[:, t, :].rearrange("p (e c) -> p e c", e=16)
            t_slg = tt(g3, s3.bitcast(F32), aff[:, 16 * t:16 * t + 16].unsqueeze(2).broadcast_to([128, 16, 32]), ALU.mult, sel[t])

        t_g = load_gain(D["norm_post_ffn_2"][0:1, :], mx_free[0])
        tt(GA[:, 1, :], GA[:, 1, :], GB, ALU.mult, t_g, ada_tok["last"])

        def xs(k):
            return M.XS[:, k, :]

        xst = []

        def gather(k):
            b, ps, freed = banks.take()
            PE.wait(freed, sel, t_xn)
            for t in range(2):
                for j in range(2):
                    tk = mm(ps, XP[j][:, t, 128 * k:128 * k + 128], SEL[:, t, :], t == j == 0, t == j == 1,
                            inc=t == j == 1)
            g, z = gs[:, 8 + k:9 + k], MT[:, 16 + k:17 + k]
            if k % 2:
                e = ts(xs(k), ps, g, z, ALU.mult, ALU.add, tk, t_router)
            else:
                e = act(xs(k), ps, ACT.Identity, tk, t_router, scale=g, bias=z)
            banks.free(b, e)
            xst.append(e)

        gu_free = [list(yfree[0:2]), list(yfree[2:4])]
        ya = [[None, None], [None, None]]
        for ex in range(16):
            e2 = ex % 2
            tok_gu = []
            for m, wname in enumerate(("w_gate_2", "w_up_2")):
                if ex == m == 0:
                    gather(0)
                    gather(1)
                for k in range(8):
                    if ex == m == 0 and k < 6:
                        gather(k + 2)
                    i, buf, freed = big.take()
                    got = load(f"b{i}", buf, D[wname][0, ex, 128 * k:128 * k + 128, :], freed)
                    PE.wait(got, xst[k])
                    if k == 0:
                        PE.wait(gu_free[m])
                    lhs = xs(k)[:, 32 * ex:32 * ex + 32]
                    for hf in range(2):
                        for q in range(4):
                            c0 = 704 * q + 352 * hf
                            t = mm(PS[32 * q:32 * q + 32, 2 * m + hf, 0:352], lhs, buf[:, c0:c0 + 352], k == 0, k == 7,
                                   inc=(hf == 1 and q == 3))
                    big.free(i, t)
                tok_gu.append(t)
            if ex == 0:
                t_gathered = (PE.key, PE.n)
                hd_free, hh_free, dn2_free, sg_free = [None, None], [t_gathered] * 2, [t_gathered] * 2, [None, None]
                dn_free = banks.freed[0:2]
                rest = Slots([PS[:, 6, :], PS[:, 7, :]])
                rest.free(0, banks.freed[2])
                rest.free(1, banks.freed[3])
            bi, ps, freed = rest.take()
            for t in range(2):
                src = SLG[:, t, 32 * ex:32 * ex + 32].unsqueeze(1).broadcast_to([128, 4, 32])
                r4 = copy(R4[:, t, :].rearrange("p (q c) -> p q c", q=4), src, t_slg, sg_free[0], q=PO)
            PE.wait(freed, r4)
            for t in range(2):
                tk = tr(ps[:, 128 * t:128 * t + 128], R4[:, t, :], inc=(t == 1))
            sg_free[0] = tk
            sgt = act(SG[e2], ps[:, 0:256], ACT.Copy, tk, dn2_free[e2])
            rest.free(bi, sgt)
            hd = HD[e2]
            for hf in range(2):
                o = hd[:, 352 * hf:352 * hf + 352]
                g, u = PS[:, hf, 0:352], PS[:, 2 + hf, 0:352]
                a = act(o, g, ACT.Tanh, tok_gu[0], hd_free[e2], scale=0.5)
                a = stt(o, o, 1.0, g, ALU.add, ALU.mult, a)
                gu_free[0] = a
                a = stt(o, o, 0.5, u, ALU.mult, ALU.mult, a, tok_gu[1])
                gu_free[1] = a
            hh = HH[e2]
            starts = [0, 128, 256, 384, 512, 640, 576]
            evac = {}
            for grp in ((0, 1, 2, 3), (4, 5, 6)):
                bi, ps, freed = rest.take()
                PE.wait(freed, a)
                for n, j in enumerate(grp):
                    s0 = starts[j]
                    wd = 64 if j == 5 else 128
                    tk = tr(ps[0:wd, 128 * n:128 * n + 128], hd[:, s0:s0 + wd], inc=(j == grp[-1]))
                if grp[0] == 0:
                    ev = act(hh[:, 0:4, :], ps.rearrange("p (a b) -> p a b", a=4), ACT.Copy, tk, hh_free[e2])
                    evac[0] = ev
                    rest.free(bi, ev)
                else:
                    v1 = copy(hh[:, 4, :], ps[:, 0:128], tk, hh_free[e2])
                    v1 = copy(hh[0:64, 5, :], ps[0:64, 128:256], tk, hh_free[e2])
                    v2 = copy(hh[64:128, 5, :], ps[64:128, 256:384], tk, hh_free[e2])
                    evac[1] = v2
                    rest.free(bi, v2)
            hd_free[e2] = tk
            wd_ = D["w_down_2"][0, ex].rearrange("(q j) d -> j q d", q=4)
            dn = DN[e2]
            jts = range(6) if ex < 15 else (5, 0, 1, 2, 3, 4)
            if ex == 15:
                rest = Slots([PS[:, i, :] for i in range(4)])
                for i in range(4):
                    rest.free(i, gu_free[i // 2])

            def scatter(hf, got):
                if hf:
                    d = copy(dn[:, 1, :], PS[:, 5, :], got, dn2_free[e2])
                else:
                    d = act(dn[:, 0, :], PS[:, 4, :], ACT.Copy, got, dn2_free[e2])
                dn_free[hf] = d
                for t in range(2):
                    bi, ps, freed = rest.take()
                    tk = mm(ps, SG[e2][:, 128 * t:128 * t + 128], dn[:, hf, :], True, True, freed, d, sgt, inc=True)
                    o = YA[:, t, 512 * hf:512 * hf + 512]
                    if ex == 0:
                        a = copy(o, ps, tk)
                    else:
                        a = tt(o, o, ps, ALU.add, tk, ya[t][hf])
                    ya[t][hf] = a
                    rest.free(bi, a)
                return tk

            for jt in jts:
                for nh in range(2 if jt < 5 else 1):
                    i, buf, freed = big.take()
                    if jt < 5:
                        v = buf[:, 0:2048].rearrange("p (q d) -> p q d", q=4)
                        got = load(f"b{i}", v, wd_[128 * jt:128 * jt + 128, :, 512 * nh:512 * nh + 512], freed)
                        PE.wait(got, evac[jt // 4])
                        if jt == jts[0]:
                            PE.wait(dn_free[nh])
                        for q in range(4):
                            t = mm(PS[32 * q:32 * q + 32, 4 + nh, :], hh[:, jt, 32 * q:32 * q + 32], v[:, q, :], jt == jts[0],
                                   jt == jts[-1], inc=(q == 3))
                    else:
                        v = buf[:, 0:2048].rearrange("p (q d) -> p q d", q=2)
                        load(f"b{i}", v[0:64], wd_[640:704, 0:2, :], freed)
                        got = load(f"b{i}", v[64:128], wd_[640:704, 2:4, :], freed)
                        PE.wait(got, evac[1])
                        if jt == jts[0]:
                            PE.wait(dn_free)
                        for hf in range(2):
                            for q in range(4):
                                r0 = 64 * (q // 2)
                                t = mm(PS[32 * q:32 * q + 32, 4 + hf, :], hh[r0:r0 + 64, 5, 32 * q:32 * q + 32],
                                       v[r0:r0 + 64, q % 2, 512 * hf:512 * hf + 512], jt == jts[0], jt == jts[-1],
                                       inc=(q == 3 and hf == 1))
                    big.free(i, t)
                    if jt == jts[-1] and jt < 5:
                        tk = scatter(nh, t)
            if jts[-1] == 5:
                for hf in range(2):
                    tk = scatter(hf, t)
            hh_free[e2] = t
            dn2_free[e2] = tk
        y = [[YA[:, t, 0:512], YA[:, t, 512:1024]] for t in range(2)]
        t_xx = post_norm(ya, GA[:, 1, :], None, src=y, tmp=YA)
        store(X, t_xx)

    run()
    return (SP, PE, AC, DV, PO), used


_DIRECT = ["x", "mem", "post_mix_g", "w_in", "w_rg", "w_ig", "w_out", "post_cross_g", "w_cq",
           "w_ck", "w_cv", "w_co", "w_gate", "w_up", "w_down", "post_ffn_g", "w_ada_2", "b_ada_2", "norm_post_mix_2",
           "w_in_2", "sink_2", "sgu_ln_g_2", "sgu_ln_b_2", "w_out_2", "norm_post_ffn_2", "w_router_2", "w_gate_2",
           "w_up_2", "w_down_2"]


def layout(inputs):
    g = {k: np.ascontiguousarray(inputs[k]) for k in _DIRECT}

    def rows(a):
        return np.asarray(a).reshape(-1, 128)

    parts = []
    for l in range(2):
        parts += [rows(inputs[n][l]) for n in ("pre_mix_g", "pre_cross_g", "pre_ffn_g", "conv_w", "conv_b", "b_rg", "b_ig",
                                               "lru_lambda")]
    parts += [rows(inputs["mem_norm_g"]), rows(inputs["norm_pre_mix_2"]), rows(inputs["norm_out_attn_2"]),
              rows(inputs["norm_out_gmlp_2"]), rows(inputs["norm_pre_ffn_2"]), rows(inputs["b_ada_2"]),
              rows(inputs["b_s_2"]), rows(inputs["c_2"])]
    g["params"] = np.ascontiguousarray(np.concatenate(parts, 0).T)
    g["w_st"] = np.ascontiguousarray(np.transpose(np.asarray(inputs["w_s_2"])[0], (2, 0, 1)))
    g["positions_t"] = np.ascontiguousarray(np.asarray(inputs["positions"]).reshape(2, 128).T)
    g["fox_b_t"] = np.ascontiguousarray(np.asarray(inputs["fox_b_f"]).T)
    g["consts"] = constants()
    return g


def kernel(**inputs):
    import concourse.bacc as _bacc
    from concourse.bass_utils import run_bass_kernel_spmd as _run

    nc = _bacc.Bacc("TRN2", target_bir_lowering=False, num_devices=1)
    arrays, D = {}, {}
    for name, a in layout(inputs).items():
        arrays[f"in_{name}"] = a
        D[name] = nc.dram_tensor(f"in_{name}", a.shape, mybir.dt.from_np(a.dtype), kind="ExternalInput").ap()
    out = nc.dram_tensor("out_0", (1, 256, 1024), F32, kind="ExternalOutput").ap()
    program(nc, D, out)
    r = _run(nc, [arrays], core_ids=[0])
    return r.results[0]["out_0"]
```
